# Optimizing a Trainium2 kernel written in Bass

```python
import jax
import jax.numpy as jnp
from jax import lax
import numpy as np

D_MODEL = 1024
BATCH = 1
SEQ = 256
DEPTH = 1

MEM_LEN = 256
EPS = 1e-5

GLA_HEADS = 4
GLA_WIDTH_V = D_MODEL // 2
GLA_DV = GLA_WIDTH_V // GLA_HEADS
GLA_DK = GLA_DV // 2
GLA_WIDTH_K = GLA_HEADS * GLA_DK
GLA_GATE_RANK = 16
GLA_TAU = 16.0
GLA_CHUNK = 64

SGU_WIDTH = D_MODEL // 2
SGU_GROUPS = 4
SGU_GROUP_DIM = SGU_WIDTH // SGU_GROUPS
SGU_CHUNK = 128

N_BRANCH = 2

OFF_Q = 0
OFF_K = OFF_Q + GLA_WIDTH_K
OFF_V = OFF_K + GLA_WIDTH_K
OFF_R = OFF_V + GLA_WIDTH_V
OFF_A = OFF_R + GLA_WIDTH_V
OFF_U = OFF_A + GLA_GATE_RANK
OFF_SV = OFF_U + SGU_WIDTH
OFF_G = OFF_SV + SGU_WIDTH
IN_COLS = OFF_G + N_BRANCH * D_MODEL

XATTN_HEADS = 4
XATTN_DH = D_MODEL // XATTN_HEADS

N_EXPERTS = 32
TOP_K = 4
D_FF_EXPERT = D_MODEL
SWIGLU_ALPHA = 1.702
SWIGLU_LIMIT = 7.0
MOE_BLOCK = 128

kernel_name = 'hybrid_gla_sgu_xattn_moe_layer'

def _rmsnorm(x, g):
    xf = x.astype(jnp.float32)
    y = xf * lax.rsqrt(jnp.mean(xf * xf, axis=-1, keepdims=True) + EPS)
    return (y * g.astype(jnp.float32)).astype(x.dtype)

def _layernorm(x, g, b):
    xf = x.astype(jnp.float32)
    mu = jnp.mean(xf, axis=-1, keepdims=True)
    var = jnp.mean(jnp.square(xf - mu), axis=-1, keepdims=True)
    y = (xf - mu) * lax.rsqrt(var + EPS)
    return (y * g.astype(jnp.float32) + b.astype(jnp.float32)).astype(x.dtype)

def _gla(q, k, v, r, a_low, w_a2, b_a, out_g):
    B, S, _ = q.shape
    H, C = GLA_HEADS, GLA_CHUNK
    NC = S // C
    f32 = jnp.float32

    def to_chunks(t, d):
        return t.astype(f32).reshape(B, NC, C, H, d).transpose(0, 3, 1, 2, 4)

    log_a = jax.nn.log_sigmoid(a_low.astype(f32) @ w_a2.astype(f32) + b_a.astype(f32)) / GLA_TAU
    qc = to_chunks(q, GLA_DK) * (GLA_DK ** -0.5)
    kc = to_chunks(k, GLA_DK)
    vc = to_chunks(v, GLA_DV)
    cum = jnp.cumsum(to_chunks(log_a, GLA_DK), axis=3)
    cum_last = cum[:, :, :, -1:, :]
    q_in = qc * jnp.exp(cum)
    k_in = kc * jnp.exp(-cum)
    k_out = kc * jnp.exp(cum_last - cum)
    causal = jnp.tril(jnp.ones((C, C), dtype=bool))
    att = jnp.where(causal, jnp.einsum('bhncd,bhnsd->bhncs', q_in, k_in), 0.0)
    o_intra = jnp.einsum('bhncs,bhnse->bhnce', att, vc)
    kv = jnp.einsum('bhncd,bhnce->bhnde', k_out, vc)
    decay = jnp.exp(cum_last[:, :, :, 0, :])

    def step(state, inp):
        dec, kv_n = inp
        return dec[..., None] * state + kv_n, state

    s0 = jnp.zeros((B, H, GLA_DK, GLA_DV), f32)
    _, s_prev = lax.scan(step, s0, (jnp.moveaxis(decay, 2, 0), jnp.moveaxis(kv, 2, 0)))
    o_inter = jnp.einsum('bhncd,nbhde->bhnce', q_in, s_prev)
    o = (o_intra + o_inter).transpose(0, 2, 3, 1, 4).reshape(B, S, H, GLA_DV)
    o = o * lax.rsqrt(jnp.mean(o * o, axis=-1, keepdims=True) + EPS) * out_g.astype(f32).reshape(H, GLA_DV)
    o = o.reshape(B, S, GLA_WIDTH_V) * jax.nn.silu(r.astype(f32))
    return o.astype(q.dtype)

def _sgu(u_pre, v_pre, norm_g, norm_b, w_s, b_s):
    B, S, _ = u_pre.shape
    NC = S // SGU_CHUNK
    u = jax.nn.gelu(u_pre, approximate=False)
    v = _layernorm(jax.nn.gelu(v_pre, approximate=False), norm_g, norm_b)
    v = v.reshape(B, NC, SGU_CHUNK, SGU_GROUPS, SGU_GROUP_DIM)
    causal = jnp.tril(jnp.ones((SGU_CHUNK, SGU_CHUNK), dtype=bool))
    w = jnp.where(causal[None], w_s, 0.0).astype(v.dtype)
    mixed = jnp.einsum('gts,bnsgc->bntgc', w, v) + b_s.T[:, :, None].astype(v.dtype)
    return u * mixed.reshape(B, S, SGU_WIDTH)

def _cross_attn(h, mem_n, wq, wk, wv, wo):
    B, S, _ = h.shape
    M = mem_n.shape[1]
    q = (h @ wq).reshape(B, S, XATTN_HEADS, XATTN_DH)
    k = (mem_n @ wk).reshape(B, M, XATTN_HEADS, XATTN_DH)
    v = (mem_n @ wv).reshape(B, M, XATTN_HEADS, XATTN_DH)
    s = jnp.einsum('bshd,bmhd->bhsm', q, k).astype(jnp.float32) * (XATTN_DH ** -0.5)
    p = jax.nn.softmax(s, axis=-1).astype(v.dtype)
    o = jnp.einsum('bhsm,bmhd->bshd', p, v).reshape(B, S, D_MODEL)
    return o @ wo

def _moe(h, w_router, b_router, w1, b1, w2, b2):
    B, S, D = h.shape
    T = B * S
    xf = h.reshape(T, D)
    logits = (xf @ w_router + b_router).astype(jnp.float32)
    top_v, top_i = lax.top_k(logits, TOP_K)
    gates = jax.nn.softmax(top_v, axis=-1)
    n_assign = T * TOP_K
    flat_e = top_i.reshape(-1)
    flat_tok = jnp.arange(n_assign, dtype=jnp.int32) // TOP_K
    order = jnp.argsort(flat_e, stable=True)
    sorted_e = flat_e[order]
    counts = jnp.bincount(flat_e, length=N_EXPERTS)
    padded = ((counts + MOE_BLOCK - 1) // MOE_BLOCK) * MOE_BLOCK
    pad_end = jnp.cumsum(padded)
    pad_start = pad_end - padded
    start = jnp.cumsum(counts) - counts
    rank = jnp.arange(n_assign, dtype=jnp.int32) - start[sorted_e]
    dest = pad_start[sorted_e] + rank
    n_blocks = -(-n_assign // MOE_BLOCK) + N_EXPERTS
    tok_buf = jnp.full((n_blocks * MOE_BLOCK,), T, jnp.int32).at[dest].set(flat_tok[order])
    block_e = jnp.minimum(
        jnp.searchsorted(pad_end, jnp.arange(n_blocks, dtype=jnp.int32) * MOE_BLOCK, side='right'),
        N_EXPERTS - 1)
    x_pad = jnp.concatenate([xf, jnp.zeros((1, D), xf.dtype)], axis=0)
    xb = x_pad[tok_buf].reshape(n_blocks, MOE_BLOCK, D)

    def expert_block(args):
        xblk, e = args
        hcat = xblk @ w1[e] + b1[e]
        glu = jnp.minimum(hcat[:, :D_FF_EXPERT], SWIGLU_LIMIT)
        lin = jnp.clip(hcat[:, D_FF_EXPERT:], -SWIGLU_LIMIT, SWIGLU_LIMIT)
        act = (lin + 1.0) * glu * jax.nn.sigmoid(SWIGLU_ALPHA * glu)
        return act @ w2[e] + b2[e]

    yb = lax.map(expert_block, (xb, block_e)).reshape(n_blocks * MOE_BLOCK, D)
    y_assign = jnp.zeros((n_assign, D), yb.dtype).at[order].set(yb[dest])
    y = jnp.einsum('tkd,tk->td', y_assign.reshape(T, TOP_K, D), gates.astype(yb.dtype))
    return y.reshape(B, S, D)

def setup_inputs(seed: int = 0) -> dict:
    key = jax.random.key(seed)
    keys = iter(jax.random.split(key, 40))
    f32 = jnp.float32

    def nrm(shape, scale):
        return jax.random.normal(next(keys), shape, f32) * scale

    L = DEPTH
    return {
        'x': nrm((BATCH, SEQ, D_MODEL), 1.0),
        'mem': nrm((BATCH, MEM_LEN, D_MODEL), 1.0),
        'norm_mix_g': 1.0 + nrm((L, D_MODEL), 0.02),
        'w_in': nrm((L, D_MODEL, IN_COLS), D_MODEL ** -0.5),
        'gla_w_a2': nrm((L, GLA_GATE_RANK, GLA_WIDTH_K), GLA_GATE_RANK ** -0.5),
        'gla_b_a': nrm((L, GLA_WIDTH_K), 0.1),
        'gla_out_g': 1.0 + nrm((L, GLA_WIDTH_V), 0.02),
        'sgu_norm_g': 1.0 + nrm((L, SGU_WIDTH), 0.02),
        'sgu_norm_b': nrm((L, SGU_WIDTH), 0.02),
        'sgu_w': nrm((L, SGU_GROUPS, SGU_CHUNK, SGU_CHUNK), SGU_CHUNK ** -0.5),
        'sgu_b': 1.0 + nrm((L, SGU_GROUPS, SGU_CHUNK), 0.1),
        'w_proj_a': nrm((L, GLA_WIDTH_V, D_MODEL), GLA_WIDTH_V ** -0.5),
        'w_proj_b': nrm((L, SGU_WIDTH, D_MODEL), SGU_WIDTH ** -0.5),
        'w_mix_out': nrm((L, D_MODEL, D_MODEL), D_MODEL ** -0.5),
        'norm_x_g': 1.0 + nrm((L, D_MODEL), 0.02),
        'norm_mem_g': 1.0 + nrm((L, D_MODEL), 0.02),
        'w_xq': nrm((L, D_MODEL, D_MODEL), D_MODEL ** -0.5),
        'w_xk': nrm((L, D_MODEL, D_MODEL), D_MODEL ** -0.5),
        'w_xv': nrm((L, D_MODEL, D_MODEL), D_MODEL ** -0.5),
        'w_xo': nrm((L, D_MODEL, D_MODEL), D_MODEL ** -0.5),
        'norm_ffn_g': 1.0 + nrm((L, D_MODEL), 0.02),
        'w_router': nrm((L, D_MODEL, N_EXPERTS), D_MODEL ** -0.5),
        'b_router': nrm((L, N_EXPERTS), 0.01),
        'w_e1': nrm((L, N_EXPERTS, D_MODEL, 2 * D_FF_EXPERT), D_MODEL ** -0.5),
        'b_e1': nrm((L, N_EXPERTS, 2 * D_FF_EXPERT), 0.01),
        'w_e2': nrm((L, N_EXPERTS, D_FF_EXPERT, D_MODEL), D_FF_EXPERT ** -0.5),
        'b_e2': nrm((L, N_EXPERTS, D_MODEL), 0.01),
        'norm_final_g': 1.0 + nrm((D_MODEL,), 0.02),
    }

def reference(x, mem, norm_mix_g, w_in, gla_w_a2, gla_b_a, gla_out_g, sgu_norm_g, sgu_norm_b,
              sgu_w, sgu_b, w_proj_a, w_proj_b, w_mix_out, norm_x_g, norm_mem_g, w_xq, w_xk,
              w_xv, w_xo, norm_ffn_g, w_router, b_router, w_e1, b_e1, w_e2, b_e2, norm_final_g):
    for l in range(DEPTH):
        h = _rmsnorm(x, norm_mix_g[l])
        p = h @ w_in[l]
        y_a = _gla(p[..., OFF_Q:OFF_K], p[..., OFF_K:OFF_V], p[..., OFF_V:OFF_R],
                   p[..., OFF_R:OFF_A], p[..., OFF_A:OFF_U],
                   gla_w_a2[l], gla_b_a[l], gla_out_g[l]) @ w_proj_a[l]
        y_b = _sgu(p[..., OFF_U:OFF_SV], p[..., OFF_SV:OFF_G],
                   sgu_norm_g[l], sgu_norm_b[l], sgu_w[l], sgu_b[l]) @ w_proj_b[l]
        gate_a = jax.nn.sigmoid(p[..., OFF_G:OFF_G + D_MODEL])
        gate_b = jax.nn.sigmoid(p[..., OFF_G + D_MODEL:OFF_G + 2 * D_MODEL])
        x = x + (gate_a * y_a + gate_b * y_b) @ w_mix_out[l]
        mem_n = _rmsnorm(mem, norm_mem_g[l])
        x = x + _cross_attn(_rmsnorm(x, norm_x_g[l]), mem_n, w_xq[l], w_xk[l], w_xv[l], w_xo[l])
        x = x + _moe(_rmsnorm(x, norm_ffn_g[l]), w_router[l], b_router[l],
                     w_e1[l], b_e1[l], w_e2[l], b_e2[l])
    return _rmsnorm(x, norm_final_g)


_drawn_inputs = setup_inputs


def setup_inputs(seed=0):
    import zlib

    import numpy as np

    out = dict(_drawn_inputs(seed))
    spreads = {}
    factors = {'sgu_norm_g': 2.738,
     'sgu_norm_b': 3.291,
     'norm_x_g': 5.209,
     'norm_mem_g': 3.605,
     'b_e1': 32.356,
     'b_e2': 37.381,
     'norm_final_g': 9.697,
     'norm_ffn_g': 4.334,
     'b_router': 8.0}
    for name, (base, spread) in spreads.items():
        noise = np.random.default_rng([zlib.crc32(name.encode()), seed]).standard_normal(out[name].shape)
        drawn = base * np.exp(spread * noise) if base else spread * noise
        out[name] = jnp.asarray(drawn.astype(out[name].dtype))
    for name, factor in factors.items():
        out[name] = (out[name] * factor).astype(out[name].dtype)
    return out
```

```python
from contextlib import ExitStack

import concourse.bass as bass
from concourse import mybir

P = 128
F32 = mybir.dt.float32
I32 = mybir.dt.int32
U32 = mybir.dt.uint32
ALU = mybir.AluOpType
ACT = mybir.ActivationFunctionType
AX = mybir.AxisListType.X

EPS = 1e-5
T = 256
TT = T // P
D = 1024
DC = D // P
HALF = 512
GLA_H, GLA_DK, GLA_DV, GLA_C, RANK, TAU = 4, 64, 128, 64, 16, 16.0
NCH = T // GLA_C
WV = GLA_H * GLA_DV
SGU_G = 4
XH, XDH = 4, 256
N_EXP, TOPK, LIMIT, ALPHA = 32, 4, 7.0, 1.702
SLOTS = 64
ROUNDS = T // SLOTS
VEXP = ROUNDS * N_EXP

OFF_V, OFF_R, OFF_A, OFF_U, OFF_SV, OFF_G = 512, 1024, 1536, 1552, 2064, 2576

PIECE = DC * HALF
N_PIECE_SLOTS = 6
W1_CHUNKS, W2_CHUNKS = DC, DC // 2
CHUNKS = W1_CHUNKS + W2_CHUNKS
CHUNK = 2 * D

PIECES = ["qk", "v", "r", "sv", "u", "ga0", "ga1", "gb0", "gb1", "pa", "pb", "xk0", "xk1",
          "mx0", "mx1", "xv0", "xv1", "xq0", "xq1", "xo0", "xo1"]
LAST_USE = {"qk": "k", "v": "v1", "r": "r1", "sv": "sv1", "u": "u1", "ga0": "ga10", "ga1": "ga11",
            "gb0": "gb10", "gb1": "gb11", "pa": "ya11", "pb": "yb11", "xk0": "kT1", "xk1": "kT3",
            "mx0": "x110", "mx1": "x111", "xv0": "vm10", "xv1": "vm11", "xq0": "xq1", "xq1": "xq3",
            "xo0": "x210", "xo1": "x211"}
TN = ["00", "10", "01", "11"]

GROUPS = (["vecs", "xT0", "xT1", "xT2", "xT3", "aL", "q", "k", "v0", "la", "v1", "r0", "r1", "sv0", "sv1",
           "wsT", "u0", "u1", "att0", "att1", "koT", "memT0", "memT1", "memT2", "memT3",
           "ga00", "ga10", "kv0", "kv1", "kv2", "mix0", "mix1", "ga01", "ga11", "o0", "o1",
           "gb00", "gb10", "sboT0", "sboT1", "gb01", "gb11", "oT0", "oT1"]
          + ["ya" + t for t in TN] + ["yb" + t for t in TN]
          + ["kT0", "kT1", "kT2", "kT3", "mT0", "mT1", "mT2", "mT3"]
          + ["x1" + t for t in TN] + ["vm" + t for t in TN]
          + ["hT0", "hT1", "hT2", "hT3", "xq0", "xq1", "sc0", "sc1", "xq2", "xq3", "sc2", "sc3",
             "pT0", "pT1", "ao0", "ao1", "pT2", "pT3", "ao2", "ao3"]
          + ["x2" + t for t in TN]
          + ["hf0", "hf1", "hf2", "hf3", "lg", "pos", "gT"] + ["y" + t for t in TN])
INDEX = {g: n for n, g in enumerate(GROUPS)}
N_BANKS = 8


def bank_of(group):
    return INDEX[group] % N_BANKS


def use_of(group):
    return INDEX[group] // N_BANKS + 1


def layer_program(nc, a, out):
    with ExitStack() as ctx:
        def sb(name, shape, dt=F32):
            return ctx.enter_context(nc.sbuf_tensor(name, shape, dt))

        def sem(name):
            return ctx.enter_context(nc.semaphore(name))

        ps = ctx.enter_context(nc.psum_tensor("ps", [P, N_BANKS, HALF], F32))

        ring = sb("ring", [P, N_PIECE_SLOTS * PIECE])
        rows = sb("rows", [P, TT, D])
        normed = sb("normed", [P, TT, D])
        side = sb("side", [P, TT, D])
        hT = sb("hT", [P, DC, T])
        memT = sb("memT", [P, DC, T])
        shared = sb("shared", [P, 13 * 1024])
        ident = sb("ident", [P, P])
        upper = sb("upper", [P, P])
        ones = sb("ones", [P, P])
        keep_att = sb("keep_att", [P, P])
        scan_keep = sb("scan_keep", [P, T])
        slot_iota = sb("slot_iota", [P, SLOTS])
        exp_iota = sb("exp_iota", [P, N_EXP])
        vec_rows = sb("vec_rows", [32, P])
        vecs = sb("vecs", [P, 32])
        wa = sb("wa", [P, DC, RANK])
        wr = sb("wr", [P, DC, N_EXP])
        wa2 = sb("wa2", [RANK, 2 * P])
        aT = sb("aT", [RANK, T])
        router_bias = sb("router_bias", [P, N_EXP])
        stat = sb("stat", [P, 128])
        G_MIX, G_X, G_MEM, B_A, B_SGU = 0, 8, 16, 24, 26

        at = [0]

        def carve(cols, p=P):
            v = shared[0:p, at[0]:at[0] + cols]
            at[0] += cols
            assert at[0] <= 13 * 1024, at[0]
            return v

        def cut(v, *dims):
            if len(dims) == 2:
                return v.rearrange("p (a b) -> p a b", a=dims[0])
            return v.rearrange("p (a b c) -> p a b c", a=dims[0], b=dims[1])

        z = cut(carve(512), 2, T)
        lns = cut(carve(512), 2, T)
        cum = cut(carve(512), 2, T)
        ec = cut(carve(512), 2, T)
        q_in = cut(carve(512), 2, T)
        k_out = cut(carve(512), 2, T)
        kz = cut(carve(1024), GLA_H, T)
        values = cut(carve(1024), TT, WV)
        gate_r = cut(carve(1024), TT, WV)
        sgu_u = cut(carve(1024), TT, WV)
        sgu_v = cut(carve(1024), TT, WV)
        attz = carve(1024).rearrange("p (t h c) -> p t h c", t=TT, h=GLA_H)
        koz = carve(1024).rearrange("p (t m d) -> p t m d", t=TT, m=2)
        states = carve(3 * 512).rearrange("p (n f e) -> p n f e", n=3, f=2)
        w_sgu = cut(carve(512), SGU_G, P)
        w_sguT = cut(carve(512), SGU_G, P)
        g_out = carve(WV)
        g_sgu = sb("g_sgu", [P, WV])
        b_sgu = sb("b_sgu", [P, WV])
        o_rows = cut(shared[:, 0:1024], TT, WV)
        oT = cut(values.rearrange("p a b -> p (a b)"), 4, T)
        sboT = cut(kz.rearrange("p a b -> p (a b)"), 4, T)
        sq_o = cut(shared[:, 1024:2048], TT, WV)
        at[0] = 0
        kT = cut(carve(2048), DC, T)
        vm = cut(carve(2048), TT, D)
        probs = carve(4 * 512).rearrange("p (h t m) -> p h t m", h=XH, t=TT)
        probsT = carve(2 * 512).rearrange("p (b m t) -> p b m t", b=2, m=2)
        g_ffn = carve(D)
        g_final = carve(D)
        b2 = carve(D, N_EXP)
        b1 = memT[0:N_EXP].rearrange("p a b -> p (a b)")
        at[0] = 0
        table = cut(carve(TT * 160), TT, 160)
        gates = cut(carve(TT * VEXP), TT, VEXP)
        pick = carve(VEXP, N_EXP)
        eq = carve(TT * TOPK * N_EXP).rearrange("p (t k e) -> p t k e", t=TT, k=TOPK)
        lg = cut(carve(TT * N_EXP), TT, N_EXP)
        mask = cut(carve(TT * N_EXP), TT, N_EXP)
        gateT = carve(T, N_EXP)
        take = cut(carve(TT * SLOTS), TT, SLOTS)
        put = carve(TT * 2 * SLOTS).rearrange("p (t j s) -> p t j s", t=TT, j=2)
        putT = cut(carve(TT * P), TT, P)
        pick_e = carve(SLOTS, N_EXP)
        gathered = carve(HALF)
        xeT = cut(carve(HALF), 4, P)
        glu = carve(HALF)
        lin = carve(HALF)
        sig = carve(HALF)
        act = carve(HALF)
        actT = cut(carve(HALF), 4, P)
        y_rows = carve(HALF)
        trips = sb("trips", [1, 1], I32)
        top_i = sb("top_i", [P, TT, 8], U32)

        bank_filled = [sem(f"bank_filled{b}") for b in range(N_BANKS)]
        bank_emptied = [sem(f"bank_emptied{b}") for b in range(N_BANKS)]
        piece_full = [sem(f"piece_full{b}") for b in range(N_PIECE_SLOTS)]
        chunk_full = [sem(f"chunk_full{b}") for b in range(CHUNKS)]
        names = """x_in mem_in small_in wa_in wa2_in wsgu_in gsgu_in wr_in gffn_in gfin_in b1_in b2_in out_sent
            ident_made consts_made zeros_made wsgu_masked
            x_sq x_eps x_std x_rstd x_normed mem_sq mem_eps mem_std mem_rstd mem_normed
            z_abs z_exp z_ln logs_made cum_made cum_exp cum_neg_exp cum_diff rest_exp
            keys_made r_sig r_gate
            sv_stat sv_mv sv_eps sv_std sv_rstd sv_g sv_normed
            o_sq o_ss o_eps o_std o_rstd o_made
            mixed x1_sq x1_eps x1_std x1_rstd x1_normed
            s_max s_neg s_exp s_rec s_made
            x2_sq x2_eps x2_std x2_rstd x2_scaled x2_normed
            top_made idx_made idxf_made top_neg gate_exp gate_rec gate_made eq_made mask_made geq_made gate_table
            pos_masked table_made cnt_cmp cnt_sum cnt_mul trips_made pick_made
            take_made put_made pick_e_made gather_filled gather_copied xeT_filled xeT_made h_filled glu_made
            sig_made lin_made lin_glu act_made putT_filled putT_made actT_filled actT_made y_filled y_copied
            scatter_filled y_added chunk_used f_sq f_eps f_std f_rstd f_scaled f_made""".split()
        s = {n: sem(n) for n in names}

        block = ctx.enter_context(nc.Block())

        def piece(name):
            n = PIECES.index(name) % N_PIECE_SLOTS
            return ring[:, n * PIECE:(n + 1) * PIECE]

        def chunk(c):
            n = (2 * len(PIECES) + c) % CHUNKS
            return ring[:, n * CHUNK:(n + 1) * CHUNK]

        def bank(group):
            return ps[:, bank_of(group), :]

        def filled(eng, group):
            eng.wait_ge(bank_filled[bank_of(group)], use_of(group))

        def emptied(eng, group):
            eng.wait_ge(bank_emptied[bank_of(group)], use_of(group))

        w_in = a["w_in"]

        def piece_source(name):
            def cols(w, lo):
                return w.rearrange("(c p) n -> p c n", p=P)[:, :, lo:lo + HALF]
            lows = {"qk": 0, "v": OFF_V, "r": OFF_R, "u": OFF_U, "sv": OFF_SV, "ga0": OFF_G,
                    "ga1": OFF_G + HALF, "gb0": OFF_G + D, "gb1": OFF_G + D + HALF}
            if name in lows:
                return cols(w_in[0], lows[name]), DC
            if name in ("pa", "pb"):
                return a["w_proj_a" if name == "pa" else "w_proj_b"][0].rearrange("(c p) n -> p c n", p=P), DC // 2
            w = {"xk": "w_xk", "xv": "w_xv", "mx": "w_mix_out", "xq": "w_xq", "xo": "w_xo"}[name[:2]]
            return cols(a[w][0], HALF * int(name[2])), DC

        def rows_of(w, c):
            return piece(w).rearrange("p (c n) -> p c n", c=DC)[:, c, :]

        @block.sync
        def _(sp):
            def load_piece(n):
                if n >= N_PIECE_SLOTS:
                    filled(sp, LAST_USE[PIECES[n - N_PIECE_SLOTS]])
                src, c = piece_source(PIECES[n])
                sp.dma_start(piece(PIECES[n]).rearrange("p (c n) -> p c n", c=c), src).then_inc(
                    piece_full[n % N_PIECE_SLOTS], 16)

            def load_chunk(c, e):
                if c < W1_CHUNKS:
                    src, dst = a["w_e1"][0, e, c * P:(c + 1) * P, :], chunk(c)
                else:
                    k = c - W1_CHUNKS
                    src = a["w_e2"][0, e, 2 * k * P:2 * (k + 1) * P, :].rearrange("(i p) n -> p i n", i=2)
                    dst = chunk(c).rearrange("p (i n) -> p i n", i=2)
                sp.dma_start(dst, src).then_inc(chunk_full[c], 16)

            sp.dma_start(rows[:], a["x"][0].rearrange("(t p) d -> p t d", p=P)).then_inc(s["x_in"], 16)
            for n in range(len(PIECES)):
                load_piece(n)
                if n == 1:
                    sp.dma_start(side[:], a["mem"][0].rearrange("(t p) d -> p t d", p=P)).then_inc(s["mem_in"], 16)
            filled(sp, "kT0")
            sp.dma_start(g_ffn, a["norm_ffn_g"][0:1, :].to_broadcast([P, D])).then_inc(s["gffn_in"], 16)
            sp.dma_start(g_final, a["norm_final_g"].rearrange("(a d) -> a d", a=1).to_broadcast([P, D])).then_inc(
                s["gfin_in"], 16)
            sp.dma_start(b2, a["b_e2"][0]).then_inc(s["b2_in"], 16)
            for c in range(CHUNKS):
                if c % 2 == 0:
                    filled(sp, LAST_USE[PIECES[len(PIECES) - N_PIECE_SLOTS + c // 2]])
                load_chunk(c, 0)
                if c == 5:
                    filled(sp, "sc3")
                    sp.dma_start(b1, a["b_e1"][0]).then_inc(s["b1_in"], 16)
            sp.wait_ge(s["trips_made"], 1)
            n = sp.value_load(trips[0:1, 0:1], min_val=N_EXP, max_val=VEXP)
            with sp.Fori(1, n) as v:
                e = sp.snap(v % N_EXP)
                for c in range(CHUNKS):
                    if c < CHUNKS - 1:
                        sp.wait_ge(s["chunk_used"], (v - 1) * (CHUNKS - 1) + (c + 1))
                    else:
                        sp.wait_ge(s["y_filled"], v)
                    load_chunk(c, e)
            sp.wait_ge(s["f_made"], 1)
            sp.dma_start(out[0].rearrange("(t p) d -> p t d", p=P)[:, 0, :], rows[:, 0, :]).then_inc(s["out_sent"], 16)
            sp.wait_ge(s["f_made"], 2)
            sp.dma_start(out[0].rearrange("(t p) d -> p t d", p=P)[:, 1, :], rows[:, 1, :]).then_inc(s["out_sent"], 16)
            sp.wait_ge(s["out_sent"], 32)

        @block.gpsimd
        def _(pool):
            g = nc.gpsimd
            g.memset(ident[:], 0.0).then_inc(s["ident_made"], 1)
            pool.wait_ge(s["ident_made"], 1)
            g.affine_select(out=ident[:], in_=ident[:], compare_op=ALU.not_equal, fill=1.0, base=0,
                            pattern=[[-1, P]], channel_multiplier=1).then_inc(s["ident_made"], 1)
            g.memset(kz, 0.0)
            g.memset(attz, 0.0)
            g.memset(koz, 0.0)
            g.memset(states, 0.0).then_inc(s["zeros_made"], 1)
            g.memset(ones[:], 1.0)
            g.memset(scan_keep[:], 1.0).then_inc(s["consts_made"], 1)
            pool.wait_ge(s["consts_made"], 1)
            g.memset(scan_keep[:].rearrange("p (n c) -> p n c", c=GLA_C)[:, :, 0:1], 0.0)
            g.affine_select(out=upper[:], in_=ones[:], compare_op=ALU.is_ge, fill=0.0, base=-1,
                            pattern=[[1, P]], channel_multiplier=-1)
            g.affine_select(out=keep_att[:], in_=ones[:], compare_op=ALU.is_ge, fill=0.0, base=0,
                            pattern=[[1, P]], channel_multiplier=-1)
            g.iota(slot_iota[:], pattern=[[1, SLOTS]], base=0, channel_multiplier=0,
                   allow_small_or_imprecise_dtypes=True)
            g.iota(exp_iota[:], pattern=[[1, N_EXP]], base=0, channel_multiplier=0,
                   allow_small_or_imprecise_dtypes=True).then_inc(s["consts_made"], 1)
            pool.wait_ge(s["consts_made"], 2)
            g.memset(keep_att[0:64, 64:128], 0.0).then_inc(s["consts_made"], 1)
            pool.wait_ge(s["wsgu_in"], 16)
            g.affine_select(out=w_sgu, in_=w_sgu, compare_op=ALU.is_ge, fill=0.0, base=0,
                            pattern=[[0, SGU_G], [-1, P]], channel_multiplier=1).then_inc(s["wsgu_masked"], 1)

        @block.scalar
        def _(sc):
            A = nc.scalar
            small = [("norm_mix_g", G_MIX, 8), ("norm_x_g", G_X, 8), ("norm_mem_g", G_MEM, 8), ("gla_b_a", B_A, 2)]
            for name, r, n in small:
                sc.dma_start(vec_rows[r:r + n, :], a[name][0].rearrange("(c p) -> c p", p=P)).then_inc(s["small_in"], 16)
            sc.dma_start(vec_rows[B_SGU:B_SGU + 4, :], a["sgu_b"][0]).then_inc(s["small_in"], 16)
            sc.dma_start(vec_rows[30:32, :], a["gla_b_a"][0].rearrange("(c p) -> c p", p=P)).then_inc(s["small_in"], 16)
            sc.dma_start(wa[:], w_in[0].rearrange("(c p) n -> p c n", p=P)[:, :, OFF_A:OFF_A + RANK]).then_inc(
                s["wa_in"], 16)
            sc.dma_start(wa2[:], a["gla_w_a2"][0]).then_inc(s["wa2_in"], 16)
            sc.dma_start(w_sgu, a["sgu_w"][0].rearrange("g t s -> t g s")).then_inc(s["wsgu_in"], 16)
            sc.dma_start(g_out, a["gla_out_g"][0:1, :].to_broadcast([P, WV])).then_inc(s["gsgu_in"], 16)
            sc.dma_start(g_sgu[:], a["sgu_norm_g"][0:1, :].to_broadcast([P, WV])).then_inc(s["gsgu_in"], 16)
            sc.dma_start(b_sgu[:], a["sgu_norm_b"][0:1, :].to_broadcast([P, WV])).then_inc(s["gsgu_in"], 16)
            sc.dma_start(wr[:], a["w_router"][0].rearrange("(c p) n -> p c n", p=P)).then_inc(s["wr_in"], 16)
            sc.dma_start(router_bias[:], a["b_router"][0:1, :].to_broadcast([P, N_EXP])).then_inc(s["wr_in"], 16)

            def squares(src, scratch, col, done):
                for t in range(TT):
                    A.activation(scratch[:, t, :], src[:, t, :], ACT.Square,
                                 accum_out=stat[:, col + t:col + t + 1]).then_inc(s[done], 1)

            def root(col, n, ready, need, done):
                sc.wait_ge(s[ready], need)
                A.activation(stat[:, col:col + n], stat[:, col:col + n], ACT.Sqrt).then_inc(s[done], 1)

            def copy_out(group, dst):
                filled(sc, group)
                A.activation(dst, bank(group)[0:dst.shape[0], :].rearrange("p (a b) -> p a b", a=dst.shape[1])
                             if len(dst.shape) == 3 else bank(group), ACT.Copy).then_inc(
                    bank_emptied[bank_of(group)], 1)

            def scaled_T(group, dst, k, gain):
                filled(sc, group)
                for i in range(2):
                    last = A.activation(dst[:, 2 * k + i, :], bank(group)[:, i * T:(i + 1) * T], ACT.Copy,
                                        scale=vecs[:, gain + 2 * k + i:gain + 2 * k + i + 1])
                last.then_inc(bank_emptied[bank_of(group)], 1)

            sc.wait_ge(s["x_in"], 16)
            squares(rows, normed, 0, "x_sq")
            root(0, 2, "x_eps", 1, "x_std")
            emptied(sc, "vecs")
            scaled_T("xT1", hT, 1, G_MIX)
            scaled_T("xT3", hT, 3, G_MIX)
            sc.wait_ge(s["mem_in"], 16)
            squares(side, memT.rearrange("p c t -> p (c t)").rearrange("p (a b) -> p a b", a=TT), 2, "mem_sq")
            root(2, 2, "mem_eps", 1, "mem_std")
            copy_out("v0", values[:, 0, :])
            emptied(sc, "la")
            A.activation(lns, z, ACT.Abs).then_inc(s["z_abs"], 1)
            sc.wait_ge(s["z_abs"], 1)
            A.activation(lns, lns, ACT.Exp, scale=-1.0).then_inc(s["z_exp"], 1)
            sc.wait_ge(s["z_exp"], 1)
            A.activation(lns, lns, ACT.Ln, bias=1.0).then_inc(s["z_ln"], 1)
            copy_out("v1", values[:, 1, :])
            sc.wait_ge(s["cum_made"], 2)
            A.activation(ec, cum, ACT.Exp, scale=1.0 / TAU).then_inc(s["cum_exp"], 1)
            A.activation(z, cum, ACT.Exp, scale=-1.0 / TAU).then_inc(s["cum_neg_exp"], 1)
            sc.wait_ge(s["cum_diff"], 1)
            A.activation(lns, lns, ACT.Exp, scale=1.0 / TAU).then_inc(s["rest_exp"], 1)
            for t in range(TT):
                filled(sc, f"r{t}")
                A.activation(gate_r[:, t, :], bank(f"r{t}"), ACT.Sigmoid).then_inc(s["r_sig"], 1)
            for n, dst in (("sv", sgu_v), ("u", sgu_u)):
                for t in range(TT):
                    filled(sc, f"{n}{t}")
                    A.activation(dst[:, t, :], bank(f"{n}{t}"), ACT.Gelu).then_inc(bank_emptied[bank_of(f"{n}{t}")], 1)
            scaled_T("memT1", memT, 1, G_MEM)
            scaled_T("memT3", memT, 3, G_MEM)
            root(4, 2, "sv_eps", 1, "sv_std")

            def gate(name, t, n, dst):
                filled(sc, f"{name}{t}{n}")
                A.activation(dst[:, t, n * HALF:(n + 1) * HALF], bank(f"{name}{t}{n}"), ACT.Sigmoid).then_inc(
                    bank_emptied[bank_of(f"{name}{t}{n}")], 1)

            for n in range(2):
                for t in range(TT):
                    gate("ga", t, n, normed)
            for t in range(TT):
                filled(sc, f"o{t}")
                A.activation(sq_o[:, t, :], bank(f"o{t}"), ACT.Square).then_inc(s["o_sq"], 1)
            root(16, 8, "o_eps", 1, "o_std")
            for t in range(TT):
                gate("gb", t, 0, side)
            copy_out("sboT0", sboT[:, 0:2, :])
            copy_out("sboT1", sboT[:, 2:4, :])
            for t in range(TT):
                gate("gb", t, 1, side)
            copy_out("oT0", oT[:, 0:2, :])
            copy_out("oT1", oT[:, 2:4, :])
            for k in range(4):
                copy_out(f"kT{k}", kT[:, 2 * k:2 * k + 2, :])
            copy_out("mT1", hT[:, 2:4, :])
            copy_out("mT3", hT[:, 6:8, :])

            sc.wait_ge(bank_emptied[bank_of("x111")], use_of("x111"))
            emptied(sc, "x101")
            emptied(sc, "x110")
            emptied(sc, "x100")
            squares(rows, normed, 6, "x1_sq")
            root(6, 2, "x1_eps", 1, "x1_std")
            for n in range(2):
                for t in range(TT):
                    copy_out(f"vm{t}{n}", vm[:, t, n * HALF:(n + 1) * HALF])
            scaled_T("hT1", hT, 1, G_X)
            scaled_T("hT3", hT, 3, G_X)
            copy_out("xq0", memT[:, 0:2, :])
            copy_out("xq1", memT[:, 2:4, :])

            def soft(h):
                sc.wait_ge(s["s_neg"], h + 1)
                for t in range(TT):
                    A.activation(probs[:, h, t, :], bank(f"sc{h}")[:, t * T:(t + 1) * T], ACT.Exp, scale=XDH ** -0.5,
                                 bias=stat[:, 40 + 2 * h + t:41 + 2 * h + t],
                                 accum_out=stat[:, 48 + 2 * h + t:49 + 2 * h + t]).then_inc(s["s_exp"], 1)

            soft(0)
            soft(1)
            copy_out("xq2", memT[:, 4:6, :])
            copy_out("xq3", memT[:, 6:8, :])
            soft(2)
            soft(3)
            aoT = side.rearrange("p a b -> p (a b)").rearrange("p (c t) -> p c t", c=DC)
            for h in range(XH):
                copy_out(f"ao{h}", aoT[:, 2 * h:2 * h + 2, :])
            for g in TN:
                emptied(sc, "x2" + g)
            squares(rows, normed, 8, "x2_sq")
            root(8, 2, "x2_eps", 1, "x2_std")
            copy_out("hf1", hT[:, 2:4, :])
            copy_out("hf3", hT[:, 6:8, :])
            for t in range(TT):
                sc.wait_ge(s["top_neg"], t + 1)
                A.activation(stat[:, 80 + 4 * t:84 + 4 * t], stat[:, 64 + 8 * t:68 + 8 * t], ACT.Exp,
                             bias=stat[:, 60 + t:61 + t], accum_out=stat[:, 88 + t:89 + t]).then_inc(s["gate_exp"], 1)

            sc.wait_ge(s["gather_filled"], 1)
            A.activation(gathered, ps[:, 3, :], ACT.Copy).then_inc(s["gather_copied"], 1)
            sc.wait_ge(s["xeT_filled"], 1)
            A.activation(xeT, ps[:, 3, :].rearrange("p (a b) -> p a b", a=4), ACT.Copy).then_inc(s["xeT_made"], 1)
            sc.wait_ge(s["trips_made"], 1)
            n = sc.value_load(trips[0:1, 0:1], min_val=N_EXP, max_val=VEXP)
            with sc.Fori(0, n) as v:
                sc.wait_ge(s["putT_filled"], v + 1)
                A.activation(putT, ps[:, 4, 0:TT * P].rearrange("p (a b) -> p a b", a=TT), ACT.Copy).then_inc(
                    s["putT_made"], 1)
                sc.wait_ge(s["glu_made"], v + 1)
                A.activation(sig, glu, ACT.Sigmoid, scale=ALPHA).then_inc(s["sig_made"], 1)
                sc.wait_ge(s["gather_filled"], v + 2)
                A.activation(gathered, ps[:, 3, :], ACT.Copy).then_inc(s["gather_copied"], 1)
                sc.wait_ge(s["xeT_filled"], v + 2)
                A.activation(xeT, ps[:, 3, :].rearrange("p (a b) -> p a b", a=4), ACT.Copy).then_inc(s["xeT_made"], 1)
                sc.wait_ge(s["actT_filled"], v + 1)
                A.activation(actT, ps[:, 4, :].rearrange("p (a b) -> p a b", a=4), ACT.Copy).then_inc(s["actT_made"], 1)
                sc.wait_ge(s["y_filled"], v + 1)
                A.activation(y_rows, ps[:, 2, :], ACT.Copy).then_inc(s["y_copied"], 1)
            sc.wait_ge(s["y_added"], n * 4)
            squares(rows, normed, 10, "f_sq")
            root(10, 2, "f_eps", 1, "f_std")

        @block.vector
        def _(ve):
            V = nc.vector

            def eps_of(src_col, n, sq, need, done, width=D):
                ve.wait_ge(s[sq], need)
                V.tensor_scalar(stat[:, src_col:src_col + n], stat[:, src_col:src_col + n], 1.0 / width, EPS,
                                ALU.mult, ALU.add).then_inc(s[done], 1)

            def inv(col, n, std, done):
                ve.wait_ge(s[std], 1)
                V.reciprocal(stat[:, col:col + n], stat[:, col:col + n]).then_inc(s[done], 1)

            def scale_rows(dst, src, col, rstd, done):
                ve.wait_ge(s[rstd], 1)
                for t in range(TT):
                    V.tensor_scalar(dst[:, t, :], src[:, t, :], stat[:, col + t:col + t + 1], None,
                                    ALU.mult).then_inc(s[done], 1)

            def copy_out(group, dst):
                filled(ve, group)
                V.tensor_copy(dst, bank(group).rearrange("p (a b) -> p a b", a=dst.shape[1])
                              if len(dst.shape) == 3 else bank(group)).then_inc(bank_emptied[bank_of(group)], 1)

            def scaled_T(group, dst, k, gain):
                filled(ve, group)
                for i in range(2):
                    last = V.tensor_scalar(dst[:, 2 * k + i, :], bank(group)[:, i * T:(i + 1) * T],
                                           vecs[:, gain + 2 * k + i:gain + 2 * k + i + 1], None, ALU.mult)
                last.then_inc(bank_emptied[bank_of(group)], 1)

            filled(ve, "vecs")
            V.tensor_copy(vecs[:], bank("vecs")[:, 0:32]).then_inc(bank_emptied[bank_of("vecs")], 1)
            eps_of(0, 2, "x_sq", 2, "x_eps")
            inv(0, 2, "x_std", "x_rstd")
            scale_rows(normed, rows, 0, "x_rstd", "x_normed")
            emptied(ve, "vecs")
            scaled_T("xT0", hT, 0, G_MIX)
            scaled_T("xT2", hT, 2, G_MIX)
            eps_of(2, 2, "mem_sq", 2, "mem_eps")
            filled(ve, "aL")
            V.tensor_copy(aT[:], bank("aL")[0:RANK, 0:T]).then_inc(bank_emptied[bank_of("aL")], 1)
            filled(ve, "la")
            V.tensor_scalar(z[:, 0, :], bank("la")[:, 0:T], vecs[:, B_A:B_A + 1], None, ALU.add)
            V.tensor_scalar(z[:, 1, :], bank("la")[:, T:2 * T], vecs[:, B_A + 1:B_A + 2], None,
                            ALU.add).then_inc(bank_emptied[bank_of("la")], 1)
            inv(2, 2, "mem_std", "mem_rstd")
            scale_rows(side, side, 2, "mem_rstd", "mem_normed")
            ve.wait_ge(s["z_ln"], 1)
            logs = q_in
            V.scalar_tensor_tensor(logs, z, 0.0, lns, ALU.min, ALU.subtract).then_inc(s["logs_made"], 1)
            ve.wait_ge(s["logs_made"], 1)
            ve.wait_ge(s["consts_made"], 3)
            for f in range(2):
                V.tensor_tensor_scan(cum[:, f, :], scan_keep[:], logs[:, f, :], 0.0, ALU.mult, ALU.add).then_inc(
                    s["cum_made"], 1)
            ve.wait_ge(s["cum_made"], 2)
            cum4 = cum.rearrange("p f (n c) -> p (f n) c", c=GLA_C)
            V.tensor_tensor(lns.rearrange("p f (n c) -> p (f n) c", c=GLA_C),
                            cum4[:, :, GLA_C - 1:GLA_C].to_broadcast([P, 2 * NCH, GLA_C]), cum4,
                            ALU.subtract).then_inc(s["cum_diff"], 1)
            filled(ve, "q")
            ve.wait_ge(s["cum_exp"], 1)
            V.scalar_tensor_tensor(q_in, bank("q").rearrange("p (a b) -> p a b", a=2), GLA_DK ** -0.5, ec,
                                   ALU.mult, ALU.mult).then_inc(bank_emptied[bank_of("q")], 1)
            filled(ve, "k")
            ve.wait_ge(s["cum_neg_exp"], 1)
            ve.wait_ge(s["zeros_made"], 1)
            for h in range(GLA_H):
                p0, f = 64 * (h % 2), h // 2
                V.tensor_tensor(kz[p0:p0 + 64, h, :], bank("k")[p0:p0 + 64, f * T:(f + 1) * T], z[p0:p0 + 64, f, :],
                                ALU.mult).then_inc(s["keys_made"], 1)
            ve.wait_ge(s["rest_exp"], 1)
            V.tensor_tensor(k_out, bank("k").rearrange("p (a b) -> p a b", a=2), lns, ALU.mult).then_inc(
                bank_emptied[bank_of("k")], 1)
            ve.wait_ge(s["gsgu_in"], 48)
            for t in range(TT):
                ve.wait_ge(s["r_sig"], t + 1)
                V.tensor_tensor(gate_r[:, t, :], bank(f"r{t}"), gate_r[:, t, :], ALU.mult).then_inc(
                    bank_emptied[bank_of(f"r{t}")], 1)
                emptied(ve, f"r{t}")
                V.tensor_tensor(gate_r[:, t, :], gate_r[:, t, :], g_out, ALU.mult).then_inc(s["r_gate"], 1)
            copy_out("wsT", w_sguT)
            for t in range(TT):
                emptied(ve, f"sv{t}")
                V.bn_stats(stat[:, 96 + 6 * t:102 + 6 * t], sgu_v[:, t, :]).then_inc(s["sv_stat"], 1)
            for t in range(TT):
                ve.wait_ge(s["sv_stat"], t + 1)
                V.bn_aggr(stat[:, 112 + 2 * t:114 + 2 * t], stat[:, 96 + 6 * t:102 + 6 * t]).then_inc(s["sv_mv"], 1)
            ve.wait_ge(s["sv_mv"], 2)
            for t in range(TT):
                last = V.tensor_scalar(stat[:, 4 + t:5 + t], stat[:, 113 + 2 * t:114 + 2 * t], EPS, None, ALU.add)
            last.then_inc(s["sv_eps"], 1)
            for t in range(TT):
                filled(ve, f"att{t}")
                V.copy_predicated(attz[:, t], keep_att[:].bitcast(U32).unsqueeze(1).to_broadcast([P, GLA_H, P]),
                                  bank(f"att{t}").rearrange("p (h c) -> p h c", h=GLA_H)).then_inc(
                    bank_emptied[bank_of(f"att{t}")], 1)
            filled(ve, "koT")
            for m in range(2):
                last = V.tensor_copy(koz[64 * m:64 * m + 64, :, m, :],
                                     bank("koT")[64 * m:64 * m + 64, :].rearrange("p (t d) -> p t d", t=TT))
            last.then_inc(bank_emptied[bank_of("koT")], 1)
            scaled_T("memT0", memT, 0, G_MEM)
            scaled_T("memT2", memT, 2, G_MEM)
            inv(4, 2, "sv_std", "sv_rstd")
            ve.wait_ge(s["sv_rstd"], 1)
            for t in range(TT):
                V.tensor_scalar(sgu_v[:, t, :], sgu_v[:, t, :], stat[:, 112 + 2 * t:113 + 2 * t],
                                stat[:, 4 + t:5 + t], ALU.subtract, ALU.mult).then_inc(s["sv_g"], 1)
            for t in range(TT):
                ve.wait_ge(s["sv_g"], t + 1)
                V.tensor_tensor(sgu_v[:, t, :], sgu_v[:, t, :], g_sgu[:], ALU.mult).then_inc(s["sv_g"], 1)
            for t in range(TT):
                ve.wait_ge(s["sv_g"], t + 3)
                V.tensor_tensor(sgu_v[:, t, :], sgu_v[:, t, :], b_sgu[:], ALU.add).then_inc(s["sv_normed"], 1)
            for n in range(3):
                filled(ve, f"kv{n}")
                if n:
                    emptied(ve, f"kv{n - 1}")
                for f in range(2):
                    for hh in range(2):
                        q, e = slice(64 * hh, 64 * hh + 64), slice(P * hh, P * hh + P)
                        src = bank(f"kv{n}")[q, f * T + P * hh:f * T + P * hh + P]
                        if n == 0:
                            last = V.tensor_copy(states[q, n, f, e], src)
                        else:
                            last_token = GLA_C * n + GLA_C - 1
                            last = V.scalar_tensor_tensor(states[q, n, f, e], states[q, n - 1, f, e],
                                                         ec[q, f, last_token:last_token + 1], src, ALU.mult, ALU.add)
                last.then_inc(bank_emptied[bank_of(f"kv{n}")], 1)
            for t in range(TT):
                filled(ve, f"mix{t}")
                emptied(ve, f"u{t}")
                for g in range(SGU_G):
                    c = slice(g * P, (g + 1) * P)
                    last = V.scalar_tensor_tensor(sgu_u[:, t, c], bank(f"mix{t}")[:, c], vecs[:, B_SGU + g:B_SGU + g + 1],
                                                  sgu_u[:, t, c], ALU.add, ALU.mult)
                last.then_inc(bank_emptied[bank_of(f"mix{t}")], 1)
            for t in range(TT):
                ve.wait_ge(s["o_sq"], t + 1)
                V.tensor_reduce(stat[:, 16 + 4 * t:20 + 4 * t], sq_o[:, t, :].rearrange("p (h e) -> p h e", h=GLA_H),
                                AX, ALU.add).then_inc(s["o_ss"], 1)
            eps_of(16, 8, "o_ss", 2, "o_eps", GLA_DV)
            inv(16, 8, "o_std", "o_rstd")
            ve.wait_ge(s["o_rstd"], 1)
            for t in range(TT):
                V.tensor_tensor(o_rows[:, t, :].rearrange("p (h e) -> p h e", h=GLA_H),
                                bank(f"o{t}").rearrange("p (h e) -> p h e", h=GLA_H),
                                stat[:, 16 + 4 * t:20 + 4 * t].unsqueeze(2).to_broadcast([P, GLA_H, GLA_DV]),
                                ALU.mult).then_inc(bank_emptied[bank_of(f"o{t}")], 1)
            ve.wait_ge(s["r_gate"], 2)
            for t in range(TT):
                emptied(ve, f"o{t}")
                V.tensor_tensor(o_rows[:, t, :], o_rows[:, t, :], gate_r[:, t, :], ALU.mult).then_inc(s["o_made"], 1)
            for g in TN:
                t, n = int(g[0]), int(g[1])
                c = slice(n * HALF, (n + 1) * HALF)
                filled(ve, "ya" + g)
                emptied(ve, "ga" + g)
                V.tensor_tensor(normed[:, t, c], bank("ya" + g), normed[:, t, c], ALU.mult).then_inc(
                    bank_emptied[bank_of("ya" + g)], 1)
            for g in TN:
                t, n = int(g[0]), int(g[1])
                c = slice(n * HALF, (n + 1) * HALF)
                filled(ve, "yb" + g)
                emptied(ve, "gb" + g)
                V.tensor_tensor(side[:, t, c], bank("yb" + g), side[:, t, c], ALU.mult).then_inc(
                    bank_emptied[bank_of("yb" + g)], 1)
                emptied(ve, "yb" + g)
                emptied(ve, "ya" + g)
                V.tensor_tensor(normed[:, t, c], normed[:, t, c], side[:, t, c], ALU.add).then_inc(s["mixed"], 1)
            copy_out("mT0", hT[:, 0:2, :])
            copy_out("mT2", hT[:, 4:6, :])

            def add_rows(name):
                for g in TN:
                    t, n = int(g[0]), int(g[1])
                    c = slice(n * HALF, (n + 1) * HALF)
                    filled(ve, name + g)
                    V.tensor_tensor(rows[:, t, c], bank(name + g), rows[:, t, c], ALU.add).then_inc(
                        bank_emptied[bank_of(name + g)], 1)

            add_rows("x1")
            eps_of(6, 2, "x1_sq", 2, "x1_eps")
            inv(6, 2, "x1_std", "x1_rstd")
            scale_rows(normed, rows, 6, "x1_rstd", "x1_normed")
            scaled_T("hT0", hT, 0, G_X)
            scaled_T("hT2", hT, 2, G_X)

            def row_max(h):
                filled(ve, f"sc{h}")
                V.tensor_reduce(stat[:, 32 + 2 * h:34 + 2 * h], bank(f"sc{h}").rearrange("p (t m) -> p t m", t=TT),
                                AX, ALU.max).then_inc(s["s_max"], 1)
                ve.wait_ge(s["s_max"], h + 1)
                V.tensor_scalar(stat[:, 40 + 2 * h:42 + 2 * h], stat[:, 32 + 2 * h:34 + 2 * h], -(XDH ** -0.5), None,
                                ALU.mult).then_inc(s["s_neg"], 1)

            def normalise(h):
                ve.wait_ge(s["s_exp"], 2 * h + 2)
                V.reciprocal(stat[:, 32 + 2 * h:34 + 2 * h], stat[:, 48 + 2 * h:50 + 2 * h]).then_inc(s["s_rec"], 1)
                ve.wait_ge(s["s_rec"], h + 1)
                V.tensor_tensor(probs[:, h], probs[:, h],
                                stat[:, 32 + 2 * h:34 + 2 * h].unsqueeze(2).to_broadcast([P, TT, T]),
                                ALU.mult).then_inc(bank_emptied[bank_of(f"sc{h}")], 1)

            row_max(0)
            row_max(1)
            normalise(0)
            normalise(1)
            row_max(2)
            row_max(3)
            normalise(2)
            normalise(3)
            for h in range(XH):
                if h >= 2:
                    filled(ve, f"ao{h - 2}")
                copy_out(f"pT{h}", probsT[:, h % 2])
            add_rows("x2")
            eps_of(8, 2, "x2_sq", 2, "x2_eps")
            inv(8, 2, "x2_std", "x2_rstd")
            scale_rows(normed, rows, 8, "x2_rstd", "x2_scaled")
            ve.wait_ge(s["gffn_in"], 16)
            for t in range(TT):
                ve.wait_ge(s["x2_scaled"], t + 1)
                V.tensor_tensor(normed[:, t, :], normed[:, t, :], g_ffn, ALU.mult).then_inc(s["x2_normed"], 1)
            copy_out("hf0", hT[:, 0:2, :])
            copy_out("hf2", hT[:, 4:6, :])
            filled(ve, "lg")
            ve.wait_ge(s["wr_in"], 32)
            V.tensor_tensor(lg, bank("lg")[:, 0:TT * N_EXP].rearrange("p (t e) -> p t e", t=TT),
                            router_bias[:].unsqueeze(1).to_broadcast([P, TT, N_EXP]), ALU.add).then_inc(
                bank_emptied[bank_of("lg")], 1)
            emptied(ve, "lg")
            for t in range(TT):
                V.max(stat[:, 64 + 8 * t:72 + 8 * t], lg[:, t, :]).then_inc(s["top_made"], 1)
            for t in range(TT):
                ve.wait_ge(s["top_made"], t + 1)
                V.tensor_scalar(stat[:, 60 + t:61 + t], stat[:, 64 + 8 * t:65 + 8 * t], -1.0, None,
                                ALU.mult).then_inc(s["top_neg"], 1)
            for t in range(TT):
                V.max_index(top_i[:, t, :], stat[:, 64 + 8 * t:72 + 8 * t], lg[:, t, :]).then_inc(s["idx_made"], 1)
            ve.wait_ge(s["idx_made"], 2)
            idx = stat[:, 0:8].rearrange("p (t k) -> p t k", t=TT)
            V.tensor_copy(idx, top_i[:, :, 0:TOPK]).then_inc(s["idxf_made"], 1)
            ve.wait_ge(s["idxf_made"], 1)
            for t in range(TT):
                V.tensor_tensor(eq[:, t], idx[:, t, :].unsqueeze(2).to_broadcast([P, TOPK, N_EXP]),
                                exp_iota[:].unsqueeze(1).to_broadcast([P, TOPK, N_EXP]), ALU.is_equal).then_inc(
                    s["eq_made"], 1)
            ve.wait_ge(s["eq_made"], 2)
            V.tensor_reduce(mask, eq.rearrange("p t k e -> p t e k"), AX, ALU.add).then_inc(s["mask_made"], 1)
            for t in range(TT):
                ve.wait_ge(s["gate_exp"], t + 1)
                V.reciprocal(stat[:, 90 + t:91 + t], stat[:, 88 + t:89 + t]).then_inc(s["gate_rec"], 1)
            for t in range(TT):
                ve.wait_ge(s["gate_rec"], t + 1)
                V.tensor_scalar(stat[:, 80 + 4 * t:84 + 4 * t], stat[:, 80 + 4 * t:84 + 4 * t],
                                stat[:, 90 + t:91 + t], None, ALU.mult).then_inc(s["gate_made"], 1)
            ve.wait_ge(s["mask_made"], 1)
            for t in range(TT):
                ve.wait_ge(s["gate_made"], t + 1)
                V.tensor_tensor(eq[:, t], eq[:, t],
                                stat[:, 80 + 4 * t:84 + 4 * t].unsqueeze(2).to_broadcast([P, TOPK, N_EXP]),
                                ALU.mult).then_inc(s["geq_made"], 1)
            ve.wait_ge(s["geq_made"], 2)
            for r in range(ROUNDS):
                V.tensor_reduce(gates[:, :, r * N_EXP:(r + 1) * N_EXP], eq.rearrange("p t k e -> p t e k"), AX,
                                ALU.add).then_inc(s["gate_table"], 1)
            filled(ve, "pos")
            V.scalar_tensor_tensor(lg, bank("pos")[:, 0:TT * N_EXP].rearrange("p (t e) -> p t e", t=TT), 1.0, mask,
                                   ALU.add, ALU.mult).then_inc(s["pos_masked"], 1)
            V.tensor_reduce(stat[:, 92:93], bank("pos")[:, TT * N_EXP:3 * N_EXP], AX, ALU.max).then_inc(
                bank_emptied[bank_of("pos")], 1)
            ve.wait_ge(s["pos_masked"], 1)
            for r in range(ROUNDS):
                V.tensor_scalar(table[:, :, r * N_EXP:(r + 1) * N_EXP], lg, float(-1 - SLOTS * r), None, ALU.add)
            V.memset(table[:, :, VEXP:160], -1.0).then_inc(s["table_made"], 1)
            emptied(ve, "pos")
            V.tensor_scalar(stat[0:1, 100:100 + ROUNDS - 1], slot_iota[0:1, 1:ROUNDS], float(SLOTS), stat[0:1, 92:93],
                            ALU.mult, ALU.is_lt).then_inc(s["cnt_cmp"], 1)
            ve.wait_ge(s["cnt_cmp"], 1)
            V.tensor_reduce(stat[0:1, 104:105], stat[0:1, 100:100 + ROUNDS - 1], AX, ALU.add).then_inc(s["cnt_sum"], 1)
            ve.wait_ge(s["cnt_sum"], 1)
            V.tensor_scalar(stat[0:1, 105:106], stat[0:1, 104:105], 1.0, float(N_EXP), ALU.add,
                            ALU.mult).then_inc(s["cnt_mul"], 1)
            ve.wait_ge(s["cnt_mul"], 1)
            V.tensor_copy(trips[0:1, 0:1], stat[0:1, 105:106]).then_inc(s["trips_made"], 1)
            V.tensor_copy(pick.rearrange("p (r e) -> p r e", r=ROUNDS),
                          ident[0:N_EXP, 0:N_EXP].unsqueeze(1).to_broadcast([N_EXP, ROUNDS, N_EXP])).then_inc(
                s["pick_made"], 1)

            def make_take(v):
                for t in range(TT):
                    last = V.tensor_scalar(take[:, t, :], slot_iota[:], table[:, t, bass.ds(v, 1)], None, ALU.is_equal)
                last.then_inc(s["take_made"], 1)

            ve.wait_ge(s["table_made"], 1)
            for t in range(TT):
                last = V.tensor_scalar(take[:, t, :], slot_iota[:], table[:, t, 0:1], None, ALU.is_equal)
            last.then_inc(s["take_made"], 1)
            filled(ve, "gT")
            V.tensor_copy(gateT, bank("gT")[0:N_EXP, 0:T]).then_inc(bank_emptied[bank_of("gT")], 1)
            add_rows("y")
            for g in TN:
                emptied(ve, "y" + g)
            ve.wait_ge(s["gate_table"], ROUNDS)
            ve.wait_ge(s["pick_made"], 1)
            ve.wait_ge(s["trips_made"], 1)
            n = ve.value_load(trips[0:1, 0:1], min_val=N_EXP, max_val=VEXP)
            with ve.Fori(0, n) as v:
                ve.wait_ge(s["gather_filled"], v + 1)
                make_take(v + 1)
                for t in range(TT):
                    last = V.tensor_scalar(put[:, t], slot_iota[:].unsqueeze(1).to_broadcast([P, 2, SLOTS]),
                                           table[:, t, bass.ds(v, 1)], gates[:, t, bass.ds(v, 1)],
                                           ALU.is_equal, ALU.mult)
                last.then_inc(s["put_made"], 1)
                V.tensor_scalar(pick_e, ones[0:N_EXP, 0:SLOTS], pick[:, bass.ds(v, 1)], None,
                                ALU.mult).then_inc(s["pick_e_made"], 1)
                ve.wait_ge(s["h_filled"], v + 1)
                V.tensor_scalar(glu, ps[:, 0, :], LIMIT, None, ALU.min).then_inc(s["glu_made"], 1)
                V.tensor_scalar(lin, ps[:, 1, :], LIMIT, -LIMIT, ALU.min, ALU.max).then_inc(s["lin_made"], 1)
                ve.wait_ge(s["lin_made"], v + 1)
                V.scalar_tensor_tensor(lin, lin, 1.0, glu, ALU.add, ALU.mult).then_inc(s["lin_glu"], 1)
                ve.wait_ge(s["lin_glu"], v + 1)
                ve.wait_ge(s["sig_made"], v + 1)
                V.tensor_tensor(act, lin, sig, ALU.mult).then_inc(s["act_made"], 1)
                for t in range(TT):
                    for j in range(2):
                        k = 2 * t + j
                        c = slice(j * HALF, (j + 1) * HALF)
                        ve.wait_ge(s["scatter_filled"], v * 4 + (k + 1))
                        V.tensor_tensor(rows[:, t, c], ps[:, (5, 6, 7, 2)[k], :], rows[:, t, c], ALU.add).then_inc(
                            s["y_added"], 1)
            eps_of(10, 2, "f_sq", 2, "f_eps")
            inv(10, 2, "f_std", "f_rstd")
            scale_rows(rows, rows, 10, "f_rstd", "f_scaled")
            ve.wait_ge(s["gfin_in"], 16)
            for t in range(TT):
                ve.wait_ge(s["f_scaled"], t + 1)
                V.tensor_tensor(rows[:, t, :], rows[:, t, :], g_final, ALU.mult).then_inc(s["f_made"], 1)

        @block.tensor
        def _(pe):
            M = nc.tensor

            def start_group(group):
                if INDEX[group] >= N_BANKS:
                    pe.wait_ge(bank_emptied[bank_of(group)], use_of(group) - 1)

            def end_group(ins, group):
                ins.then_inc(bank_filled[bank_of(group)], 1)

            def has_piece(name):
                n = PIECES.index(name)
                pe.wait_ge(piece_full[n % N_PIECE_SLOTS], 16 * (n // N_PIECE_SLOTS + 1))

            def transposes(group, blocks):
                start_group(group)
                for n, (src, rows_) in enumerate(blocks):
                    w = src.shape[0]
                    last = M.transpose(bank(group)[0:rows_, n * w:(n + 1) * w], src, ident[0:w, 0:w])
                end_group(last, group)

            def rows_T(prefix, src, ready):
                for k in range(4):
                    start_group(f"{prefix}{k}")
                    for i in range(2):
                        for t in range(TT):
                            if k == 0 and i == 0:
                                pe.wait_ge(s[ready], t + 1)
                            c = 2 * k + i
                            last = M.transpose(bank(f"{prefix}{k}")[:, i * T + t * P:i * T + (t + 1) * P],
                                               src[:, t, c * P:(c + 1) * P], ident[:])
                    end_group(last, f"{prefix}{k}")

            def row_product(group, lhs, weight, t, c_count=DC):
                start_group(group)
                for c in range(c_count):
                    last = M.matmul(bank(group), lhs[:, c, t * P:(t + 1) * P], weight(c), start=c == 0,
                                    stop=c == c_count - 1)
                end_group(last, group)

            def feature_product(group, name, f0, rhs, n=2):
                start_group(group)
                for i in range(n):
                    for c in range(DC):
                        last = M.matmul(bank(group)[:, i * T:(i + 1) * T],
                                        rows_of(name, c)[:, (f0 + i) * P:(f0 + i + 1) * P],
                                        rhs[:, c, :], start=c == 0, stop=c == DC - 1)
                end_group(last, group)

            pe.wait_ge(s["ident_made"], 2)
            pe.wait_ge(s["small_in"], 16 * 6)
            transposes("vecs", [(vec_rows[:], P)])
            rows_T("xT", normed, "x_normed")
            for k in range(4):
                emptied(pe, f"xT{k}")
            pe.wait_ge(s["wa_in"], 16)
            start_group("aL")
            for c in range(DC):
                last = M.matmul(bank("aL")[0:RANK, 0:T], wa[:, c, :], hT[:, c, :], start=c == 0, stop=c == DC - 1)
            end_group(last, "aL")
            has_piece("qk")
            feature_product("q", "qk", 0, hT)
            feature_product("k", "qk", 2, hT)
            has_piece("v")
            row_product("v0", hT, lambda c: rows_of("v", c), 0)
            emptied(pe, "aL")
            pe.wait_ge(s["wa2_in"], 16)
            start_group("la")
            for f in range(2):
                last = M.matmul(bank("la")[:, f * T:(f + 1) * T], wa2[:, f * P:(f + 1) * P], aT[:], start=True, stop=True)
            end_group(last, "la")
            row_product("v1", hT, lambda c: rows_of("v", c), 1)
            for name in ("r", "sv"):
                has_piece(name)
                for t in range(TT):
                    row_product(f"{name}{t}", hT, lambda c: rows_of(name, c), t)
            pe.wait_ge(s["wsgu_masked"], 1)
            transposes("wsT", [(w_sgu[:, g, :], P) for g in range(SGU_G)])
            has_piece("u")
            for t in range(TT):
                row_product(f"u{t}", hT, lambda c: rows_of("u", c), t)
            emptied(pe, "q")
            pe.wait_ge(s["keys_made"], GLA_H)
            for t in range(TT):
                start_group(f"att{t}")
                for h in range(GLA_H):
                    last = M.matmul(bank(f"att{t}")[:, h * P:(h + 1) * P], kz[:, h, t * P:(t + 1) * P],
                                    q_in[:, h // 2, t * P:(t + 1) * P], start=True, stop=True)
                end_group(last, f"att{t}")
            emptied(pe, "k")
            transposes("koT", [(k_out[:, f, t * P:(t + 1) * P], P) for t in range(TT) for f in range(2)])
            rows_T("memT", side, "mem_normed")

            def gate_product(name, t, n):
                if t == 0:
                    has_piece(f"{name}{n}")
                row_product(f"{name}{t}{n}", hT, lambda c: rows_of(f"{name}{n}", c), t)

            gate_product("ga", 0, 0)
            gate_product("ga", 1, 0)
            emptied(pe, "koT")
            emptied(pe, "v1")
            emptied(pe, "v0")
            for n in range(3):
                start_group(f"kv{n}")
                for f in range(2):
                    last = M.matmul(bank(f"kv{n}")[:, f * T:(f + 1) * T], koz[:, n // 2, n % 2, f * P:(f + 1) * P],
                                    values[:, n // 2, f * T:(f + 1) * T], start=True, stop=True)
                end_group(last, f"kv{n}")
            emptied(pe, "wsT")
            pe.wait_ge(s["sv_normed"], 2)
            for t in range(TT):
                start_group(f"mix{t}")
                for g in range(SGU_G):
                    c = slice(g * P, (g + 1) * P)
                    last = M.matmul(bank(f"mix{t}")[:, c], w_sguT[:, g, :], sgu_v[:, t, c], start=True, stop=True)
                end_group(last, f"mix{t}")
            gate_product("ga", 0, 1)
            gate_product("ga", 1, 1)
            emptied(pe, "att0")
            emptied(pe, "att1")
            for t in range(TT):
                start_group(f"o{t}")
                emptied(pe, f"kv{2 * t}")
                todo = []
                for h in range(GLA_H):
                    c = slice(h * P, (h + 1) * P)
                    todo.append((bank(f"o{t}")[:, c], attz[:, t, h, :], values[:, t, c]))
                for m in range(2):
                    n = 2 * t + m
                    if n:
                        for f in range(2):
                            todo.append((bank(f"o{t}")[64 * m:64 * m + 64, f * T:(f + 1) * T],
                                         q_in[:, f, n * GLA_C:(n + 1) * GLA_C], states[:, n - 1, f, :]))
                for i, (o, l, r) in enumerate(todo):
                    last = M.matmul(o, l, r, start=i == 0, stop=i == len(todo) - 1, skip_group_check=True)
                end_group(last, f"o{t}")
            gate_product("gb", 0, 0)
            gate_product("gb", 1, 0)
            for t in range(TT):
                emptied(pe, f"mix{t}")
            for k in range(2):
                transposes(f"sboT{k}", [(sgu_u[:, t, (2 * k + i) * P:(2 * k + i + 1) * P], P)
                                        for i in range(2) for t in range(TT)])
            gate_product("gb", 0, 1)
            gate_product("gb", 1, 1)
            pe.wait_ge(s["o_made"], 2)
            for k in range(2):
                transposes(f"oT{k}", [(o_rows[:, t, (2 * k + i) * P:(2 * k + i + 1) * P], P)
                                      for i in range(2) for t in range(TT)])
            for branch, src, name, tr in (("ya", oT, "pa", "oT"), ("yb", sboT, "pb", "sboT")):
                emptied(pe, tr + "0")
                emptied(pe, tr + "1")
                has_piece(name)
                w = piece(name).rearrange("p (c n) -> p c n", c=DC // 2)
                for g in TN:
                    t, n = int(g[0]), int(g[1])
                    row_product(branch + g, src, lambda c: w[:, c, n * HALF:(n + 1) * HALF], t, DC // 2)
            for k in range(4):
                emptied(pe, f"memT{k}")
            for k in range(4):
                if k % 2 == 0:
                    has_piece(f"xk{k // 2}")
                feature_product(f"kT{k}", f"xk{k // 2}", 2 * (k % 2), memT)
            pe.wait_ge(s["mixed"], 4)
            rows_T("mT", normed, "mixed")

            def full_rows(group, src, name):
                for g in TN:
                    t, n = int(g[0]), int(g[1])
                    if t == 0:
                        has_piece(f"{name}{n}")
                    row_product(group + g, src, lambda c: rows_of(f"{name}{n}", c), t)

            for k in range(4):
                emptied(pe, f"mT{k}")
            full_rows("x1", hT, "mx")
            full_rows("vm", memT, "xv")
            rows_T("hT", normed, "x1_normed")
            for k in range(4):
                emptied(pe, f"hT{k}")

            def queries(k):
                if k % 2 == 0:
                    has_piece(f"xq{k // 2}")
                feature_product(f"xq{k}", f"xq{k // 2}", 2 * (k % 2), hT)

            def scores(h):
                emptied(pe, f"xq{h}")
                emptied(pe, f"kT{h}")
                start_group(f"sc{h}")
                for t in range(TT):
                    for i in range(2):
                        last = M.matmul(bank(f"sc{h}")[:, t * T:(t + 1) * T], memT[:, 2 * h + i, t * P:(t + 1) * P],
                                        kT[:, 2 * h + i, :], start=i == 0, stop=i == 1)
                end_group(last, f"sc{h}")

            def probs_T(h):
                emptied(pe, f"sc{h}")
                transposes(f"pT{h}", [(probs[:, h, t, m * P:(m + 1) * P], P) for m in range(2) for t in range(TT)])

            def attend(h):
                emptied(pe, f"pT{h}")
                if h == 0:
                    for g in TN:
                        emptied(pe, "vm" + g)
                start_group(f"ao{h}")
                for i in range(2):
                    for m in range(2):
                        c = XDH * h + P * i
                        last = M.matmul(bank(f"ao{h}")[:, i * T:(i + 1) * T], vm[:, m, c:c + P], probsT[:, h % 2, m, :],
                                        start=m == 0, stop=m == 1)
                end_group(last, f"ao{h}")

            queries(0)
            queries(1)
            scores(0)
            scores(1)
            queries(2)
            queries(3)
            scores(2)
            scores(3)
            probs_T(0)
            probs_T(1)
            attend(0)
            attend(1)
            probs_T(2)
            probs_T(3)
            attend(2)
            attend(3)
            aoT = side.rearrange("p a b -> p (a b)").rearrange("p (c t) -> p c t", c=DC)
            for h in range(XH):
                emptied(pe, f"ao{h}")
            full_rows("x2", aoT, "xo")
            rows_T("hf", normed, "x2_normed")
            for k in range(4):
                emptied(pe, f"hf{k}")
            pe.wait_ge(s["wr_in"], 32)
            start_group("lg")
            for t in range(TT):
                for c in range(DC):
                    last = M.matmul(bank("lg")[:, t * N_EXP:(t + 1) * N_EXP], hT[:, c, t * P:(t + 1) * P], wr[:, c, :],
                                    start=c == 0, stop=c == DC - 1)
            end_group(last, "lg")
            pe.wait_ge(s["mask_made"], 1)
            start_group("pos")
            pos = [(0, upper, 0), (1, upper, 1), (1, ones, 0), (2, ones, 0), (2, ones, 1)]
            for n, (o, l, t) in enumerate(pos):
                last = M.matmul(bank("pos")[:, o * N_EXP:(o + 1) * N_EXP], l[:], mask[:, t, :], start=n == 0,
                                stop=n == len(pos) - 1, skip_group_check=True)
            end_group(last, "pos")
            pe.wait_ge(s["gate_table"], ROUNDS)
            transposes("gT", [(gates[:, t, 0:N_EXP], N_EXP) for t in range(TT)])
            emptied(pe, "gT")
            pe.wait_ge(s["b2_in"], 16)
            for g in TN:
                t, n = int(g[0]), int(g[1])
                start_group("y" + g)
                end_group(M.matmul(bank("y" + g), gateT[:, t * P:(t + 1) * P], b2[:, n * HALF:(n + 1) * HALF],
                                   start=True, stop=True), "y" + g)
            for g in GROUPS[-N_BANKS:]:
                emptied(pe, g)

            def gather(need_take):
                pe.wait_ge(s["take_made"], need_take)
                for t in range(TT):
                    for j in range(2):
                        last = M.matmul(ps[64 * j:64 * j + 64, 3, :], take[:, t, :],
                                        normed[:, t, j * HALF:(j + 1) * HALF], start=t == 0, stop=t == 1,
                                        skip_group_check=True)
                last.then_inc(s["gather_filled"], 1)

            def gather_T(need_copy):
                pe.wait_ge(s["gather_copied"], need_copy)
                for q in range(4):
                    last = M.transpose(ps[:, 3, q * P:(q + 1) * P], gathered[:, q * P:(q + 1) * P], ident[:])
                last.then_inc(s["xeT_filled"], 1)

            gather(1)
            gather_T(1)
            pe.wait_ge(s["b1_in"], 16)
            pe.wait_ge(s["trips_made"], 1)
            n = pe.value_load(trips[0:1, 0:1], min_val=N_EXP, max_val=VEXP)
            with pe.Fori(0, n) as v:
                pe.wait_ge(s["xeT_made"], v + 1)
                for c in range(W1_CHUNKS):
                    pe.wait_ge(chunk_full[c], v * 16 + 16)
                    for i in range(2):
                        for j in range(2):
                            last = M.matmul(ps[64 * j:64 * j + 64, i, :], xeT[:, c % 4, (c // 4) * SLOTS:(c // 4 + 1) * SLOTS],
                                            chunk(c)[:, i * D + j * HALF:i * D + (j + 1) * HALF],
                                            start=c == 0, stop=False, skip_group_check=True)
                    last.then_inc(s["chunk_used"], 1)
                pe.wait_ge(s["pick_e_made"], v + 1)
                for i in range(2):
                    for j in range(2):
                        last = M.matmul(ps[64 * j:64 * j + 64, i, :], pick_e, b1[:, i * D + j * HALF:i * D + (j + 1) * HALF],
                                        start=False, stop=True, skip_group_check=True)
                last.then_inc(s["h_filled"], 1)
                pe.wait_ge(s["put_made"], v + 1)
                for t in range(TT):
                    last = M.transpose(ps[:, 4, t * P:(t + 1) * P], put[:, t].rearrange("p j s -> p (j s)"), ident[:])
                last.then_inc(s["putT_filled"], 1)
                gather(v + 2)
                gather_T(v + 2)
                pe.wait_ge(s["act_made"], v + 1)
                pe.wait_ge(s["putT_made"], v + 1)
                for q in range(4):
                    last = M.transpose(ps[:, 4, q * P:(q + 1) * P], act[:, q * P:(q + 1) * P], ident[:])
                last.then_inc(s["actT_filled"], 1)
                pe.wait_ge(s["actT_made"], v + 1)
                for k in range(W2_CHUNKS):
                    pe.wait_ge(chunk_full[W1_CHUNKS + k], v * 16 + 16)
                    w = chunk(W1_CHUNKS + k).rearrange("p (i n) -> p i n", i=2)
                    for i in range(2):
                        c = 2 * k + i
                        for j in range(2):
                            last = M.matmul(ps[64 * j:64 * j + 64, 2, :], actT[:, c % 4, (c // 4) * SLOTS:(c // 4 + 1) * SLOTS],
                                            w[:, i, j * HALF:(j + 1) * HALF], start=c == 0, stop=c == DC - 1,
                                            skip_group_check=True)
                    last.then_inc(s["chunk_used"] if k < W2_CHUNKS - 1 else s["y_filled"], 1)
                pe.wait_ge(s["y_copied"], v + 1)
                for t in range(TT):
                    for j in range(2):
                        q = slice(64 * j, 64 * j + 64)
                        M.matmul(ps[:, (5, 6, 7, 2)[2 * t + j], :], putT[q, t, :], y_rows[q, :], start=True,
                                 stop=True).then_inc(s["scatter_filled"], 1)


INPUTS = ["x", "mem", "norm_mix_g", "w_in", "gla_w_a2", "gla_b_a", "gla_out_g", "sgu_norm_g", "sgu_norm_b", "sgu_w",
          "sgu_b", "w_proj_a", "w_proj_b", "w_mix_out", "norm_x_g", "norm_mem_g", "w_xq", "w_xk", "w_xv", "w_xo",
          "norm_ffn_g", "w_router", "b_router", "w_e1", "b_e1", "w_e2", "b_e2", "norm_final_g"]


def kernel(**inputs):
    import numpy as np
    import concourse.bacc as bacc
    from concourse.bass_utils import run_bass_kernel_spmd

    nc = bacc.Bacc("TRN2", target_bir_lowering=False, num_devices=1)
    arrays = {f"in_{n}": np.ascontiguousarray(inputs[n]) for n in INPUTS}
    aps = {n: nc.dram_tensor(f"in_{n}", arrays[f"in_{n}"].shape, F32, kind="ExternalInput").ap() for n in INPUTS}
    out = nc.dram_tensor("out", (1, T, D), F32, kind="ExternalOutput").ap()
    layer_program(nc, aps, out)
    result = run_bass_kernel_spmd(nc, [arrays], core_ids=[0])
    return result.results[0]["out"]
```

```python
from contextlib import ExitStack

import concourse.bass as bass
from concourse import mybir

P = 128
F32 = mybir.dt.float32
F32R = mybir.dt.float32r
I32 = mybir.dt.int32
U32 = mybir.dt.uint32
ALU = mybir.AluOpType
ACT = mybir.ActivationFunctionType
AX = mybir.AxisListType.X

EPS = 1e-5
T = 256
TT = T // P
D = 1024
DC = D // P
HALF = 512
GLA_H, GLA_DK, GLA_DV, GLA_C, RANK, TAU = 4, 64, 128, 64, 16, 16.0
NCH = T // GLA_C
WV = GLA_H * GLA_DV
SGU_G = 4
XH, XDH = 4, 256
N_EXP, TOPK, LIMIT, ALPHA = 32, 4, 7.0, 1.702
SLOTS = 64
ROUNDS = T // SLOTS
VEXP = ROUNDS * N_EXP

OFF_V, OFF_R, OFF_A, OFF_U, OFF_SV, OFF_G = 512, 1024, 1536, 1552, 2064, 2576

PIECE = DC * HALF
PIECE_HALF = PIECE // 2
N_RAW_SLOTS = 4
N_PAIR_SLOTS = 3
W1_CHUNKS, W2_CHUNKS = DC, DC // 2
CHUNKS = W1_CHUNKS + W2_CHUNKS
CHUNK = 2 * D
N_CHUNK_SLOTS = 16
UNROLL = 4
GROUPS_OF_EXPERTS = N_EXP // UNROLL
assert UNROLL * CHUNKS % N_CHUNK_SLOTS == 0
LOADS_PER_SLOT = UNROLL * CHUNKS // N_CHUNK_SLOTS

PIECES = ["qk", "v", "r", "sv", "u", "ga0", "ga1", "gb0", "gb1", "pa", "pb", "xk0", "xk1",
          "mx0", "mx1", "xv0", "xv1", "xq0", "xq1", "xo0", "xo1"]
SPLIT = [name for name in PIECES if name not in ("pa", "pb")]
LAST_USE = {"qk": "k", "v": "v1", "r": "r1", "sv": "sv1", "u": "u1", "ga0": "ga10", "ga1": "ga11",
            "gb0": "gb10", "gb1": "gb11", "pa": "ya11", "pb": "yb11", "xk0": "kT1", "xk1": "kT3",
            "mx0": "x110", "mx1": "x111", "xv0": "vm10", "xv1": "vm11", "xq0": "xq1", "xq1": "xq3",
            "xo0": "x210", "xo1": "x211"}
TN = ["00", "01", "10", "11"]


def each(prefix):
    return [prefix + g for g in TN]


GROUPS = (["vecs"] + each("xT") + ["aL", "q", "k", "la", "v0", "v1", "r0", "r1", "sv0", "sv1", "wsT", "u0", "u1",
                                   "att0", "att1", "koT"] + each("memT")
          + ["ga00", "ga10", "kv0", "kv1", "kv2", "mix0", "mix1", "ga01", "ga11", "o0", "o1",
             "gb00", "gb10", "sboT0", "sboT1", "gb01", "gb11", "oT0", "oT1"]
          + each("ya") + each("yb") + ["kT0", "kT1"] + each("mT") + ["kT2", "kT3"]
          + ["x100", "x110", "x101", "x111", "hT00", "hT01", "vm00", "vm10", "hT10", "hT11", "vm01", "vm11"]
          + ["xq0", "xq1", "xq2", "xq3", "sc0", "sc1", "pT0", "pT1", "sc2", "sc3", "ao0", "ao1", "pT2", "pT3",
             "ao2", "ao3"]
          + ["x200", "x210", "x201", "x211", "hf00", "hf01", "lg0", "hf10", "hf11", "lg1", "pos", "gT"] + each("y"))
HIGH_BY_SCALAR = ["xT01", "xT11", "memT01", "memT11", "mT00", "mT01", "mT10", "mT11", "hT01", "hT11",
                  "ao0", "ao1", "ao2", "ao3"]
HIGH_BY_VECTOR = ["xT00", "xT10", "memT00", "memT10", "hT00", "hT10"]
INDEX = {g: n for n, g in enumerate(GROUPS)}
N_BANKS = 8


def bank_of(group):
    return INDEX[group] % N_BANKS


BASE = bank_of("gT")
PUT_BANK, Y_BANK, GATHER_BANK = BASE, (BASE + 1) % N_BANKS, (BASE + 5) % N_BANKS
HIDDEN_BANKS = [(BASE + 6) % N_BANKS, (BASE + 7) % N_BANKS]
SCATTER_BANKS = [(BASE + 2) % N_BANKS, (BASE + 3) % N_BANKS, (BASE + 4) % N_BANKS, Y_BANK]


def use_of(group):
    return INDEX[group] // N_BANKS + 1


def layer_program(nc, a, out):
    with ExitStack() as ctx:
        def sb(name, shape, dt=F32):
            return ctx.enter_context(nc.sbuf_tensor(name, shape, dt))

        def sem(name):
            return ctx.enter_context(nc.semaphore(name))

        ps = ctx.enter_context(nc.psum_tensor("ps", [P, N_BANKS, HALF], F32))

        raw = sb("raw", [P, N_RAW_SLOTS * PIECE_HALF])
        with ExitStack() as early:
            def early_sb(name, shape):
                return early.enter_context(nc.sbuf_tensor(name, shape, F32R))

            pairs = early_sb("pairs", [P, N_PAIR_SLOTS, 2, DC // 2, HALF])
            hT = early_sb("hT", [P, 2, DC, T])
            memT = early_sb("memT", [P, 2, DC, T])
        late = sb("late", [P, 2 * N_PAIR_SLOTS * PIECE_HALF + 4 * DC * T])
        wa_parts = ctx.enter_context(nc.sbuf_tensor("wa_parts", [P, 2, DC, RANK], F32R))
        rows = sb("rows", [P, TT, D])
        normed = sb("normed", [P, TT, D])
        side = sb("side", [P, TT, D])
        shared = sb("shared", [P, 13 * 1024])
        ident = sb("ident", [P, P])
        upper = sb("upper", [P, P])
        ones = sb("ones", [P, P])
        keep_att = sb("keep_att", [P, P])
        scan_keep = sb("scan_keep", [P, T])
        slot_iota = sb("slot_iota", [P, SLOTS])
        exp_iota = sb("exp_iota", [P, N_EXP])
        vec_rows = sb("vec_rows", [30, P])
        vecs = sb("vecs", [P, 30])
        wa = sb("wa", [P, DC, RANK])
        wr = sb("wr", [P, DC, N_EXP])
        wa2 = sb("wa2", [RANK, 2 * P])
        aT = sb("aT", [RANK, T])
        router_bias = sb("router_bias", [P, N_EXP])
        stat = sb("stat", [P, 192])
        G_MIX, G_X, G_MEM, B_A, B_SGU = 0, 8, 16, 24, 26
        N_X, N_MEM, N_X1, N_X2, N_OUT, EPS_COL = 128, 136, 144, 152, 160, 191
        eps = stat[:, EPS_COL:EPS_COL + 1]

        at = [0]

        def carve(cols, p=P):
            v = shared[0:p, at[0]:at[0] + cols]
            at[0] += cols
            assert at[0] <= 13 * 1024, at[0]
            return v

        def cut(v, *dims):
            if len(dims) == 2:
                return v.rearrange("p (a b) -> p a b", a=dims[0])
            return v.rearrange("p (a b c) -> p a b c", a=dims[0], b=dims[1])

        z = cut(carve(512), 2, T)
        lns = cut(carve(512), 2, T)
        cum = cut(carve(512), 2, T)
        ec = cut(carve(512), 2, T)
        q_in = cut(carve(512), 2, T)
        k_out = cut(carve(512), 2, T)
        kz = cut(carve(1024), GLA_H, T)
        values = cut(carve(1024), TT, WV)
        gate_r = cut(carve(1024), TT, WV)
        sgu_u = cut(carve(1024), TT, WV)
        sgu_v = cut(carve(1024), TT, WV)
        attz = carve(1024).rearrange("p (t h c) -> p t h c", t=TT, h=GLA_H)
        koz = carve(1024).rearrange("p (t m d) -> p t m d", t=TT, m=2)
        states = carve(3 * 512).rearrange("p (n f e) -> p n f e", n=3, f=2)
        w_sgu = cut(carve(512), SGU_G, P)
        w_sguT = cut(carve(512), SGU_G, P)
        g_out = carve(WV)
        g_sgu = sb("g_sgu", [P, WV])
        b_sgu = sb("b_sgu", [P, WV])
        o_rows = cut(shared[:, 0:1024], TT, WV)
        oT = cut(values.rearrange("p a b -> p (a b)"), 4, T)
        sboT = cut(kz.rearrange("p a b -> p (a b)"), 4, T)
        sq_o = cut(shared[:, 1024:2048], TT, WV)
        at[0] = 0
        kT = cut(carve(2048), DC, T)
        vm = cut(carve(2048), TT, D)
        probs = carve(4 * 512).rearrange("p (h t m) -> p h t m", h=XH, t=TT)
        probsT = carve(2 * 512).rearrange("p (b m t) -> p b m t", b=2, m=2)
        g_ffn = carve(D)
        at[0] = 13 * 1024 - 2 * D
        g_final = carve(D)
        b2 = carve(D, N_EXP)
        b1 = side[0:N_EXP].rearrange("p a b -> p (a b)")
        side_T = side.rearrange("p a b -> p (a b)").rearrange("p (c t) -> p c t", c=DC)
        at[0] = 2 * CHUNK
        table = cut(carve(TT * 160), TT, 160)
        gates = cut(carve(TT * VEXP), TT, VEXP)
        pick = carve(VEXP, N_EXP)
        eq = carve(TT * TOPK * N_EXP).rearrange("p (t k e) -> p t k e", t=TT, k=TOPK)
        lg = cut(carve(TT * N_EXP), TT, N_EXP)
        mask = cut(carve(TT * N_EXP), TT, N_EXP)
        gateT = carve(T, N_EXP)
        take = cut(carve(TT * SLOTS), TT, SLOTS)
        put = carve(TT * 2 * SLOTS).rearrange("p (t j s) -> p t j s", t=TT, j=2)
        putT = cut(carve(TT * P), TT, P)
        pick_e = carve(SLOTS, N_EXP)
        gathered = carve(HALF)
        xeT = cut(carve(HALF), 4, P)
        glu = carve(HALF)
        lin = carve(HALF)
        sig = carve(HALF)
        act = carve(HALF)
        actT = cut(carve(HALF), 4, P)
        y_rows = carve(HALF)
        assert at[0] <= 13 * 1024 - 2 * D
        trips = sb("trips", [1, 1], I32)
        top_i = sb("top_i", [P, TT, 8], U32)

        bank_filled = [sem(f"bank_filled{b}") for b in range(N_BANKS)]
        bank_emptied = [sem(f"bank_emptied{b}") for b in range(N_BANKS)]
        raw_full = [sem(f"raw_full{b}") for b in range(N_RAW_SLOTS)]
        chunk_full = [sem(f"chunk_full{b}") for b in range(N_CHUNK_SLOTS)]
        names = """high_made low_made first_half_used wa_high wa_split high_by_scalar high_by_vector x_in0 x_in1 mem_in small_in wa_in wa2_in wsgu_in gsgu_in wr_in gffn_in gfin_in b1_in b2_in out_sent
            ident_made consts_made zeros_made eps_made x1_ss x2_ss f_ss wsgu_masked
            x_sq x_std x_rstd x_normed mem_sq mem_std mem_rstd mem_normed
            z_abs z_exp z_ln logs_made cum_made cum_exp cum_neg_exp cum_diff rest_exp
            keys_made r_sig r_gate
            sv_stat sv_mv sv_std sv_rstd sv_g sv_normed
            o_sq o_ss o_std o_rstd o_made
            mixed x1_sq x1_std x1_rstd x1_normed
            s_max s_neg s_exp s_rec s_made
            x2_sq x2_std x2_rstd x2_normed
            top_made idx_made idxf_made top_neg gate_exp gate_rec gate_made eq_made mask_made geq_made gate_table
            pos_masked table_made cnt_cmp cnt_sum cnt_mul trips_made pick_made
            take_made put_made pick_e_made gather_filled gather_copied xeT_filled xeT_made h_filled glu_made
            sig_made lin_made lin_glu act_made putT_filled putT_made actT_filled actT_made y_filled y_copied
            scatter_filled y_added0 y_added1 y_added2 y_added3 chunk_used f_sq f_std f_rstd f_made""".split()
        s = {n: sem(n) for n in names}

        block = ctx.enter_context(nc.Block())

        def raw_half(n):
            k = n % N_RAW_SLOTS
            return raw[:, k * PIECE_HALF:(k + 1) * PIECE_HALF]

        def raw_arrived(eng, n):
            eng.wait_ge(raw_full[n % N_RAW_SLOTS], 16 * (n // N_RAW_SLOTS + 1))

        def pair(m):
            return pairs[:, m % N_PAIR_SLOTS]

        def loaded_as(m):
            return 2 * PIECES.index(SPLIT[m // 2]) + m % 2

        def split_used(eng, m):
            if m % 2 == 0:
                eng.wait_ge(s["first_half_used"], m // 2 + 1)
            else:
                filled(eng, LAST_USE[SPLIT[m // 2]])

        def late_slot(n):
            return late[:, n * CHUNK:(n + 1) * CHUNK]

        def last_split(slot):
            return max(m for m in range(2 * len(SPLIT)) if loaded_as(m) % N_RAW_SLOTS == slot)

        raw_order = sorted(range(N_RAW_SLOTS), key=last_split)
        pair_order = [(2 * len(SPLIT) - k) % N_PAIR_SLOTS for k in (3, 2, 1)]
        first_T = 2 * N_PAIR_SLOTS
        chunk_slots = ([late_slot(first_T + 2), late_slot(first_T + 3), shared[:, 0:CHUNK]]
                       + [raw_half(r) for r in raw_order] + [shared[:, CHUNK:2 * CHUNK]]
                       + [late_slot(2 * q + i) for q in pair_order for i in range(2)]
                       + [late_slot(first_T), late_slot(first_T + 1)])
        assert len(chunk_slots) == N_CHUNK_SLOTS and PIECE_HALF == CHUNK == DC * T

        def slot_of(c):
            return c % N_CHUNK_SLOTS

        def chunk(c):
            return chunk_slots[slot_of(c)]

        def bank(group):
            return ps[:, bank_of(group), :]

        def filled(eng, group):
            eng.wait_ge(bank_filled[bank_of(group)], use_of(group))

        def emptied(eng, group):
            eng.wait_ge(bank_emptied[bank_of(group)], use_of(group))

        w_in = a["w_in"]

        def piece_source(name):
            def cols(w, lo):
                return w.rearrange("(c p) n -> p c n", p=P)[:, :, lo:lo + HALF]
            lows = {"qk": 0, "v": OFF_V, "r": OFF_R, "u": OFF_U, "sv": OFF_SV, "ga0": OFF_G,
                    "ga1": OFF_G + HALF, "gb0": OFF_G + D, "gb1": OFF_G + D + HALF}
            if name in lows:
                return cols(w_in[0], lows[name]), DC
            if name in ("pa", "pb"):
                return a["w_proj_a" if name == "pa" else "w_proj_b"][0].rearrange("(c p) n -> p c n", p=P), DC // 2
            w = {"xk": "w_xk", "xv": "w_xv", "mx": "w_mix_out", "xq": "w_xq", "xo": "w_xo"}[name[:2]]
            return cols(a[w][0], HALF * int(name[2])), DC

        @block.sync
        def _(sp):
            def load_half(n):
                name = PIECES[n // 2]
                if n >= N_RAW_SLOTS:
                    old = PIECES[(n - N_RAW_SLOTS) // 2]
                    if old in SPLIT:
                        sp.wait_ge(s["low_made"], 2 * SPLIT.index(old) + n % 2 + 1)
                    else:
                        filled(sp, LAST_USE[old])
                src, c = piece_source(name)
                src = src[:, (n % 2) * (c // 2):(n % 2 + 1) * (c // 2), :]
                sp.dma_start(raw_half(n).rearrange("p (c n) -> p c n", c=c // 2), src).then_inc(
                    raw_full[n % N_RAW_SLOTS], 16)

            def load_chunk(c, e):
                k = c % CHUNKS
                if k < W1_CHUNKS:
                    src, dst = a["w_e1"][0, e, k * P:(k + 1) * P, :], chunk(c)
                else:
                    k -= W1_CHUNKS
                    src = a["w_e2"][0, e, 2 * k * P:2 * (k + 1) * P, :].rearrange("(i p) n -> p i n", i=2)
                    dst = chunk(c).rearrange("p (i n) -> p i n", i=2)
                sp.dma_start(dst, src).then_inc(chunk_full[slot_of(c)], 16)

            def chunk_was_used(v, c):
                if c < CHUNKS - 1:
                    sp.wait_ge(s["chunk_used"], v * (CHUNKS - 1) + (c + 1))
                else:
                    sp.wait_ge(s["y_filled"], v + 1)

            x_rows = a["x"][0].rearrange("(t p) d -> p t d", p=P)
            sp.dma_start(rows[:, 0, :], x_rows[:, 0, :]).then_inc(s["x_in0"], 16)
            sp.dma_start(rows[:, 1, :], x_rows[:, 1, :]).then_inc(s["x_in1"], 16)
            sp.dma_start(wa[:], w_in[0].rearrange("(c p) n -> p c n", p=P)[:, :, OFF_A:OFF_A + RANK]).then_inc(
                s["wa_in"], 16)
            load_half(0)
            load_half(1)
            sp.dma_start(wa2[:], a["gla_w_a2"][0]).then_inc(s["wa2_in"], 16)
            load_half(2)
            load_half(3)
            sp.dma_start(side[:], a["mem"][0].rearrange("(t p) d -> p t d", p=P)).then_inc(s["mem_in"], 16)
            sp.dma_start(g_out, a["gla_out_g"][0:1, :].to_broadcast([P, WV])).then_inc(s["gsgu_in"], 16)
            sp.dma_start(g_sgu[:], a["sgu_norm_g"][0:1, :].to_broadcast([P, WV])).then_inc(s["gsgu_in"], 16)
            sp.dma_start(b_sgu[:], a["sgu_norm_b"][0:1, :].to_broadcast([P, WV])).then_inc(s["gsgu_in"], 16)
            sp.dma_start(w_sgu, a["sgu_w"][0].rearrange("g t s -> t g s")).then_inc(s["wsgu_in"], 16)
            sp.dma_start(wr[:], a["w_router"][0].rearrange("(c p) n -> p c n", p=P)).then_inc(s["wr_in"], 16)
            sp.dma_start(router_bias[:], a["b_router"][0:1, :].to_broadcast([P, N_EXP])).then_inc(s["wr_in"], 16)
            for n in range(N_RAW_SLOTS, 2 * len(PIECES)):
                load_half(n)
                if n == 2 * PIECES.index("xv1"):
                    filled(sp, "kT0")
                    sp.dma_start(g_ffn, a["norm_ffn_g"][0:1, :].to_broadcast([P, D])).then_inc(s["gffn_in"], 16)
                    sp.dma_start(g_final, a["norm_final_g"].rearrange("(a d) -> a d", a=1).to_broadcast(
                        [P, D])).then_inc(s["gfin_in"], 16)
                    sp.dma_start(b2, a["b_e2"][0]).then_inc(s["b2_in"], 16)

            def tenant_dead(m):
                if m == 0:
                    filled(sp, "vm11")
                elif m == 2:
                    filled(sp, "sc3")
                elif 3 <= m < 7:
                    sp.wait_ge(s["low_made"], last_split(raw_order[m - 3]) + 1)
                elif m == 7:
                    filled(sp, "ao3")
                elif m == 8:
                    filled(sp, "x210")
                elif m == 10:
                    filled(sp, "x211")

            for m in range(UNROLL * CHUNKS):
                if m < N_CHUNK_SLOTS:
                    tenant_dead(m)
                else:
                    chunk_was_used((m - N_CHUNK_SLOTS) // CHUNKS, (m - N_CHUNK_SLOTS) % CHUNKS)
                load_chunk(m, m // CHUNKS)
                if m == N_CHUNK_SLOTS - 1:
                    filled(sp, "lg1")
                    sp.dma_start(b1, a["b_e1"][0]).then_inc(s["b1_in"], 16)
            sp.wait_ge(s["trips_made"], 1)
            n = sp.value_load(trips[0:1, 0:1], min_val=GROUPS_OF_EXPERTS, max_val=ROUNDS * GROUPS_OF_EXPERTS)
            with sp.Fori(1, n) as i:
                e0 = sp.snap((i % GROUPS_OF_EXPERTS) * UNROLL)
                for m in range(UNROLL * CHUNKS):
                    before = m - N_CHUNK_SLOTS + UNROLL * CHUNKS
                    chunk_was_used((i - 1) * UNROLL + before // CHUNKS, before % CHUNKS)
                    load_chunk(m, e0 + m // CHUNKS)
            out_rows = out[0].rearrange("(t p) d -> p t d", p=P)
            for k in range(4):
                c = slice(k % 2 * HALF, (k % 2 + 1) * HALF)
                sp.wait_ge(s["f_made"], k + 1)
                sp.dma_start(out_rows[:, k // 2, c], rows[:, k // 2, c]).then_inc(s["out_sent"], 16)
            sp.wait_ge(s["out_sent"], 64)

        @block.gpsimd
        def _(pool):
            g = nc.gpsimd
            g.memset(ident[:], 0.0).then_inc(s["ident_made"], 1)
            pool.wait_ge(s["ident_made"], 1)
            g.affine_select(out=ident[:], in_=ident[:], compare_op=ALU.not_equal, fill=1.0, base=0,
                            pattern=[[-1, P]], channel_multiplier=1).then_inc(s["ident_made"], 1)
            g.memset(eps, EPS).then_inc(s["eps_made"], 1)

            def low_part(m):
                pool.wait_ge(s["high_made"], m + 1)
                high, low = (pair(m)[:, i].rearrange("p c n -> p (c n)") for i in range(2))
                g.tensor_tensor(low, raw_half(loaded_as(m)), high, ALU.subtract).then_inc(s["low_made"], 1)

            g.memset(kz, 0.0)
            g.memset(attz, 0.0)
            g.memset(koz, 0.0)
            g.memset(states, 0.0).then_inc(s["zeros_made"], 1)
            g.memset(ones[:], 1.0)
            g.memset(scan_keep[:], 1.0).then_inc(s["consts_made"], 1)
            pool.wait_ge(s["consts_made"], 1)
            g.memset(scan_keep[:].rearrange("p (n c) -> p n c", c=GLA_C)[:, :, 0:1], 0.0)
            g.affine_select(out=upper[:], in_=ones[:], compare_op=ALU.is_ge, fill=0.0, base=-1,
                            pattern=[[1, P]], channel_multiplier=-1)
            g.affine_select(out=keep_att[:], in_=ones[:], compare_op=ALU.is_ge, fill=0.0, base=0,
                            pattern=[[1, P]], channel_multiplier=-1)
            g.iota(slot_iota[:], pattern=[[1, SLOTS]], base=0, channel_multiplier=0,
                   allow_small_or_imprecise_dtypes=True)
            g.iota(exp_iota[:], pattern=[[1, N_EXP]], base=0, channel_multiplier=0,
                   allow_small_or_imprecise_dtypes=True).then_inc(s["consts_made"], 1)
            pool.wait_ge(s["consts_made"], 2)
            g.memset(keep_att[0:64, 64:128], 0.0).then_inc(s["consts_made"], 1)
            pool.wait_ge(s["wa_in"], 16)
            g.tensor_copy(wa_parts[:, 0], wa[:]).then_inc(s["wa_high"], 1)
            pool.wait_ge(s["wa_high"], 1)
            g.tensor_tensor(wa_parts[:, 1], wa[:], wa_parts[:, 0], ALU.subtract).then_inc(s["wa_split"], 1)
            low_part(0)
            low_part(1)
            pool.wait_ge(s["wsgu_in"], 16)
            g.affine_select(out=w_sgu, in_=w_sgu, compare_op=ALU.is_ge, fill=0.0, base=0,
                            pattern=[[0, SGU_G], [-1, P]], channel_multiplier=1).then_inc(s["wsgu_masked"], 1)
            for m in range(2, 2 * len(SPLIT)):
                low_part(m)

        @block.scalar
        def _(sc):
            A = nc.scalar
            small = [("norm_mix_g", G_MIX, 8), ("norm_x_g", G_X, 8), ("norm_mem_g", G_MEM, 8), ("gla_b_a", B_A, 2)]
            for name, r, n in small:
                sc.dma_start(vec_rows[r:r + n, :], a[name][0].rearrange("(c p) -> c p", p=P)).then_inc(s["small_in"], 16)
            sc.dma_start(vec_rows[B_SGU:B_SGU + 4, :], a["sgu_b"][0]).then_inc(s["small_in"], 16)

            A.preload_act_table(ACT.Sqrt)

            def squares(src, scratch, col, done):
                for t in range(TT):
                    A.activation(scratch[:, t, :], src[:, t, :], ACT.Square,
                                 accum_out=stat[:, col + t:col + t + 1]).then_inc(s[done], 1)

            def root(dst, src, width, ready, need, done):
                sc.wait_ge(s[ready], need)
                A.activation(dst, src, ACT.Sqrt, scale=1.0 / width, bias=eps).then_inc(s[done], 1)

            def half_squares(name, col, t, n, scratch):
                c = slice(n * HALF, (n + 1) * HALF)
                A.activation(scratch[:, t, c], rows[:, t, c], ACT.Square,
                             accum_out=stat[:, col + 2 * t + n:col + 2 * t + n + 1]).then_inc(s[name + "_sq"], 1)

            def copy_out(group, dst):
                filled(sc, group)
                A.activation(dst, bank(group)[0:dst.shape[0], :].rearrange("p (a b) -> p a b", a=dst.shape[1])
                             if len(dst.shape) == 3 else bank(group), ACT.Copy).then_inc(
                    bank_emptied[bank_of(group)], 1)

            split = [0]

            def high_parts(name, half):
                stop = 2 * SPLIT.index(name) + half + 1
                for m in range(split[0], stop):
                    high_part(m)
                split[0] = max(split[0], stop)

            def high_part(m):
                if m >= N_PAIR_SLOTS:
                    split_used(sc, m - N_PAIR_SLOTS)
                raw_arrived(sc, loaded_as(m))
                A.activation(pair(m)[:, 0].rearrange("p c n -> p (c n)"), raw_half(loaded_as(m)), ACT.Copy).then_inc(
                    s["high_made"], 1)

            def plain_T(prefix, t, k, dst):
                copy_out(f"{prefix}{t}{k}", dst[:, 4 * k:4 * k + 4, t * P:(t + 1) * P])

            def high_of(group, dst):
                filled(sc, group)
                A.activation(dst, bank(group).rearrange("p (a b) -> p a b", a=dst.shape[1]), ACT.Copy).then_inc(
                    s["high_by_scalar"], 1)

            def high_scaled(prefix, t, k, dst, gain):
                group = f"{prefix}{t}{k}"
                filled(sc, group)
                for i in range(4):
                    c = 4 * k + i
                    last = A.activation(dst[:, 0, c, t * P:(t + 1) * P], bank(group)[:, i * P:(i + 1) * P], ACT.Copy,
                                        scale=vecs[:, gain + c:gain + c + 1])
                last.then_inc(s["high_by_scalar"], 1)

            sc.wait_ge(s["x_in0"], 16)
            A.activation(normed[:, 0, :], rows[:, 0, :], ACT.Square, accum_out=stat[:, N_X + 4:N_X + 5]).then_inc(
                s["x_sq"], 1)
            sc.wait_ge(s["eps_made"], 1)
            root(stat[:, N_X + 4:N_X + 6], stat[:, N_X + 4:N_X + 6], D, "x_sq", 2, "x_std")
            high_parts("qk", 0)
            emptied(sc, "vecs")
            high_scaled("xT", 0, 1, hT, G_MIX)
            high_scaled("xT", 1, 1, hT, G_MIX)
            high_parts("v", 0)
            sc.wait_ge(s["mem_in"], 16)
            squares(side, memT[:, 0].rearrange("p c t -> p (c t)").rearrange("p (a b) -> p a b", a=TT), N_MEM + 4, "mem_sq")
            root(stat[:, N_MEM + 4:N_MEM + 6], stat[:, N_MEM + 4:N_MEM + 6], D, "mem_sq", 2, "mem_std")
            A.preload_act_table_set("natural_log_exp_and_others")
            high_parts("v", 1)
            emptied(sc, "la")
            A.activation(lns, z, ACT.Abs).then_inc(s["z_abs"], 1)
            sc.wait_ge(s["z_abs"], 1)
            A.activation(lns, lns, ACT.Exp, scale=-1.0).then_inc(s["z_exp"], 1)
            sc.wait_ge(s["z_exp"], 1)
            A.activation(lns, lns, ACT.Ln, bias=1.0).then_inc(s["z_ln"], 1)
            high_parts("r", 1)
            sc.wait_ge(s["cum_made"], 2)
            A.activation(ec, cum, ACT.Exp, scale=1.0 / TAU).then_inc(s["cum_exp"], 1)
            A.activation(z, cum, ACT.Exp, scale=-1.0 / TAU).then_inc(s["cum_neg_exp"], 1)
            sc.wait_ge(s["cum_diff"], 1)
            A.activation(lns, lns, ACT.Exp, scale=1.0 / TAU).then_inc(s["rest_exp"], 1)
            copy_out("v0", values[:, 0, :])
            copy_out("v1", values[:, 1, :])
            high_parts("sv", 1)
            for t in range(TT):
                filled(sc, f"r{t}")
                A.activation(gate_r[:, t, :], bank(f"r{t}"), ACT.Sigmoid).then_inc(s["r_sig"], 1)
            for n, dst, following in (("sv", sgu_v, "u"), ("u", sgu_u, "ga0")):
                high_parts(following, 1)
                for t in range(TT):
                    filled(sc, f"{n}{t}")
                    A.activation(dst[:, t, :], bank(f"{n}{t}"), ACT.Gelu).then_inc(bank_emptied[bank_of(f"{n}{t}")], 1)
            high_parts("ga1", 0)
            high_scaled("memT", 0, 1, memT, G_MEM)
            high_scaled("memT", 1, 1, memT, G_MEM)
            sc.wait_ge(s["sv_mv"], 2)
            A.activation(stat[:, 4:6], stat[:, 112:116].rearrange("p (t k) -> p t k", t=TT)[:, :, 1], ACT.Sqrt,
                         bias=eps).then_inc(s["sv_std"], 1)

            def gates_of(name, n, dst):
                for t in range(TT):
                    group = f"{name}{t}{n}"
                    filled(sc, group)
                    A.activation(dst[:, t, n * HALF:(n + 1) * HALF], bank(group), ACT.Sigmoid).then_inc(
                        bank_emptied[bank_of(group)], 1)

            high_parts("ga1", 1)
            gates_of("ga", 0, normed)
            high_parts("gb0", 1)
            gates_of("ga", 1, normed)
            high_parts("gb1", 0)
            for t in range(TT):
                filled(sc, f"o{t}")
                A.activation(sq_o[:, t, :], bank(f"o{t}"), ACT.Square).then_inc(s["o_sq"], 1)
            root(stat[:, 16:24], stat[:, 16:24], GLA_DV, "o_ss", 2, "o_std")
            high_parts("gb1", 1)
            gates_of("gb", 0, side)
            copy_out("sboT0", sboT[:, 0:2, :])
            copy_out("sboT1", sboT[:, 2:4, :])
            gates_of("gb", 1, side)
            copy_out("oT0", oT[:, 0:2, :])
            copy_out("oT1", oT[:, 2:4, :])
            high_parts("xk1", 1)
            for k in range(2):
                copy_out(f"kT{k}", kT[:, 2 * k:2 * k + 2, :])
            high_parts("mx0", 0)
            for g in TN:
                t, k = int(g[0]), int(g[1])
                high_of("mT" + g, hT[:, 0, 4 * k:4 * k + 4, t * P:(t + 1) * P])
            high_parts("mx0", 1)
            for k in range(2, 4):
                copy_out(f"kT{k}", kT[:, 2 * k:2 * k + 2, :])
            high_parts("mx1", 1)

            def norm_half(name, col, t, n, scratch=normed):
                emptied(sc, f"{name}{t}{n}")
                half_squares(name, col, t, n, scratch)
                if n == 1:
                    root(stat[:, col + 4 + t:col + 5 + t], stat[:, col + 4 + t:col + 5 + t], D, name + "_ss", t + 1,
                         name + "_std")

            norm_half("x1", N_X1, 0, 0)
            norm_half("x1", N_X1, 1, 0)
            high_parts("xv0", 0)
            norm_half("x1", N_X1, 0, 1)
            high_parts("xv0", 1)
            norm_half("x1", N_X1, 1, 1)
            high_parts("xv1", 0)

            def value_rows(t, n):
                copy_out(f"vm{t}{n}", vm[:, t, n * HALF:(n + 1) * HALF])

            high_scaled("hT", 0, 1, hT, G_X)
            high_parts("xv1", 1)
            value_rows(0, 0)
            value_rows(1, 0)
            high_scaled("hT", 1, 1, hT, G_X)
            high_parts("xq0", 1)
            value_rows(0, 1)
            value_rows(1, 1)
            high_parts("xq1", 1)
            copy_out("xq0", side_T[:, 0:2, :])
            copy_out("xq1", side_T[:, 2:4, :])
            high_parts("xo0", 0)

            def soft(h):
                sc.wait_ge(s["s_neg"], h + 1)
                for t in range(TT):
                    A.activation(probs[:, h, t, :], bank(f"sc{h}")[:, t * T:(t + 1) * T], ACT.Exp, scale=XDH ** -0.5,
                                 bias=stat[:, 40 + 2 * h + t:41 + 2 * h + t],
                                 accum_out=stat[:, 48 + 2 * h + t:49 + 2 * h + t]).then_inc(s["s_exp"], 1)

            soft(0)
            soft(1)
            high_parts("xo0", 1)
            copy_out("xq2", side_T[:, 4:6, :])
            copy_out("xq3", side_T[:, 6:8, :])
            high_parts("xo1", 0)
            soft(2)
            soft(3)
            for h in range(XH):
                high_of(f"ao{h}", hT[:, 0, 2 * h:2 * h + 2, :])
            high_parts("xo1", 1)
            norm_half("x2", N_X2, 0, 0)
            norm_half("x2", N_X2, 1, 0)
            norm_half("x2", N_X2, 0, 1)
            norm_half("x2", N_X2, 1, 1)
            plain_T("hf", 0, 1, side_T)
            plain_T("hf", 1, 1, side_T)
            for t in range(TT):
                sc.wait_ge(s["top_neg"], t + 1)
                A.activation(stat[:, 80 + 4 * t:84 + 4 * t], stat[:, 64 + 8 * t:68 + 8 * t], ACT.Exp,
                             bias=stat[:, 60 + t:61 + t], accum_out=stat[:, 88 + t:89 + t]).then_inc(s["gate_exp"], 1)

            def copy_gathered(need):
                sc.wait_ge(s["gather_filled"], need)
                A.activation(gathered, ps[:, GATHER_BANK, :], ACT.Copy).then_inc(s["gather_copied"], 1)

            def copy_gathered_T(need):
                sc.wait_ge(s["xeT_filled"], need)
                A.activation(xeT, ps[:, GATHER_BANK, :].rearrange("p (a b) -> p a b", a=4), ACT.Copy).then_inc(
                    s["xeT_made"], 1)

            A.preload_act_table(ACT.Sigmoid)
            copy_gathered(1)
            copy_gathered_T(1)
            sc.wait_ge(s["trips_made"], 1)
            n = sc.value_load(trips[0:1, 0:1], min_val=GROUPS_OF_EXPERTS, max_val=ROUNDS * GROUPS_OF_EXPERTS)

            def expert(v):
                sc.wait_ge(s["putT_filled"], v + 1)
                A.activation(putT, ps[:, PUT_BANK, 0:TT * P].rearrange("p (a b) -> p a b", a=TT), ACT.Copy).then_inc(
                    s["putT_made"], 1)
                sc.wait_ge(s["glu_made"], v + 1)
                A.activation(sig, glu, ACT.Sigmoid, scale=ALPHA).then_inc(s["sig_made"], 1)
                copy_gathered(v + 2)
                copy_gathered_T(v + 2)
                sc.wait_ge(s["actT_filled"], v + 1)
                A.activation(actT, ps[:, PUT_BANK, :].rearrange("p (a b) -> p a b", a=4), ACT.Copy).then_inc(
                    s["actT_made"], 1)
                sc.wait_ge(s["y_filled"], v + 1)
                A.activation(y_rows, ps[:, Y_BANK, :], ACT.Copy).then_inc(s["y_copied"], 1)

            with sc.Fori(0, n) as i:
                A.preload_act_table(ACT.Sigmoid)
                for k in range(UNROLL):
                    expert(i * UNROLL + k)
            A.preload_act_table(ACT.Sqrt)
            for k in range(4):
                sc.wait_ge(s[f"y_added{k}"], n * UNROLL)
                half_squares("f", N_OUT, k // 2, k % 2, normed)
                if k % 2:
                    col = N_OUT + 4 + k // 2
                    root(stat[:, col:col + 1], stat[:, col:col + 1], D, "f_ss", k // 2 + 1, "f_std")

        @block.vector
        def _(ve):
            V = nc.vector

            def inv(col, n, std, done, need=1):
                ve.wait_ge(s[std], need)
                V.reciprocal(stat[:, col:col + n], stat[:, col:col + n]).then_inc(s[done], 1)

            def norm_tile(name, col, t, dst, done, squared, gain=None):
                ve.wait_ge(s[name + "_sq"], squared)
                ss = stat[:, col + 4 + t:col + 5 + t]
                V.tensor_tensor(ss, stat[:, col + 2 * t:col + 2 * t + 1], stat[:, col + 2 * t + 1:col + 2 * t + 2],
                                ALU.add).then_inc(s[name + "_ss"], 1)
                inv(col + 4 + t, 1, name + "_std", name + "_rstd", t + 1)
                ve.wait_ge(s[name + "_rstd"], t + 1)
                for n in range(2):
                    c = slice(n * HALF, (n + 1) * HALF)
                    if gain is None:
                        ins = V.tensor_scalar(dst[:, t, c], rows[:, t, c], ss, None, ALU.mult)
                    else:
                        ins = V.scalar_tensor_tensor(dst[:, t, c], rows[:, t, c], ss, gain[:, c], ALU.mult, ALU.mult)
                    ins.then_inc(s[done], 1)

            def scale_rows(dst, src, col, rstd, done):
                ve.wait_ge(s[rstd], 1)
                for t in range(TT):
                    for n in range(2):
                        c = slice(n * HALF, (n + 1) * HALF)
                        V.tensor_scalar(dst[:, t, c], src[:, t, c], stat[:, col + t:col + t + 1], None,
                                        ALU.mult).then_inc(s[done], 1)

            def copy_out(group, dst):
                filled(ve, group)
                V.tensor_copy(dst, bank(group).rearrange("p (a b) -> p a b", a=dst.shape[1])
                              if len(dst.shape) == 3 else bank(group)).then_inc(bank_emptied[bank_of(group)], 1)

            def plain_T(prefix, t, k, dst):
                copy_out(f"{prefix}{t}{k}", dst[:, 4 * k:4 * k + 4, t * P:(t + 1) * P])

            def low_of(group, dst, high):
                ve.wait_ge(s["high_by_scalar"], HIGH_BY_SCALAR.index(group) + 1)
                V.tensor_tensor(dst, bank(group).rearrange("p (a b) -> p a b", a=dst.shape[1]), high,
                                ALU.subtract).then_inc(bank_emptied[bank_of(group)], 1)

            def scaled_T(prefix, t, k, dst, gain):
                group = f"{prefix}{t}{k}"
                r = slice(t * P, (t + 1) * P)
                if group in HIGH_BY_VECTOR:
                    filled(ve, group)
                    V.tensor_tensor(dst[:, 0, 4 * k:4 * k + 4, r], bank(group).rearrange("p (c r) -> p c r", c=4),
                                    vecs[:, gain + 4 * k:gain + 4 * k + 4].unsqueeze(2).to_broadcast([P, 4, P]),
                                    ALU.mult).then_inc(s["high_by_vector"], 1)
                    ve.wait_ge(s["high_by_vector"], HIGH_BY_VECTOR.index(group) + 1)
                else:
                    ve.wait_ge(s["high_by_scalar"], HIGH_BY_SCALAR.index(group) + 1)
                for i in range(4):
                    c = 4 * k + i
                    last = V.scalar_tensor_tensor(dst[:, 1, c, r], bank(group)[:, i * P:(i + 1) * P],
                                                  vecs[:, gain + c:gain + c + 1], dst[:, 0, c, r],
                                                  ALU.mult, ALU.subtract)
                last.then_inc(bank_emptied[bank_of(group)], 1)

            ve.wait_ge(s["x_in1"], 16)
            V.tensor_tensor_reduce(normed[:, 1, :], rows[:, 1, :], rows[:, 1, :], 1.0, 0.0, ALU.mult, ALU.add,
                                   stat[:, N_X + 5:N_X + 6]).then_inc(s["x_sq"], 1)
            filled(ve, "vecs")
            V.tensor_copy(vecs[:], bank("vecs")[:, 0:30]).then_inc(bank_emptied[bank_of("vecs")], 1)
            inv(N_X + 4, 2, "x_std", "x_rstd")
            scale_rows(normed, rows, N_X + 4, "x_rstd", "x_normed")
            emptied(ve, "vecs")
            for g in TN:
                scaled_T("xT", int(g[0]), int(g[1]), hT, G_MIX)
            filled(ve, "aL")
            V.tensor_copy(aT[:], bank("aL")[0:RANK, 0:T]).then_inc(bank_emptied[bank_of("aL")], 1)
            filled(ve, "la")
            V.tensor_scalar(z[:, 0, :], bank("la")[:, 0:T], vecs[:, B_A:B_A + 1], None, ALU.add)
            V.tensor_scalar(z[:, 1, :], bank("la")[:, T:2 * T], vecs[:, B_A + 1:B_A + 2], None,
                            ALU.add).then_inc(bank_emptied[bank_of("la")], 1)
            inv(N_MEM + 4, 2, "mem_std", "mem_rstd")
            scale_rows(side, side, N_MEM + 4, "mem_rstd", "mem_normed")
            ve.wait_ge(s["z_ln"], 1)
            logs = q_in
            V.scalar_tensor_tensor(logs, z, 0.0, lns, ALU.min, ALU.subtract).then_inc(s["logs_made"], 1)
            ve.wait_ge(s["logs_made"], 1)
            ve.wait_ge(s["consts_made"], 3)
            for f in range(2):
                V.tensor_tensor_scan(cum[:, f, :], scan_keep[:], logs[:, f, :], 0.0, ALU.mult, ALU.add).then_inc(
                    s["cum_made"], 1)
            ve.wait_ge(s["cum_made"], 2)
            cum4 = cum.rearrange("p f (n c) -> p (f n) c", c=GLA_C)
            V.tensor_tensor(lns.rearrange("p f (n c) -> p (f n) c", c=GLA_C),
                            cum4[:, :, GLA_C - 1:GLA_C].to_broadcast([P, 2 * NCH, GLA_C]), cum4,
                            ALU.subtract).then_inc(s["cum_diff"], 1)
            filled(ve, "q")
            ve.wait_ge(s["cum_exp"], 1)
            V.scalar_tensor_tensor(q_in, bank("q").rearrange("p (a b) -> p a b", a=2), GLA_DK ** -0.5, ec,
                                   ALU.mult, ALU.mult).then_inc(bank_emptied[bank_of("q")], 1)
            filled(ve, "k")
            ve.wait_ge(s["cum_neg_exp"], 1)
            ve.wait_ge(s["zeros_made"], 1)
            for h in range(GLA_H):
                p0, f = 64 * (h % 2), h // 2
                V.tensor_tensor(kz[p0:p0 + 64, h, :], bank("k")[p0:p0 + 64, f * T:(f + 1) * T], z[p0:p0 + 64, f, :],
                                ALU.mult).then_inc(s["keys_made"], 1)
            ve.wait_ge(s["rest_exp"], 1)
            V.tensor_tensor(k_out, bank("k").rearrange("p (a b) -> p a b", a=2), lns, ALU.mult).then_inc(
                bank_emptied[bank_of("k")], 1)
            ve.wait_ge(s["gsgu_in"], 48)
            for t in range(TT):
                ve.wait_ge(s["r_sig"], t + 1)
                V.tensor_tensor(gate_r[:, t, :], bank(f"r{t}"), gate_r[:, t, :], ALU.mult).then_inc(
                    bank_emptied[bank_of(f"r{t}")], 1)
                emptied(ve, f"r{t}")
                V.tensor_tensor(gate_r[:, t, :], gate_r[:, t, :], g_out, ALU.mult).then_inc(s["r_gate"], 1)
            copy_out("wsT", w_sguT)
            for t in range(TT):
                emptied(ve, f"sv{t}")
                V.bn_stats(stat[:, 96 + 6 * t:102 + 6 * t], sgu_v[:, t, :]).then_inc(s["sv_stat"], 1)
            for t in range(TT):
                ve.wait_ge(s["sv_stat"], t + 1)
                V.bn_aggr(stat[:, 112 + 2 * t:114 + 2 * t], stat[:, 96 + 6 * t:102 + 6 * t]).then_inc(s["sv_mv"], 1)
            for t in range(TT):
                filled(ve, f"att{t}")
                V.copy_predicated(attz[:, t], keep_att[:].bitcast(U32).unsqueeze(1).to_broadcast([P, GLA_H, P]),
                                  bank(f"att{t}").rearrange("p (h c) -> p h c", h=GLA_H)).then_inc(
                    bank_emptied[bank_of(f"att{t}")], 1)
            filled(ve, "koT")
            for m in range(2):
                last = V.tensor_copy(koz[64 * m:64 * m + 64, :, m, :],
                                     bank("koT")[64 * m:64 * m + 64, :].rearrange("p (t d) -> p t d", t=TT))
            last.then_inc(bank_emptied[bank_of("koT")], 1)
            for g in TN:
                scaled_T("memT", int(g[0]), int(g[1]), memT, G_MEM)
            inv(4, 2, "sv_std", "sv_rstd")
            ve.wait_ge(s["sv_rstd"], 1)
            for t in range(TT):
                V.tensor_scalar(sgu_v[:, t, :], sgu_v[:, t, :], stat[:, 112 + 2 * t:113 + 2 * t],
                                stat[:, 4 + t:5 + t], ALU.subtract, ALU.mult).then_inc(s["sv_g"], 1)
            for t in range(TT):
                ve.wait_ge(s["sv_g"], t + 1)
                V.tensor_tensor(sgu_v[:, t, :], sgu_v[:, t, :], g_sgu[:], ALU.mult).then_inc(s["sv_g"], 1)
            for t in range(TT):
                ve.wait_ge(s["sv_g"], t + 3)
                V.tensor_tensor(sgu_v[:, t, :], sgu_v[:, t, :], b_sgu[:], ALU.add).then_inc(s["sv_normed"], 1)
            for n in range(3):
                filled(ve, f"kv{n}")
                if n:
                    emptied(ve, f"kv{n - 1}")
                for f in range(2):
                    for hh in range(2):
                        q, e = slice(64 * hh, 64 * hh + 64), slice(P * hh, P * hh + P)
                        src = bank(f"kv{n}")[q, f * T + P * hh:f * T + P * hh + P]
                        if n == 0:
                            last = V.tensor_copy(states[q, n, f, e], src)
                        else:
                            last_token = GLA_C * n + GLA_C - 1
                            last = V.scalar_tensor_tensor(states[q, n, f, e], states[q, n - 1, f, e],
                                                         ec[q, f, last_token:last_token + 1], src, ALU.mult, ALU.add)
                last.then_inc(bank_emptied[bank_of(f"kv{n}")], 1)
            for t in range(TT):
                filled(ve, f"mix{t}")
                emptied(ve, f"u{t}")
                for g in range(SGU_G):
                    c = slice(g * P, (g + 1) * P)
                    last = V.scalar_tensor_tensor(sgu_u[:, t, c], bank(f"mix{t}")[:, c], vecs[:, B_SGU + g:B_SGU + g + 1],
                                                  sgu_u[:, t, c], ALU.add, ALU.mult)
                last.then_inc(bank_emptied[bank_of(f"mix{t}")], 1)
            for t in range(TT):
                ve.wait_ge(s["o_sq"], t + 1)
                V.tensor_reduce(stat[:, 16 + 4 * t:20 + 4 * t], sq_o[:, t, :].rearrange("p (h e) -> p h e", h=GLA_H),
                                AX, ALU.add).then_inc(s["o_ss"], 1)
            inv(16, 8, "o_std", "o_rstd")
            ve.wait_ge(s["o_rstd"], 1)
            for t in range(TT):
                V.tensor_tensor(o_rows[:, t, :].rearrange("p (h e) -> p h e", h=GLA_H),
                                bank(f"o{t}").rearrange("p (h e) -> p h e", h=GLA_H),
                                stat[:, 16 + 4 * t:20 + 4 * t].unsqueeze(2).to_broadcast([P, GLA_H, GLA_DV]),
                                ALU.mult).then_inc(bank_emptied[bank_of(f"o{t}")], 1)
            ve.wait_ge(s["r_gate"], 2)
            for t in range(TT):
                emptied(ve, f"o{t}")
                V.tensor_tensor(o_rows[:, t, :], o_rows[:, t, :], gate_r[:, t, :], ALU.mult).then_inc(s["o_made"], 1)
            for g in TN:
                t, n = int(g[0]), int(g[1])
                c = slice(n * HALF, (n + 1) * HALF)
                filled(ve, "ya" + g)
                emptied(ve, "ga" + g)
                V.tensor_tensor(normed[:, t, c], bank("ya" + g), normed[:, t, c], ALU.mult).then_inc(
                    bank_emptied[bank_of("ya" + g)], 1)
            for g in TN:
                t, n = int(g[0]), int(g[1])
                c = slice(n * HALF, (n + 1) * HALF)
                filled(ve, "yb" + g)
                emptied(ve, "gb" + g)
                V.tensor_tensor(side[:, t, c], bank("yb" + g), side[:, t, c], ALU.mult).then_inc(
                    bank_emptied[bank_of("yb" + g)], 1)
                emptied(ve, "yb" + g)
                emptied(ve, "ya" + g)
                V.tensor_tensor(normed[:, t, c], normed[:, t, c], side[:, t, c], ALU.add).then_inc(s["mixed"], 1)
            for g in TN:
                t, k = int(g[0]), int(g[1])
                dst = hT[:, :, 4 * k:4 * k + 4, t * P:(t + 1) * P]
                low_of("mT" + g, dst[:, 1], dst[:, 0])

            def add_rows(name, t, n):
                group, c = f"{name}{t}{n}", slice(n * HALF, (n + 1) * HALF)
                filled(ve, group)
                V.tensor_tensor(rows[:, t, c], bank(group), rows[:, t, c], ALU.add).then_inc(
                    bank_emptied[bank_of(group)], 1)

            add_rows("x1", 0, 0)
            add_rows("x1", 1, 0)
            add_rows("x1", 0, 1)
            norm_tile("x1", N_X1, 0, normed, "x1_normed", 3)
            add_rows("x1", 1, 1)
            norm_tile("x1", N_X1, 1, normed, "x1_normed", 4)
            for g in TN:
                scaled_T("hT", int(g[0]), int(g[1]), hT, G_X)

            def row_max(h):
                filled(ve, f"sc{h}")
                V.tensor_reduce(stat[:, 32 + 2 * h:34 + 2 * h], bank(f"sc{h}").rearrange("p (t m) -> p t m", t=TT),
                                AX, ALU.max).then_inc(s["s_max"], 1)
                ve.wait_ge(s["s_max"], h + 1)
                V.tensor_scalar(stat[:, 40 + 2 * h:42 + 2 * h], stat[:, 32 + 2 * h:34 + 2 * h], -(XDH ** -0.5), None,
                                ALU.mult).then_inc(s["s_neg"], 1)

            def normalise(h):
                ve.wait_ge(s["s_exp"], 2 * h + 2)
                V.reciprocal(stat[:, 32 + 2 * h:34 + 2 * h], stat[:, 48 + 2 * h:50 + 2 * h]).then_inc(s["s_rec"], 1)
                ve.wait_ge(s["s_rec"], h + 1)
                V.tensor_tensor(probs[:, h], probs[:, h],
                                stat[:, 32 + 2 * h:34 + 2 * h].unsqueeze(2).to_broadcast([P, TT, T]),
                                ALU.mult).then_inc(bank_emptied[bank_of(f"sc{h}")], 1)

            def probs_turned(h):
                if h >= 2:
                    filled(ve, f"ao{h - 2}")
                copy_out(f"pT{h}", probsT[:, h % 2])

            for h in range(0, XH, 2):
                row_max(h)
                row_max(h + 1)
                normalise(h)
                normalise(h + 1)
                probs_turned(h)
                probs_turned(h + 1)
            for h in range(XH):
                low_of(f"ao{h}", hT[:, 1, 2 * h:2 * h + 2, :], hT[:, 0, 2 * h:2 * h + 2, :])
            add_rows("x2", 0, 0)
            add_rows("x2", 1, 0)
            add_rows("x2", 0, 1)
            ve.wait_ge(s["gffn_in"], 16)
            norm_tile("x2", N_X2, 0, normed, "x2_normed", 3, g_ffn)
            add_rows("x2", 1, 1)
            norm_tile("x2", N_X2, 1, normed, "x2_normed", 4, g_ffn)
            plain_T("hf", 0, 0, side_T)

            ve.wait_ge(s["wr_in"], 32)
            idx = stat[:, 0:8].rearrange("p (t k) -> p t k", t=TT)

            def route(t):
                filled(ve, f"lg{t}")
                V.tensor_tensor(lg[:, t], bank(f"lg{t}")[:, 0:N_EXP], router_bias[:], ALU.add).then_inc(
                    bank_emptied[bank_of(f"lg{t}")], 1)
                emptied(ve, f"lg{t}")
                top = stat[:, 64 + 8 * t:72 + 8 * t]
                V.max(top, lg[:, t, :]).then_inc(s["top_made"], 1)
                ve.wait_ge(s["top_made"], t + 1)
                V.max_index(top_i[:, t, :], top, lg[:, t, :]).then_inc(s["idx_made"], 1)
                V.tensor_scalar(stat[:, 60 + t:61 + t], top[:, 0:1], -1.0, None, ALU.mult).then_inc(s["top_neg"], 1)
                ve.wait_ge(s["idx_made"], t + 1)
                V.tensor_copy(idx[:, t, :], top_i[:, t, 0:TOPK]).then_inc(s["idxf_made"], 1)
                ve.wait_ge(s["idxf_made"], t + 1)
                V.tensor_tensor(eq[:, t], idx[:, t, :].unsqueeze(2).to_broadcast([P, TOPK, N_EXP]),
                                exp_iota[:].unsqueeze(1).to_broadcast([P, TOPK, N_EXP]), ALU.is_equal).then_inc(
                    s["eq_made"], 1)
                ve.wait_ge(s["eq_made"], t + 1)
                V.tensor_reduce(mask[:, t], eq[:, t].rearrange("p k e -> p e k"), AX, ALU.add).then_inc(
                    s["mask_made"], 1)

            route(0)
            plain_T("hf", 1, 0, side_T)
            route(1)
            filled(ve, "pos")
            V.scalar_tensor_tensor(lg, bank("pos")[:, 0:TT * N_EXP].rearrange("p (t e) -> p t e", t=TT), 1.0, mask,
                                   ALU.add, ALU.mult).then_inc(s["pos_masked"], 1)
            V.tensor_reduce(stat[:, 92:93], bank("pos")[:, TT * N_EXP:3 * N_EXP], AX, ALU.max).then_inc(
                bank_emptied[bank_of("pos")], 1)
            ve.wait_ge(s["pos_masked"], 1)
            for r in range(ROUNDS):
                V.tensor_scalar(table[:, :, r * N_EXP:(r + 1) * N_EXP], lg, float(-1 - SLOTS * r), None, ALU.add)
            V.memset(table[:, :, VEXP:160], -1.0).then_inc(s["table_made"], 1)

            def make_take(v):
                for t in range(TT):
                    last = V.tensor_scalar(take[:, t, :], slot_iota[:], table[:, t, bass.ds(v, 1)], None, ALU.is_equal)
                last.then_inc(s["take_made"], 1)

            ve.wait_ge(s["table_made"], 1)
            make_take(0)
            gate4 = stat[:, 80:88].rearrange("p (t k) -> p t k", t=TT)
            for t in range(TT):
                ve.wait_ge(s["gate_exp"], t + 1)
                V.reciprocal(stat[:, 90 + t:91 + t], stat[:, 88 + t:89 + t]).then_inc(s["gate_rec"], 1)
            for t in range(TT):
                ve.wait_ge(s["gate_rec"], t + 1)
                V.tensor_scalar(gate4[:, t, :], gate4[:, t, :], stat[:, 90 + t:91 + t], None,
                                ALU.mult).then_inc(s["gate_made"], 1)
            for t in range(TT):
                ve.wait_ge(s["gate_made"], t + 1)
                V.tensor_tensor(eq[:, t], eq[:, t], gate4[:, t, :].unsqueeze(2).to_broadcast([P, TOPK, N_EXP]),
                                ALU.mult).then_inc(s["geq_made"], 1)
            ve.wait_ge(s["geq_made"], 2)
            for r in range(ROUNDS):
                V.tensor_reduce(gates[:, :, r * N_EXP:(r + 1) * N_EXP], eq.rearrange("p t k e -> p t e k"), AX,
                                ALU.add).then_inc(s["gate_table"], 1)
            filled(ve, "gT")
            V.tensor_copy(gateT, bank("gT")[0:N_EXP, 0:T]).then_inc(bank_emptied[bank_of("gT")], 1)
            emptied(ve, "pos")
            V.tensor_scalar(stat[0:1, 100:100 + ROUNDS - 1], slot_iota[0:1, 1:ROUNDS], float(SLOTS), stat[0:1, 92:93],
                            ALU.mult, ALU.is_lt).then_inc(s["cnt_cmp"], 1)
            ve.wait_ge(s["cnt_cmp"], 1)
            V.tensor_reduce(stat[0:1, 104:105], stat[0:1, 100:100 + ROUNDS - 1], AX, ALU.add).then_inc(s["cnt_sum"], 1)
            ve.wait_ge(s["cnt_sum"], 1)
            V.tensor_scalar(stat[0:1, 105:106], stat[0:1, 104:105], 1.0, float(GROUPS_OF_EXPERTS), ALU.add,
                            ALU.mult).then_inc(s["cnt_mul"], 1)
            ve.wait_ge(s["cnt_mul"], 1)
            V.tensor_copy(trips[0:1, 0:1], stat[0:1, 105:106]).then_inc(s["trips_made"], 1)
            V.tensor_copy(pick.rearrange("p (r e) -> p r e", r=ROUNDS),
                          ident[0:N_EXP, 0:N_EXP].unsqueeze(1).to_broadcast([N_EXP, ROUNDS, N_EXP])).then_inc(
                s["pick_made"], 1)
            for g in TN:
                add_rows("y", int(g[0]), int(g[1]))
            for g in TN:
                emptied(ve, "y" + g)
            ve.wait_ge(s["gate_table"], ROUNDS)
            ve.wait_ge(s["pick_made"], 1)
            ve.wait_ge(s["trips_made"], 1)
            n = ve.value_load(trips[0:1, 0:1], min_val=GROUPS_OF_EXPERTS, max_val=ROUNDS * GROUPS_OF_EXPERTS)

            def expert(v):
                ve.wait_ge(s["gather_filled"], v + 1)
                make_take(v + 1)
                for t in range(TT):
                    last = V.tensor_scalar(put[:, t], slot_iota[:].unsqueeze(1).to_broadcast([P, 2, SLOTS]),
                                           table[:, t, bass.ds(v, 1)], gates[:, t, bass.ds(v, 1)],
                                           ALU.is_equal, ALU.mult)
                last.then_inc(s["put_made"], 1)
                V.tensor_scalar(pick_e, ones[0:N_EXP, 0:SLOTS], pick[:, bass.ds(v, 1)], None,
                                ALU.mult).then_inc(s["pick_e_made"], 1)
                ve.wait_ge(s["h_filled"], v + 1)
                V.tensor_scalar(glu, ps[:, HIDDEN_BANKS[0], :], LIMIT, None, ALU.min).then_inc(s["glu_made"], 1)
                V.tensor_scalar(lin, ps[:, HIDDEN_BANKS[1], :], LIMIT, -LIMIT, ALU.min, ALU.max).then_inc(s["lin_made"], 1)
                ve.wait_ge(s["lin_made"], v + 1)
                V.scalar_tensor_tensor(lin, lin, 1.0, glu, ALU.add, ALU.mult).then_inc(s["lin_glu"], 1)
                ve.wait_ge(s["lin_glu"], v + 1)
                ve.wait_ge(s["sig_made"], v + 1)
                V.tensor_tensor(act, lin, sig, ALU.mult).then_inc(s["act_made"], 1)
                for t in range(TT):
                    for j in range(2):
                        k = 2 * t + j
                        c = slice(j * HALF, (j + 1) * HALF)
                        ve.wait_ge(s["scatter_filled"], v * 4 + (k + 1))
                        V.tensor_tensor(rows[:, t, c], ps[:, SCATTER_BANKS[k], :], rows[:, t, c], ALU.add).then_inc(
                            s[f"y_added{k}"], 1)

            with ve.Fori(0, n) as i:
                for k in range(UNROLL):
                    expert(i * UNROLL + k)
            ve.wait_ge(s["gfin_in"], 16)
            for t in range(TT):
                norm_tile("f", N_OUT, t, rows, "f_made", 2 * t + 2, g_final)

        @block.tensor
        def _(pe):
            M = nc.tensor

            def start_group(group):
                if INDEX[group] >= N_BANKS:
                    pe.wait_ge(bank_emptied[bank_of(group)], use_of(group) - 1)

            def end_group(ins, group):
                ins.then_inc(bank_filled[bank_of(group)], 1)

            def transposes(group, blocks):
                start_group(group)
                for n, (src, rows_) in enumerate(blocks):
                    w = src.shape[0]
                    last = M.transpose(bank(group)[0:rows_, n * w:(n + 1) * w], src, ident[0:w, 0:w])
                end_group(last, group)

            def rows_T(prefix, t, k, src, ready, need):
                pe.wait_ge(s[ready], need)
                transposes(f"{prefix}{t}{k}", [(src[:, t, c * P:(c + 1) * P], P) for c in range(4 * k, 4 * k + 4)])

            PART_PRODUCTS = [(0, 0), (0, 1), (1, 0)]

            def has_half(name, half):
                pe.wait_ge(s["low_made"], 2 * SPLIT.index(name) + half + 1)

            def rows_half(group, lhs, name, half, t):
                if half == 0:
                    start_group(group)
                w = pair(2 * SPLIT.index(name) + half)
                for a, b in PART_PRODUCTS:
                    for c in range(DC // 2):
                        first, final = half == 0 and a + b + c == 0, half == 1 and a == 1 and c == DC // 2 - 1
                        last = M.matmul(bank(group), lhs[:, a, half * (DC // 2) + c, t * P:(t + 1) * P], w[:, b, c, :],
                                        start=first, stop=final, skip_group_check=True)
                if half == 1:
                    end_group(last, group)
                return last

            def row_products(prefix, suffix, lhs, name, made=None):
                for half in range(2):
                    has_half(name, half)
                    for t in range(TT):
                        if made:
                            made(half, t)
                        last = rows_half(f"{prefix}{t}{suffix}", lhs, name, half, t)
                    if half == 0:
                        last.then_inc(s["first_half_used"], 1)

            def row_products_in_turn(prefix, suffix, lhs, name):
                for t in range(TT):
                    for half in range(2):
                        if t == 0:
                            has_half(name, half)
                        last = rows_half(f"{prefix}{t}{suffix}", lhs, name, half, t)
                        if half == 0 and t == TT - 1:
                            last.then_inc(s["first_half_used"], 1)

            def features_half(groups, name, half, rhs, made=None):
                has_half(name, half)
                if made:
                    for t in range(TT):
                        made(half, t)
                w = pair(2 * SPLIT.index(name) + half)
                for n, group in enumerate(groups):
                    if half == 0:
                        start_group(group)
                    for i in range(2):
                        f = 2 * n + i
                        for b, a in PART_PRODUCTS:
                            for c in range(DC // 2):
                                first = half == 0 and i + a + b + c == 0
                                final = half == 1 and i == 1 and b == 1 and c == DC // 2 - 1
                                last = M.matmul(bank(group)[:, i * T:(i + 1) * T], w[:, b, c, f * P:(f + 1) * P],
                                                rhs[:, a, half * (DC // 2) + c, :], start=first, stop=final,
                                                skip_group_check=True)
                    if half == 1:
                        end_group(last, group)
                if half == 0:
                    last.then_inc(s["first_half_used"], 1)

            def turned(prefix):
                return lambda half, t: emptied(pe, f"{prefix}{t}{half}")

            pe.wait_ge(s["ident_made"], 2)
            pe.wait_ge(s["small_in"], 16 * 5)
            transposes("vecs", [(vec_rows[:], P)])
            for g in TN:
                t, k = int(g[0]), int(g[1])
                rows_T("xT", t, k, normed, "x_normed", 2 * t + k + 1)
            pe.wait_ge(s["wa_split"], 1)
            start_group("aL")
            for half in range(2):
                for t in range(TT):
                    emptied(pe, f"xT{t}{half}")
                for b, a in PART_PRODUCTS:
                    for c in range(half * (DC // 2), (half + 1) * (DC // 2)):
                        last = M.matmul(bank("aL")[0:RANK, 0:T], wa_parts[:, b, c, :], hT[:, a, c, :],
                                        start=half + a + b + c == 0, stop=half == 1 and b == 1 and c == DC - 1)
            end_group(last, "aL")
            for half in range(2):
                features_half(["q", "k"], "qk", half, hT)
            emptied(pe, "aL")
            pe.wait_ge(s["wa2_in"], 16)
            start_group("la")
            for f in range(2):
                last = M.matmul(bank("la")[:, f * T:(f + 1) * T], wa2[:, f * P:(f + 1) * P], aT[:], start=True, stop=True)
            end_group(last, "la")
            for name in ("v", "r", "sv"):
                row_products(name, "", hT, name)
            pe.wait_ge(s["wsgu_masked"], 1)
            transposes("wsT", [(w_sgu[:, g, :], P) for g in range(SGU_G)])
            row_products("u", "", hT, "u")
            emptied(pe, "q")
            pe.wait_ge(s["keys_made"], GLA_H)
            for t in range(TT):
                start_group(f"att{t}")
                for h in range(GLA_H):
                    last = M.matmul(bank(f"att{t}")[:, h * P:(h + 1) * P], kz[:, h, t * P:(t + 1) * P],
                                    q_in[:, h // 2, t * P:(t + 1) * P], start=True, stop=True)
                end_group(last, f"att{t}")
            emptied(pe, "k")
            transposes("koT", [(k_out[:, f, t * P:(t + 1) * P], P) for t in range(TT) for f in range(2)])
            for g in TN:
                t, k = int(g[0]), int(g[1])
                rows_T("memT", t, k, side, "mem_normed", 2 * t + k + 1)

            row_products("ga", "0", hT, "ga0")
            emptied(pe, "koT")
            emptied(pe, "v1")
            emptied(pe, "v0")
            for n in range(3):
                start_group(f"kv{n}")
                for f in range(2):
                    last = M.matmul(bank(f"kv{n}")[:, f * T:(f + 1) * T], koz[:, n // 2, n % 2, f * P:(f + 1) * P],
                                    values[:, n // 2, f * T:(f + 1) * T], start=True, stop=True)
                end_group(last, f"kv{n}")
            emptied(pe, "wsT")
            pe.wait_ge(s["sv_normed"], 2)
            for t in range(TT):
                start_group(f"mix{t}")
                for g in range(SGU_G):
                    c = slice(g * P, (g + 1) * P)
                    last = M.matmul(bank(f"mix{t}")[:, c], w_sguT[:, g, :], sgu_v[:, t, c], start=True, stop=True)
                end_group(last, f"mix{t}")
            row_products("ga", "1", hT, "ga1")
            emptied(pe, "att0")
            emptied(pe, "att1")
            for t in range(TT):
                start_group(f"o{t}")
                emptied(pe, f"kv{2 * t}")
                todo = []
                for h in range(GLA_H):
                    c = slice(h * P, (h + 1) * P)
                    todo.append((bank(f"o{t}")[:, c], attz[:, t, h, :], values[:, t, c]))
                for m in range(2):
                    n = 2 * t + m
                    if n:
                        for f in range(2):
                            todo.append((bank(f"o{t}")[64 * m:64 * m + 64, f * T:(f + 1) * T],
                                         q_in[:, f, n * GLA_C:(n + 1) * GLA_C], states[:, n - 1, f, :]))
                for i, (o, l, r) in enumerate(todo):
                    last = M.matmul(o, l, r, start=i == 0, stop=i == len(todo) - 1, skip_group_check=True)
                end_group(last, f"o{t}")
            row_products("gb", "0", hT, "gb0")
            for t in range(TT):
                emptied(pe, f"mix{t}")
            for k in range(2):
                transposes(f"sboT{k}", [(sgu_u[:, t, (2 * k + i) * P:(2 * k + i + 1) * P], P)
                                        for i in range(2) for t in range(TT)])
            row_products("gb", "1", hT, "gb1")
            pe.wait_ge(s["o_made"], 2)
            for k in range(2):
                transposes(f"oT{k}", [(o_rows[:, t, (2 * k + i) * P:(2 * k + i + 1) * P], P)
                                      for i in range(2) for t in range(TT)])
            for branch, src, name, tr in (("ya", oT, "pa", "oT"), ("yb", sboT, "pb", "sboT")):
                emptied(pe, tr + "0")
                emptied(pe, tr + "1")
                for half in range(2):
                    raw_arrived(pe, 2 * PIECES.index(name) + half)
                for g in TN:
                    t, n = int(g[0]), int(g[1])
                    start_group(branch + g)
                    for c in range(DC // 2):
                        w = raw_half(2 * PIECES.index(name) + c // 2).rearrange("p (c n) -> p c n", c=2)[:, c % 2]
                        last = M.matmul(bank(branch + g), src[:, c, t * P:(t + 1) * P], w[:, n * HALF:(n + 1) * HALF],
                                        start=c == 0, stop=c == DC // 2 - 1)
                    end_group(last, branch + g)
            for half in range(2):
                features_half(["kT0", "kT1"], "xk0", half, memT, turned("memT"))
            for g in TN:
                t, k = int(g[0]), int(g[1])
                rows_T("mT", t, k, normed, "mixed", 2 * t + k + 1)
            for half in range(2):
                features_half(["kT2", "kT3"], "xk1", half, memT)
            row_products("x1", "0", hT, "mx0", turned("mT"))
            row_products_in_turn("x1", "1", hT, "mx1")
            rows_T("hT", 0, 0, normed, "x1_normed", 1)
            rows_T("hT", 0, 1, normed, "x1_normed", 2)
            row_products("vm", "0", memT, "xv0")
            rows_T("hT", 1, 0, normed, "x1_normed", 3)
            rows_T("hT", 1, 1, normed, "x1_normed", 4)
            row_products("vm", "1", memT, "xv1")

            def scores(h):
                emptied(pe, f"xq{h}")
                emptied(pe, f"kT{h}")
                start_group(f"sc{h}")
                for t in range(TT):
                    for i in range(2):
                        last = M.matmul(bank(f"sc{h}")[:, t * T:(t + 1) * T], side_T[:, 2 * h + i, t * P:(t + 1) * P],
                                        kT[:, 2 * h + i, :], start=i == 0, stop=i == 1)
                end_group(last, f"sc{h}")

            def probs_T(h):
                emptied(pe, f"sc{h}")
                transposes(f"pT{h}", [(probs[:, h, t, m * P:(m + 1) * P], P) for m in range(2) for t in range(TT)])

            def attend(h):
                emptied(pe, f"pT{h}")
                if h == 0:
                    for g in TN:
                        emptied(pe, "vm" + g)
                start_group(f"ao{h}")
                for i in range(2):
                    for m in range(2):
                        c = XDH * h + P * i
                        last = M.matmul(bank(f"ao{h}")[:, i * T:(i + 1) * T], vm[:, m, c:c + P], probsT[:, h % 2, m, :],
                                        start=m == 0, stop=m == 1)
                end_group(last, f"ao{h}")

            for half in range(2):
                features_half(["xq0", "xq1"], "xq0", half, hT, turned("hT"))
            features_half(["xq2", "xq3"], "xq1", 0, hT)
            scores(0)
            scores(1)
            features_half(["xq2", "xq3"], "xq1", 1, hT)
            probs_T(0)
            probs_T(1)
            scores(2)
            scores(3)
            attend(0)
            attend(1)
            probs_T(2)
            probs_T(3)
            attend(2)
            attend(3)

            def logits(t):
                start_group(f"lg{t}")
                for c in range(DC):
                    if c % 4 == 0:
                        emptied(pe, f"hf{t}{c // 4}")
                    last = M.matmul(bank(f"lg{t}")[:, 0:N_EXP], side_T[:, c, t * P:(t + 1) * P], wr[:, c, :],
                                    start=c == 0, stop=c == DC - 1)
                end_group(last, f"lg{t}")

            def heads_made(half, t):
                emptied(pe, f"ao{2 * half}")
                emptied(pe, f"ao{2 * half + 1}")

            row_products("x2", "0", hT, "xo0", heads_made)
            row_products_in_turn("x2", "1", hT, "xo1")
            rows_T("hf", 0, 0, normed, "x2_normed", 1)
            rows_T("hf", 0, 1, normed, "x2_normed", 2)
            pe.wait_ge(s["wr_in"], 32)
            logits(0)
            rows_T("hf", 1, 0, normed, "x2_normed", 3)
            rows_T("hf", 1, 1, normed, "x2_normed", 4)
            logits(1)
            pe.wait_ge(s["mask_made"], 2)
            start_group("pos")
            pos = [(0, upper, 0), (1, upper, 1), (1, ones, 0), (2, ones, 0), (2, ones, 1)]
            for n, (o, l, t) in enumerate(pos):
                last = M.matmul(bank("pos")[:, o * N_EXP:(o + 1) * N_EXP], l[:], mask[:, t, :], start=n == 0,
                                stop=n == len(pos) - 1, skip_group_check=True)
            end_group(last, "pos")
            def gather(need_take):
                pe.wait_ge(s["take_made"], need_take)
                for t in range(TT):
                    for j in range(2):
                        last = M.matmul(ps[64 * j:64 * j + 64, GATHER_BANK, :], take[:, t, :],
                                        normed[:, t, j * HALF:(j + 1) * HALF], start=t == 0, stop=t == 1,
                                        skip_group_check=True)
                last.then_inc(s["gather_filled"], 1)

            def gather_T(need_copy):
                pe.wait_ge(s["gather_copied"], need_copy)
                for q in range(4):
                    last = M.transpose(ps[:, GATHER_BANK, q * P:(q + 1) * P], gathered[:, q * P:(q + 1) * P], ident[:])
                last.then_inc(s["xeT_filled"], 1)

            gather(1)
            pe.wait_ge(s["gate_table"], ROUNDS)
            transposes("gT", [(gates[:, t, 0:N_EXP], N_EXP) for t in range(TT)])
            emptied(pe, "gT")
            pe.wait_ge(s["b2_in"], 16)
            for g in TN:
                t, n = int(g[0]), int(g[1])
                start_group("y" + g)
                end_group(M.matmul(bank("y" + g), gateT[:, t * P:(t + 1) * P], b2[:, n * HALF:(n + 1) * HALF],
                                   start=True, stop=True), "y" + g)
            gather_T(1)
            pe.wait_ge(s["b1_in"], 16)
            pe.wait_ge(s["trips_made"], 1)
            n = pe.value_load(trips[0:1, 0:1], min_val=GROUPS_OF_EXPERTS, max_val=ROUNDS * GROUPS_OF_EXPERTS)

            def chunk_arrived(i, k, c):
                m = k * CHUNKS + c
                pe.wait_ge(chunk_full[slot_of(m)], i * (16 * LOADS_PER_SLOT) + 16 * (m // N_CHUNK_SLOTS + 1))

            def expert(i, k):
                v = i * UNROLL + k
                pe.wait_ge(s["xeT_made"], v + 1)
                for c in range(W1_CHUNKS):
                    chunk_arrived(i, k, c)
                    for h in range(2):
                        for j in range(2):
                            last = M.matmul(ps[64 * j:64 * j + 64, HIDDEN_BANKS[h], :], xeT[:, c % 4, (c // 4) * SLOTS:(c // 4 + 1) * SLOTS],
                                            chunk(k * CHUNKS + c)[:, h * D + j * HALF:h * D + (j + 1) * HALF],
                                            start=c == 0, stop=False, skip_group_check=True)
                    last.then_inc(s["chunk_used"], 1)
                pe.wait_ge(s["pick_e_made"], v + 1)
                for h in range(2):
                    for j in range(2):
                        last = M.matmul(ps[64 * j:64 * j + 64, HIDDEN_BANKS[h], :], pick_e,
                                        b1[:, h * D + j * HALF:h * D + (j + 1) * HALF],
                                        start=False, stop=True, skip_group_check=True)
                last.then_inc(s["h_filled"], 1)
                pe.wait_ge(s["put_made"], v + 1)
                emptied(pe, "y11")
                for t in range(TT):
                    last = M.transpose(ps[:, PUT_BANK, t * P:(t + 1) * P], put[:, t].rearrange("p j s -> p (j s)"), ident[:])
                last.then_inc(s["putT_filled"], 1)
                gather(v + 2)
                gather_T(v + 2)
                pe.wait_ge(s["act_made"], v + 1)
                pe.wait_ge(s["putT_made"], v + 1)
                for q in range(4):
                    last = M.transpose(ps[:, PUT_BANK, q * P:(q + 1) * P], act[:, q * P:(q + 1) * P], ident[:])
                last.then_inc(s["actT_filled"], 1)
                pe.wait_ge(s["actT_made"], v + 1)
                for w2 in range(W2_CHUNKS):
                    chunk_arrived(i, k, W1_CHUNKS + w2)
                    w = chunk(k * CHUNKS + W1_CHUNKS + w2).rearrange("p (i n) -> p i n", i=2)
                    for h in range(2):
                        c = 2 * w2 + h
                        for j in range(2):
                            last = M.matmul(ps[64 * j:64 * j + 64, Y_BANK, :], actT[:, c % 4, (c // 4) * SLOTS:(c // 4 + 1) * SLOTS],
                                            w[:, h, j * HALF:(j + 1) * HALF], start=c == 0, stop=c == DC - 1,
                                            skip_group_check=True)
                    last.then_inc(s["chunk_used"] if w2 < W2_CHUNKS - 1 else s["y_filled"], 1)
                pe.wait_ge(s["y_copied"], v + 1)
                for t in range(TT):
                    for j in range(2):
                        q = slice(64 * j, 64 * j + 64)
                        M.matmul(ps[:, SCATTER_BANKS[2 * t + j], :], putT[q, t, :], y_rows[q, :], start=True,
                                 stop=True).then_inc(s["scatter_filled"], 1)

            with pe.Fori(0, n) as i:
                for k in range(UNROLL):
                    expert(i, k)


INPUTS = ["x", "mem", "norm_mix_g", "w_in", "gla_w_a2", "gla_b_a", "gla_out_g", "sgu_norm_g", "sgu_norm_b", "sgu_w",
          "sgu_b", "w_proj_a", "w_proj_b", "w_mix_out", "norm_x_g", "norm_mem_g", "w_xq", "w_xk", "w_xv", "w_xo",
          "norm_ffn_g", "w_router", "b_router", "w_e1", "b_e1", "w_e2", "b_e2", "norm_final_g"]


def kernel(**inputs):
    import numpy as np
    import concourse.bacc as bacc
    from concourse.bass_utils import run_bass_kernel_spmd

    nc = bacc.Bacc("TRN2", target_bir_lowering=False, num_devices=1)
    arrays = {f"in_{n}": np.ascontiguousarray(inputs[n]) for n in INPUTS}
    aps = {n: nc.dram_tensor(f"in_{n}", arrays[f"in_{n}"].shape, F32, kind="ExternalInput").ap() for n in INPUTS}
    out = nc.dram_tensor("out", (1, T, D), F32, kind="ExternalOutput").ap()
    layer_program(nc, aps, out)
    result = run_bass_kernel_spmd(nc, [arrays], core_ids=[0])
    return result.results[0]["out"]
```

```python
from contextlib import ExitStack

import concourse.bass as bass
from concourse import mybir

P = 128
F32 = mybir.dt.float32
F32R = mybir.dt.float32r
I32 = mybir.dt.int32
U32 = mybir.dt.uint32
ALU = mybir.AluOpType
ACT = mybir.ActivationFunctionType
AX = mybir.AxisListType.X

EPS = 1e-5
T = 256
TT = T // P
D = 1024
DC = D // P
HALF = 512
GLA_H, GLA_DK, GLA_DV, GLA_C, RANK, TAU = 4, 64, 128, 64, 16, 16.0
NCH = T // GLA_C
WV = GLA_H * GLA_DV
SGU_G = 4
XH, XDH = 4, 256
N_EXP, TOPK, LIMIT, ALPHA = 32, 4, 7.0, 1.702
SLOTS = 64
ROUNDS = T // SLOTS
VEXP = ROUNDS * N_EXP

OFF_V, OFF_R, OFF_A, OFF_U, OFF_SV, OFF_G = 512, 1024, 1536, 1552, 2064, 2576

PIECE_HALF = DC * HALF // 2
N_RAW_SLOTS = 4
N_PAIR_SLOTS = 3
W1_CHUNKS, W2_CHUNKS = DC, DC // 2
CHUNKS = W1_CHUNKS + W2_CHUNKS
CHUNK = 2 * D
N_CHUNK_SLOTS = 16
UNROLL = 4
GROUPS_OF_EXPERTS = N_EXP // UNROLL
assert UNROLL * CHUNKS % N_CHUNK_SLOTS == 0
EXTRA_CHUNKS = (0, 6, 7)
LOADS_PER_SLOT = UNROLL * CHUNKS // N_CHUNK_SLOTS

PIECES = ["qk", "v", "r", "sv", "u", "ga0", "ga1", "gb0", "gb1", "pa", "pb", "xk0", "xk1",
          "mx0", "mx1", "xv0", "xv1", "xq0", "xq1", "xo0", "xo1"]
LAST_USE = {"qk": "k", "v": "v1", "r": "r1", "sv": "sv1", "u": "u1", "ga0": "ga10", "ga1": "ga11",
            "gb0": "gb10", "gb1": "gb11", "pa": "ya11", "pb": "yb11", "xk0": "kT1", "xk1": "kT3",
            "mx0": "x110", "mx1": "x111", "xv0": "vm10", "xv1": "vm11", "xq0": "xq1", "xq1": "xq3",
            "xo0": "x210", "xo1": "x211"}
TN = ["00", "01", "10", "11"]


def each(prefix):
    return [prefix + g for g in TN]


GROUPS = (["vecs"] + each("xT") + ["aL", "q", "k", "la", "v0", "v1", "r0", "r1", "sv0", "sv1", "wsT", "u0", "u1",
                                   "att0", "att1", "koT"] + each("memT")
          + ["ga00", "ga10", "kv0", "kv1", "kv2", "mix0", "mix1", "ga01", "ga11", "o0", "o1",
             "gb00", "gb10", "gb01", "gb11", "oT0", "oT1", "sboT0", "sboT1"]
          + each("ya") + each("yb") + ["kT0", "kT1"] + each("mT") + ["kT2", "kT3"]
          + ["x100", "x110", "x101", "x111", "hT00", "hT01", "vm00", "vm10", "hT10", "hT11", "vm01", "vm11"]
          + ["xq0", "xq1", "xq2", "xq3", "sc0", "sc1", "pT0", "pT1", "sc2", "sc3", "ao0", "ao1", "pT2", "pT3",
             "ao2", "ao3"]
          + ["x200", "x210", "x201", "x211", "hf00", "hf01", "lg0", "hf10", "hf11", "lg1", "pos", "gT"])
HIGH_BY_SCALAR = ["xT01", "xT11", "memT01", "memT11", "oT0", "oT1", "sboT0", "sboT1", "mT00", "mT01", "mT10", "mT11", "hT01", "hT11",
                  "ao0", "ao1", "ao2", "ao3"]
HIGH_BY_VECTOR = ["xT00", "xT10", "memT00", "memT10", "hT00", "hT10"]
INDEX = {g: n for n, g in enumerate(GROUPS)}
N_BANKS = 8


def bank_of(group):
    return INDEX[group] % N_BANKS


BASE = bank_of("gT")
PUT_BANK, Y_BANK, GATHER_BANK = BASE, (BASE + 1) % N_BANKS, (BASE + 5) % N_BANKS
HIDDEN_BANKS = [(BASE + 6) % N_BANKS, (BASE + 7) % N_BANKS]
GATHER_BANK_USES = sum(n % N_BANKS == GATHER_BANK for n in range(INDEX["gT"]))
SCATTER_BANKS = [(BASE + 2) % N_BANKS, (BASE + 3) % N_BANKS, (BASE + 4) % N_BANKS, Y_BANK]


def use_of(group):
    return INDEX[group] // N_BANKS + 1


def layer_program(nc, a, out):
    with ExitStack() as ctx:
        def sb(name, shape, dt=F32):
            return ctx.enter_context(nc.sbuf_tensor(name, shape, dt))

        def sem(name):
            return ctx.enter_context(nc.semaphore(name))

        ps = ctx.enter_context(nc.psum_tensor("ps", [P, N_BANKS, HALF], F32))

        raw = sb("raw", [P, N_RAW_SLOTS * PIECE_HALF])
        with ExitStack() as early:
            def early_sb(name, shape):
                return early.enter_context(nc.sbuf_tensor(name, shape, F32R))

            pairs = early_sb("pairs", [P, N_PAIR_SLOTS, 2, DC // 2, HALF])
            hT = early_sb("hT", [P, 2, DC, T])
            memT = early_sb("memT", [P, 2, DC, T])
        late = sb("late", [P, 2 * N_PAIR_SLOTS * PIECE_HALF + 4 * DC * T])
        wa_parts = ctx.enter_context(nc.sbuf_tensor("wa_parts", [P, 2, DC, RANK], F32R))
        rows = sb("rows", [P, TT, D])
        normed = sb("normed", [P, TT, D])
        side = sb("side", [P, TT, D])
        shared = sb("shared", [P, 13 * 1024])
        ident = sb("ident", [P, P])
        upper = sb("upper", [P, P])
        upper_r = ctx.enter_context(nc.sbuf_tensor("upper_r", [P, P], F32R))
        ones_r = ctx.enter_context(nc.sbuf_tensor("ones_r", [P, P], F32R))
        mask = ctx.enter_context(nc.sbuf_tensor("mask", [P, TT, N_EXP], F32R))
        ones = sb("ones", [P, P])
        keep_att = sb("keep_att", [P, P])
        scan_keep = sb("scan_keep", [P, T])
        slot_iota = sb("slot_iota", [P, SLOTS])
        exp_iota = sb("exp_iota", [P, N_EXP])
        vec_rows = sb("vec_rows", [30, P])
        vecs = sb("vecs", [P, 30])
        wa = sb("wa", [P, DC, RANK])
        wr = sb("wr", [P, DC, N_EXP])
        wa2 = sb("wa2", [RANK, 2 * P])
        aT = sb("aT", [RANK, T])
        router_bias = sb("router_bias", [P, N_EXP])
        stat = sb("stat", [P, 192])
        G_MIX, G_X, G_MEM, B_A, B_SGU = 0, 8, 16, 24, 26
        N_X, N_MEM, N_X1, N_X2, N_OUT, EPS_COL = 128, 136, 144, 152, 160, 191
        eps = stat[:, EPS_COL:EPS_COL + 1]

        at = [0]

        def carve(cols, p=P):
            v = shared[0:p, at[0]:at[0] + cols]
            at[0] += cols
            assert at[0] <= 13 * 1024, at[0]
            return v

        def cut(v, *dims):
            if len(dims) == 2:
                return v.rearrange("p (a b) -> p a b", a=dims[0])
            return v.rearrange("p (a b c) -> p a b c", a=dims[0], b=dims[1])

        z = cut(carve(512), 2, T)
        lns = cut(carve(512), 2, T)
        cum = cut(carve(512), 2, T)
        ec = cut(carve(512), 2, T)
        q_in = cut(carve(512), 2, T)
        k_out = cut(carve(512), 2, T)
        kz = cut(carve(1024), GLA_H, T)
        values = cut(carve(1024), TT, WV)
        gate_r = cut(carve(1024), TT, WV)
        sgu_u = cut(carve(1024), TT, WV)
        sgu_v = cut(carve(1024), TT, WV)
        attz = carve(1024).rearrange("p (t h c) -> p t h c", t=TT, h=GLA_H)
        koz = carve(1024).rearrange("p (t m d) -> p t m d", t=TT, m=2)
        states = carve(3 * 512).rearrange("p (n f e) -> p n f e", n=3, f=2)
        w_sgu = cut(carve(512), SGU_G, P)
        w_sguT = cut(carve(512), SGU_G, P)
        g_out = carve(WV)
        sgu_vectors = sb("sgu_vectors", [P, CHUNK])
        g_sgu = sgu_vectors[:, 0:WV]
        b_sgu = sgu_vectors[:, WV:2 * WV]
        o_rows = cut(shared[:, 0:1024], TT, WV)
        oT, sboT = hT[:, :, 0:4, :], hT[:, :, 4:8, :]
        sq_o = cut(shared[:, 1024:2048], TT, WV)
        at[0] = 0
        kT = cut(carve(2048), DC, T)
        vm = cut(carve(2048), TT, D)
        probs = carve(4 * 512).rearrange("p (h t m) -> p h t m", h=XH, t=TT)
        probsT = carve(2 * 512).rearrange("p (b m t) -> p b m t", b=2, m=2)
        at[0] = 13 * 1024 - 3 * D
        g_ffn = carve(D)
        g_final = carve(D)
        b2 = carve(D, N_EXP)
        b1 = side[0:N_EXP].rearrange("p a b -> p (a b)")
        side_T = side.rearrange("p a b -> p (a b)").rearrange("p (c t) -> p c t", c=DC)
        at[0] = 2 * CHUNK
        table = cut(carve(TT * 160), TT, 160)
        gates = cut(carve(TT * VEXP), TT, VEXP)
        pick = carve(VEXP, N_EXP)
        eq = carve(TT * TOPK * N_EXP).rearrange("p (t k e) -> p t k e", t=TT, k=TOPK)
        lg = cut(carve(TT * N_EXP), TT, N_EXP)
        gateT = carve(T, N_EXP)
        take = cut(carve(TT * SLOTS), TT, SLOTS)
        put = carve(TT * 2 * SLOTS).rearrange("p (t j s) -> p t j s", t=TT, j=2)
        putT = cut(carve(TT * P), TT, P)
        pick_e = carve(SLOTS, N_EXP)
        gathered = carve(HALF)
        xeT = cut(carve(HALF), 4, P)
        glu_at = at[0]
        glu = carve(HALF)
        lin = carve(HALF)
        sig = carve(HALF)
        act = carve(HALF)
        before_glu = shared[:, glu_at:glu_at + CHUNK]
        actT = cut(carve(HALF), 4, P)
        y_rows = carve(HALF)
        assert at[0] <= 13 * 1024 - 3 * D and glu_at + 2 * CHUNK <= 13 * 1024 - 2 * D
        after_act = shared[:, glu_at + CHUNK:glu_at + 2 * CHUNK]
        trips = sb("trips", [1, 1], I32)
        top_i = sb("top_i", [P, TT, 8], U32)

        bank_filled = [sem(f"bank_filled{b}") for b in range(N_BANKS)]
        bank_emptied = [sem(f"bank_emptied{b}") for b in range(N_BANKS)]
        raw_full = [sem(f"raw_full{b}") for b in range(N_RAW_SLOTS)]
        extras_full = sem("extras_full")
        last_extra_full = sem("last_extra_full")
        chunk_full = [sem(f"chunk_full{b}") for b in range(N_CHUNK_SLOTS)]
        names = """high_made low_made first_half_used wa_split high_by_scalar high_by_vector x_in0 x_in1 mem_in
            small_in wa_in wa2_in wsgu_in gsgu_in wr_in gffn_in gfin_in b1_in b2_in out_sent ident_made
            consts_made zeros_made eps_made x1_ss x2_ss f_ss wsgu_masked x_sq x_std x_rstd x_normed mem_sq
            mem_std mem_rstd mem_normed z_abs z_exp z_ln logs_made cum_made cum_exp cum_neg_exp cum_diff
            rest_exp keys_made r_sig r_gate sv_stat sv_mv sv_std sv_rstd sv_g sv_normed o_sq o_ss o_std
            o_rstd o_made mixed x1_sq x1_std x1_rstd x1_normed s_max s_neg s_exp s_rec x2_sq x2_std x2_rstd
            x2_normed top_made idx_made idxf_made top_neg gate_exp gate_rec gate_made eq_made mask_made
            geq_made gate_table pos_masked table_made cnt_cmp cnt_sum cnt_mul trips_made pick_made take_made
            put_made pick_e_made gather_filled gather_copied xeT_filled xeT_made h_filled glu_made sig_made
            lin_made lin_glu act_made putT_filled putT_made actT_filled actT_made y_filled y_copied
            scatter_filled y_added0 y_added1 y_added2 y_added3 chunk_used f_sq f_std f_rstd f_made""".split()
        s = {n: sem(n) for n in names}

        block = ctx.enter_context(nc.Block())

        def raw_half(n):
            k = n % N_RAW_SLOTS
            return raw[:, k * PIECE_HALF:(k + 1) * PIECE_HALF]

        def raw_arrived(eng, n):
            eng.wait_ge(raw_full[n % N_RAW_SLOTS], 16 * (n // N_RAW_SLOTS + 1))

        def pair(m):
            return pairs[:, m % N_PAIR_SLOTS]

        def split_used(eng, m):
            if m % 2 == 0:
                eng.wait_ge(s["first_half_used"], m // 2 + 1)
            else:
                filled(eng, LAST_USE[PIECES[m // 2]])

        def late_slot(n):
            return late[:, n * CHUNK:(n + 1) * CHUNK]

        HALVES = 2 * len(PIECES)
        raw_order = range(HALVES - N_RAW_SLOTS, HALVES)
        pair_order = [m % N_PAIR_SLOTS for m in range(HALVES - N_PAIR_SLOTS, HALVES)]
        first_T = 2 * N_PAIR_SLOTS
        chunk_slots = ([late_slot(first_T + 2), late_slot(first_T + 3), shared[:, 0:CHUNK]]
                       + [raw_half(r) for r in raw_order[:3]] + [shared[:, CHUNK:2 * CHUNK], raw_half(raw_order[3])]
                       + [late_slot(2 * q + i) for q in pair_order for i in range(2)]
                       + [late_slot(first_T), late_slot(first_T + 1)])
        assert len(chunk_slots) == N_CHUNK_SLOTS and PIECE_HALF == CHUNK == DC * T

        def turn_of(c):
            return c - sum(extra < c for extra in EXTRA_CHUNKS)

        def slot_of(c, step_is_first):
            return (turn_of(c) if step_is_first else c - len(EXTRA_CHUNKS)) % N_CHUNK_SLOTS

        def chunk(c, step_is_first):
            if step_is_first and c in EXTRA_CHUNKS:
                return (sgu_vectors[:], before_glu, after_act)[EXTRA_CHUNKS.index(c)]
            return chunk_slots[slot_of(c, step_is_first)]

        def bank(group):
            return ps[:, bank_of(group), :]

        def filled(eng, group):
            eng.wait_ge(bank_filled[bank_of(group)], use_of(group))

        def emptied(eng, group):
            eng.wait_ge(bank_emptied[bank_of(group)], use_of(group))

        w_in = a["w_in"]

        def piece_source(name):
            def cols(w, lo):
                return w.rearrange("(c p) n -> p c n", p=P)[:, :, lo:lo + HALF]
            lows = {"qk": 0, "v": OFF_V, "r": OFF_R, "u": OFF_U, "sv": OFF_SV, "ga0": OFF_G,
                    "ga1": OFF_G + HALF, "gb0": OFF_G + D, "gb1": OFF_G + D + HALF}
            if name in lows:
                return cols(w_in[0], lows[name]), DC
            if name in ("pa", "pb"):
                return a["w_proj_a" if name == "pa" else "w_proj_b"][0].rearrange("(c p) n -> p c n", p=P), DC // 2
            w = {"xk": "w_xk", "xv": "w_xv", "mx": "w_mix_out", "xq": "w_xq", "xo": "w_xo"}[name[:2]]
            return cols(a[w][0], HALF * int(name[2])), DC

        @block.sync
        def _(sp):
            def load_half(n):
                if n >= N_RAW_SLOTS:
                    sp.wait_ge(s["low_made"], n - N_RAW_SLOTS + 1)
                src, c = piece_source(PIECES[n // 2])
                src = src[:, (n % 2) * (c // 2):(n % 2 + 1) * (c // 2), :]
                sp.dma_start(raw_half(n).rearrange("p (c n) -> p c n", c=c // 2), src).then_inc(
                    raw_full[n % N_RAW_SLOTS], 16)

            def load_chunk(c, e, step_is_first=False):
                k = c % CHUNKS
                dst = chunk(c, step_is_first)
                if k < W1_CHUNKS:
                    src = a["w_e1"][0, e, k * P:(k + 1) * P, :]
                else:
                    k -= W1_CHUNKS
                    src = a["w_e2"][0, e, 2 * k * P:2 * (k + 1) * P, :].rearrange("(i p) n -> p i n", i=2)
                    dst = dst.rearrange("p (i n) -> p i n", i=2)
                full = chunk_full[slot_of(c, step_is_first)]
                if step_is_first and c in EXTRA_CHUNKS:
                    full = last_extra_full if c == EXTRA_CHUNKS[-1] else extras_full
                sp.dma_start(dst, src).then_inc(full, 16)

            def chunk_was_used(v, c):
                if c < CHUNKS - 1:
                    sp.wait_ge(s["chunk_used"], v * (CHUNKS - 1) + (c + 1))
                else:
                    sp.wait_ge(s["y_filled"], v + 1)

            x_rows = a["x"][0].rearrange("(t p) d -> p t d", p=P)
            sp.dma_start(rows[:, 0, :], x_rows[:, 0, :]).then_inc(s["x_in0"], 16)
            sp.dma_start(rows[:, 1, :], x_rows[:, 1, :]).then_inc(s["x_in1"], 16)
            sp.dma_start(wa[:], w_in[0].rearrange("(c p) n -> p c n", p=P)[:, :, OFF_A:OFF_A + RANK]).then_inc(
                s["wa_in"], 16)
            sp.dma_start(wa2[:], a["gla_w_a2"][0]).then_inc(s["wa2_in"], 16)
            sp.dma_start(router_bias[:], a["b_router"][0:1, :].to_broadcast([P, N_EXP])).then_inc(s["wr_in"], 16)
            load_half(0)
            load_half(1)
            load_half(2)
            load_half(3)
            sp.dma_start(side[:], a["mem"][0].rearrange("(t p) d -> p t d", p=P)).then_inc(s["mem_in"], 16)
            sp.dma_start(g_out, a["gla_out_g"][0:1, :].to_broadcast([P, WV])).then_inc(s["gsgu_in"], 16)
            sp.dma_start(g_sgu, a["sgu_norm_g"][0:1, :].to_broadcast([P, WV])).then_inc(s["gsgu_in"], 16)
            sp.dma_start(b_sgu, a["sgu_norm_b"][0:1, :].to_broadcast([P, WV])).then_inc(s["gsgu_in"], 16)
            sp.dma_start(w_sgu, a["sgu_w"][0].rearrange("g t s -> t g s")).then_inc(s["wsgu_in"], 16)
            sp.dma_start(wr[:], a["w_router"][0].rearrange("(c p) n -> p c n", p=P)).then_inc(s["wr_in"], 16)
            for n in range(N_RAW_SLOTS, HALVES):
                load_half(n)
                if n == 2 * PIECES.index("xv1"):
                    filled(sp, "kT0")
                    sp.dma_start(g_ffn, a["norm_ffn_g"][0:1, :].to_broadcast([P, D])).then_inc(s["gffn_in"], 16)
                    sp.dma_start(g_final, a["norm_final_g"].rearrange("(a d) -> a d", a=1).to_broadcast(
                        [P, D])).then_inc(s["gfin_in"], 16)
                    sp.dma_start(b2, a["b_e2"][0]).then_inc(s["b2_in"], 16)

            def tenant_dead(turn):
                if turn == 0:
                    filled(sp, "vm11")
                elif turn == 2:
                    filled(sp, "sc3")
                elif 3 <= turn < 6:
                    sp.wait_ge(s["low_made"], raw_order[turn - 3] + 1)
                elif turn == 6:
                    filled(sp, "ao3")
                elif turn == 7:
                    sp.wait_ge(s["low_made"], raw_order[3] + 1)
                elif turn == 8:
                    filled(sp, "x210")
                elif turn == 10:
                    filled(sp, "x211")

            in_turn = []
            for m in range(UNROLL * CHUNKS):
                if m == EXTRA_CHUNKS[0]:
                    sp.wait_ge(s["sv_normed"], 2)
                elif m == EXTRA_CHUNKS[1]:
                    filled(sp, "ao3")
                elif m == EXTRA_CHUNKS[2]:
                    continue
                else:
                    if turn_of(m) < N_CHUNK_SLOTS:
                        tenant_dead(turn_of(m))
                    else:
                        before = in_turn[turn_of(m) - N_CHUNK_SLOTS]
                        chunk_was_used(before // CHUNKS, before % CHUNKS)
                    in_turn.append(m)
                load_chunk(m, m // CHUNKS, True)
                if turn_of(m) == N_CHUNK_SLOTS - 1:
                    filled(sp, "lg1")
                    sp.dma_start(b1, a["b_e1"][0]).then_inc(s["b1_in"], 16)
                    sp.wait_ge(s["x2_normed"], 4)
                    load_chunk(EXTRA_CHUNKS[2], 0, True)
            sp.wait_ge(s["trips_made"], 1)
            n = sp.value_load(trips[0:1, 0:1], min_val=GROUPS_OF_EXPERTS, max_val=ROUNDS * GROUPS_OF_EXPERTS)
            with sp.Fori(1, n) as i:
                e0 = sp.snap((i % GROUPS_OF_EXPERTS) * UNROLL)
                for m in range(UNROLL * CHUNKS):
                    before = m - N_CHUNK_SLOTS + UNROLL * CHUNKS
                    chunk_was_used((i - 1) * UNROLL + before // CHUNKS, before % CHUNKS)
                    load_chunk(m, e0 + m // CHUNKS)
            out_rows = out[0].rearrange("(t p) d -> p t d", p=P)
            for k in range(4):
                c = slice(k % 2 * HALF, (k % 2 + 1) * HALF)
                sp.wait_ge(s["f_made"], k + 1)
                sp.dma_start(out_rows[:, k // 2, c], rows[:, k // 2, c]).then_inc(s["out_sent"], 16)
            sp.wait_ge(s["out_sent"], 64)

        @block.gpsimd
        def _(pool):
            g = nc.gpsimd
            g.memset(ident[:], 0.0).then_inc(s["ident_made"], 1)
            pool.wait_ge(s["ident_made"], 1)
            g.affine_select(out=ident[:], in_=ident[:], compare_op=ALU.not_equal, fill=1.0, base=0,
                            pattern=[[-1, P]], channel_multiplier=1).then_inc(s["ident_made"], 1)
            g.memset(eps, EPS).then_inc(s["eps_made"], 1)

            def low_part(m):
                pool.wait_ge(s["high_made"], m + 1)
                high, low = (pair(m)[:, i].rearrange("p c n -> p (c n)") for i in range(2))
                g.tensor_tensor(low, raw_half(m), high, ALU.subtract).then_inc(s["low_made"], 1)

            g.memset(kz, 0.0)
            g.memset(attz, 0.0)
            g.memset(koz, 0.0)
            g.memset(states, 0.0).then_inc(s["zeros_made"], 1)
            g.memset(ones[:], 1.0)
            g.memset(scan_keep[:], 1.0).then_inc(s["consts_made"], 1)
            pool.wait_ge(s["consts_made"], 1)
            g.memset(scan_keep[:].rearrange("p (n c) -> p n c", c=GLA_C)[:, :, 0:1], 0.0)
            g.affine_select(out=upper[:], in_=ones[:], compare_op=ALU.is_ge, fill=0.0, base=-1,
                            pattern=[[1, P]], channel_multiplier=-1)
            g.affine_select(out=keep_att[:], in_=ones[:], compare_op=ALU.is_ge, fill=0.0, base=0,
                            pattern=[[1, P]], channel_multiplier=-1)
            g.iota(slot_iota[:], pattern=[[1, SLOTS]], base=0, channel_multiplier=0,
                   allow_small_or_imprecise_dtypes=True)
            g.iota(exp_iota[:], pattern=[[1, N_EXP]], base=0, channel_multiplier=0,
                   allow_small_or_imprecise_dtypes=True).then_inc(s["consts_made"], 1)
            pool.wait_ge(s["consts_made"], 2)
            g.memset(keep_att[0:64, 64:128], 0.0).then_inc(s["consts_made"], 1)
            g.tensor_copy(ones_r[:], ones[:])
            g.tensor_copy(upper_r[:], upper[:]).then_inc(s["consts_made"], 1)
            pool.wait_ge(s["wa_in"], 16)
            g.tensor_copy(wa_parts[:, 0], wa[:]).then_inc(s["wa_split"], 1)
            pool.wait_ge(s["wa_split"], 1)
            g.tensor_tensor(wa_parts[:, 1], wa[:], wa_parts[:, 0], ALU.subtract).then_inc(s["wa_split"], 1)
            low_part(0)
            low_part(1)
            pool.wait_ge(s["wsgu_in"], 16)
            g.affine_select(out=w_sgu, in_=w_sgu, compare_op=ALU.is_ge, fill=0.0, base=0,
                            pattern=[[0, SGU_G], [-1, P]], channel_multiplier=1).then_inc(s["wsgu_masked"], 1)
            for m in range(2, HALVES):
                low_part(m)

        @block.scalar
        def _(sc):
            A = nc.scalar
            small = [("norm_mix_g", G_MIX, 8), ("norm_x_g", G_X, 8), ("norm_mem_g", G_MEM, 8), ("gla_b_a", B_A, 2)]
            for name, r, n in small:
                sc.dma_start(vec_rows[r:r + n, :], a[name][0].rearrange("(c p) -> c p", p=P)).then_inc(s["small_in"], 16)
            sc.dma_start(vec_rows[B_SGU:B_SGU + 4, :], a["sgu_b"][0]).then_inc(s["small_in"], 16)

            A.preload_act_table(ACT.Sqrt)

            def squares(src, scratch, col, done):
                for t in range(TT):
                    A.activation(scratch[:, t, :], src[:, t, :], ACT.Square,
                                 accum_out=stat[:, col + t:col + t + 1]).then_inc(s[done], 1)

            def root(dst, src, width, ready, need, done):
                sc.wait_ge(s[ready], need)
                A.activation(dst, src, ACT.Sqrt, scale=1.0 / width, bias=eps).then_inc(s[done], 1)

            def half_squares(name, col, t, n, scratch):
                c = slice(n * HALF, (n + 1) * HALF)
                A.activation(scratch[:, t, c], rows[:, t, c], ACT.Square,
                             accum_out=stat[:, col + 2 * t + n:col + 2 * t + n + 1]).then_inc(s[name + "_sq"], 1)

            def copy_out(group, dst):
                filled(sc, group)
                A.activation(dst, bank(group)[0:dst.shape[0], :].rearrange("p (a b) -> p a b", a=dst.shape[1])
                             if len(dst.shape) == 3 else bank(group), ACT.Copy).then_inc(
                    bank_emptied[bank_of(group)], 1)

            split = [0]

            def high_parts(name, half):
                stop = 2 * PIECES.index(name) + half + 1
                for m in range(split[0], stop):
                    high_part(m)
                split[0] = max(split[0], stop)

            def high_part(m):
                if m >= N_PAIR_SLOTS:
                    split_used(sc, m - N_PAIR_SLOTS)
                raw_arrived(sc, m)
                A.activation(pair(m)[:, 0].rearrange("p c n -> p (c n)"), raw_half(m), ACT.Copy).then_inc(
                    s["high_made"], 1)

            def plain_T(prefix, t, k, dst):
                copy_out(f"{prefix}{t}{k}", dst[:, 4 * k:4 * k + 4, t * P:(t + 1) * P])

            def high_of(group, dst):
                filled(sc, group)
                A.activation(dst, bank(group).rearrange("p (a b) -> p a b", a=dst.shape[1]), ACT.Copy).then_inc(
                    s["high_by_scalar"], 1)

            def high_scaled(prefix, t, k, dst, gain):
                group = f"{prefix}{t}{k}"
                filled(sc, group)
                for i in range(4):
                    c = 4 * k + i
                    last = A.activation(dst[:, 0, c, t * P:(t + 1) * P], bank(group)[:, i * P:(i + 1) * P], ACT.Copy,
                                        scale=vecs[:, gain + c:gain + c + 1])
                last.then_inc(s["high_by_scalar"], 1)

            sc.wait_ge(s["x_in0"], 16)
            A.activation(normed[:, 0, :], rows[:, 0, :], ACT.Square, accum_out=stat[:, N_X + 4:N_X + 5]).then_inc(
                s["x_sq"], 1)
            sc.wait_ge(s["eps_made"], 1)
            root(stat[:, N_X + 4:N_X + 6], stat[:, N_X + 4:N_X + 6], D, "x_sq", 2, "x_std")
            high_parts("qk", 0)
            emptied(sc, "vecs")
            high_scaled("xT", 0, 1, hT, G_MIX)
            high_scaled("xT", 1, 1, hT, G_MIX)
            high_parts("v", 0)
            sc.wait_ge(s["mem_in"], 16)
            scratch = memT[:, 0].rearrange("p c t -> p (c t)").rearrange("p (a b) -> p a b", a=TT)
            squares(side, scratch, N_MEM + 4, "mem_sq")
            root(stat[:, N_MEM + 4:N_MEM + 6], stat[:, N_MEM + 4:N_MEM + 6], D, "mem_sq", 2, "mem_std")
            A.preload_act_table_set("natural_log_exp_and_others")
            high_parts("v", 1)
            emptied(sc, "la")
            A.activation(lns, z, ACT.Abs).then_inc(s["z_abs"], 1)
            sc.wait_ge(s["z_abs"], 1)
            A.activation(lns, lns, ACT.Exp, scale=-1.0).then_inc(s["z_exp"], 1)
            sc.wait_ge(s["z_exp"], 1)
            A.activation(lns, lns, ACT.Ln, bias=1.0).then_inc(s["z_ln"], 1)
            high_parts("r", 1)
            sc.wait_ge(s["cum_made"], 2)
            A.activation(ec, cum, ACT.Exp, scale=1.0 / TAU).then_inc(s["cum_exp"], 1)
            A.activation(z, cum, ACT.Exp, scale=-1.0 / TAU).then_inc(s["cum_neg_exp"], 1)
            sc.wait_ge(s["cum_diff"], 1)
            A.activation(lns, lns, ACT.Exp, scale=1.0 / TAU).then_inc(s["rest_exp"], 1)
            copy_out("v0", values[:, 0, :])
            copy_out("v1", values[:, 1, :])
            high_parts("sv", 1)
            for t in range(TT):
                filled(sc, f"r{t}")
                A.activation(gate_r[:, t, :], bank(f"r{t}"), ACT.Sigmoid).then_inc(s["r_sig"], 1)
            for n, dst, following in (("sv", sgu_v, "u"), ("u", sgu_u, "ga0")):
                high_parts(following, 1)
                for t in range(TT):
                    filled(sc, f"{n}{t}")
                    A.activation(dst[:, t, :], bank(f"{n}{t}"), ACT.Gelu).then_inc(bank_emptied[bank_of(f"{n}{t}")], 1)
            high_parts("ga1", 0)
            high_scaled("memT", 0, 1, memT, G_MEM)
            high_scaled("memT", 1, 1, memT, G_MEM)
            sc.wait_ge(s["sv_mv"], 2)
            A.activation(stat[:, 4:6], stat[:, 112:116].rearrange("p (t k) -> p t k", t=TT)[:, :, 1], ACT.Sqrt,
                         bias=eps).then_inc(s["sv_std"], 1)

            def gates_of(name, n, dst):
                for t in range(TT):
                    group = f"{name}{t}{n}"
                    filled(sc, group)
                    A.activation(dst[:, t, n * HALF:(n + 1) * HALF], bank(group), ACT.Sigmoid).then_inc(
                        bank_emptied[bank_of(group)], 1)

            high_parts("ga1", 1)
            gates_of("ga", 0, normed)
            high_parts("gb0", 1)
            gates_of("ga", 1, normed)
            high_parts("gb1", 0)
            for t in range(TT):
                filled(sc, f"o{t}")
                A.activation(sq_o[:, t, :], bank(f"o{t}"), ACT.Square).then_inc(s["o_sq"], 1)
            root(stat[:, 16:24], stat[:, 16:24], GLA_DV, "o_ss", 2, "o_std")
            high_parts("gb1", 1)
            gates_of("gb", 0, side)
            high_parts("pa", 1)
            gates_of("gb", 1, side)
            for name, dst in (("oT", oT), ("sboT", sboT)):
                for k in range(2):
                    high_of(f"{name}{k}", dst[:, 0, 2 * k:2 * k + 2, :])
                if name == "oT":
                    high_parts("pb", 0)
            high_parts("xk1", 1)
            for k in range(2):
                copy_out(f"kT{k}", kT[:, 2 * k:2 * k + 2, :])
            high_parts("mx0", 0)
            for g in TN:
                t, k = int(g[0]), int(g[1])
                high_of("mT" + g, hT[:, 0, 4 * k:4 * k + 4, t * P:(t + 1) * P])
            high_parts("mx0", 1)
            for k in range(2, 4):
                copy_out(f"kT{k}", kT[:, 2 * k:2 * k + 2, :])
            high_parts("mx1", 1)

            def norm_half(name, col, t, n, scratch=normed):
                emptied(sc, f"{name}{t}{n}")
                half_squares(name, col, t, n, scratch)
                if n == 1:
                    root(stat[:, col + 4 + t:col + 5 + t], stat[:, col + 4 + t:col + 5 + t], D, name + "_ss", t + 1,
                         name + "_std")

            norm_half("x1", N_X1, 0, 0)
            norm_half("x1", N_X1, 1, 0)
            high_parts("xv0", 0)
            norm_half("x1", N_X1, 0, 1)
            high_parts("xv0", 1)
            norm_half("x1", N_X1, 1, 1)
            high_parts("xv1", 0)

            def value_rows(t, n):
                copy_out(f"vm{t}{n}", vm[:, t, n * HALF:(n + 1) * HALF])

            high_scaled("hT", 0, 1, hT, G_X)
            high_parts("xv1", 1)
            value_rows(0, 0)
            value_rows(1, 0)
            high_scaled("hT", 1, 1, hT, G_X)
            high_parts("xq0", 1)
            value_rows(0, 1)
            value_rows(1, 1)
            high_parts("xq1", 1)
            copy_out("xq0", side_T[:, 0:2, :])
            copy_out("xq1", side_T[:, 2:4, :])
            high_parts("xo0", 0)

            def soft(h):
                sc.wait_ge(s["s_neg"], h + 1)
                for t in range(TT):
                    A.activation(probs[:, h, t, :], bank(f"sc{h}")[:, t * T:(t + 1) * T], ACT.Exp, scale=XDH ** -0.5,
                                 bias=stat[:, 40 + 2 * h + t:41 + 2 * h + t],
                                 accum_out=stat[:, 48 + 2 * h + t:49 + 2 * h + t]).then_inc(s["s_exp"], 1)

            soft(0)
            soft(1)
            high_parts("xo0", 1)
            copy_out("xq2", side_T[:, 4:6, :])
            copy_out("xq3", side_T[:, 6:8, :])
            high_parts("xo1", 0)
            soft(2)
            soft(3)
            for h in range(XH):
                high_of(f"ao{h}", hT[:, 0, 2 * h:2 * h + 2, :])
            high_parts("xo1", 1)
            norm_half("x2", N_X2, 0, 0)
            norm_half("x2", N_X2, 1, 0)
            norm_half("x2", N_X2, 0, 1)
            norm_half("x2", N_X2, 1, 1)
            plain_T("hf", 0, 1, side_T)
            plain_T("hf", 1, 1, side_T)
            for t in range(TT):
                sc.wait_ge(s["top_neg"], t + 1)
                A.activation(stat[:, 80 + 4 * t:84 + 4 * t], stat[:, 64 + 8 * t:68 + 8 * t], ACT.Exp,
                             bias=stat[:, 60 + t:61 + t], accum_out=stat[:, 88 + t:89 + t]).then_inc(s["gate_exp"], 1)

            def copy_gathered(need):
                sc.wait_ge(s["gather_filled"], need)
                A.activation(gathered, ps[:, GATHER_BANK, :], ACT.Copy).then_inc(s["gather_copied"], 1)

            def copy_gathered_T(need):
                sc.wait_ge(s["xeT_filled"], need)
                A.activation(xeT, ps[:, GATHER_BANK, :].rearrange("p (a b) -> p a b", a=4), ACT.Copy).then_inc(
                    s["xeT_made"], 1)

            A.preload_act_table(ACT.Sigmoid)
            copy_gathered(1)
            copy_gathered_T(1)
            sc.wait_ge(s["trips_made"], 1)
            n = sc.value_load(trips[0:1, 0:1], min_val=GROUPS_OF_EXPERTS, max_val=ROUNDS * GROUPS_OF_EXPERTS)

            def expert(v):
                sc.wait_ge(s["putT_filled"], v + 1)
                A.activation(putT, ps[:, PUT_BANK, 0:TT * P].rearrange("p (a b) -> p a b", a=TT), ACT.Copy).then_inc(
                    s["putT_made"], 1)
                sc.wait_ge(s["glu_made"], v + 1)
                A.activation(sig, glu, ACT.Sigmoid, scale=ALPHA).then_inc(s["sig_made"], 1)
                copy_gathered(v + 2)
                copy_gathered_T(v + 2)
                sc.wait_ge(s["actT_filled"], v + 1)
                A.activation(actT, ps[:, PUT_BANK, :].rearrange("p (a b) -> p a b", a=4), ACT.Copy).then_inc(
                    s["actT_made"], 1)
                sc.wait_ge(s["y_filled"], v + 1)
                A.activation(y_rows, ps[:, Y_BANK, :], ACT.Copy).then_inc(s["y_copied"], 1)

            with sc.Fori(0, n) as i:
                A.preload_act_table(ACT.Sigmoid)
                for k in range(UNROLL):
                    expert(i * UNROLL + k)
            A.preload_act_table(ACT.Sqrt)
            for k in range(4):
                sc.wait_ge(s[f"y_added{k}"], n * UNROLL)
                half_squares("f", N_OUT, k // 2, k % 2, normed)
                if k % 2:
                    col = N_OUT + 4 + k // 2
                    root(stat[:, col:col + 1], stat[:, col:col + 1], D, "f_ss", k // 2 + 1, "f_std")

        @block.vector
        def _(ve):
            V = nc.vector

            def inv(col, n, std, done, need=1):
                ve.wait_ge(s[std], need)
                V.reciprocal(stat[:, col:col + n], stat[:, col:col + n]).then_inc(s[done], 1)

            def norm_tile(name, col, t, dst, done, squared, gain=None):
                ve.wait_ge(s[name + "_sq"], squared)
                ss = stat[:, col + 4 + t:col + 5 + t]
                V.tensor_tensor(ss, stat[:, col + 2 * t:col + 2 * t + 1], stat[:, col + 2 * t + 1:col + 2 * t + 2],
                                ALU.add).then_inc(s[name + "_ss"], 1)
                inv(col + 4 + t, 1, name + "_std", name + "_rstd", t + 1)
                ve.wait_ge(s[name + "_rstd"], t + 1)
                for n in range(2):
                    c = slice(n * HALF, (n + 1) * HALF)
                    if gain is None:
                        ins = V.tensor_scalar(dst[:, t, c], rows[:, t, c], ss, None, ALU.mult)
                    else:
                        ins = V.scalar_tensor_tensor(dst[:, t, c], rows[:, t, c], ss, gain[:, c], ALU.mult, ALU.mult)
                    ins.then_inc(s[done], 1)

            def scale_rows(dst, src, col, rstd, done):
                ve.wait_ge(s[rstd], 1)
                for t in range(TT):
                    for n in range(2):
                        c = slice(n * HALF, (n + 1) * HALF)
                        V.tensor_scalar(dst[:, t, c], src[:, t, c], stat[:, col + t:col + t + 1], None,
                                        ALU.mult).then_inc(s[done], 1)

            def copy_out(group, dst):
                filled(ve, group)
                V.tensor_copy(dst, bank(group).rearrange("p (a b) -> p a b", a=dst.shape[1])
                              if len(dst.shape) == 3 else bank(group)).then_inc(bank_emptied[bank_of(group)], 1)

            def plain_T(prefix, t, k, dst):
                copy_out(f"{prefix}{t}{k}", dst[:, 4 * k:4 * k + 4, t * P:(t + 1) * P])

            def low_of(group, dst, high):
                ve.wait_ge(s["high_by_scalar"], HIGH_BY_SCALAR.index(group) + 1)
                V.tensor_tensor(dst, bank(group).rearrange("p (a b) -> p a b", a=dst.shape[1]), high,
                                ALU.subtract).then_inc(bank_emptied[bank_of(group)], 1)

            def scaled_T(prefix, t, k, dst, gain):
                group = f"{prefix}{t}{k}"
                r = slice(t * P, (t + 1) * P)
                if group in HIGH_BY_VECTOR:
                    filled(ve, group)
                    V.tensor_tensor(dst[:, 0, 4 * k:4 * k + 4, r], bank(group).rearrange("p (c r) -> p c r", c=4),
                                    vecs[:, gain + 4 * k:gain + 4 * k + 4].unsqueeze(2).to_broadcast([P, 4, P]),
                                    ALU.mult).then_inc(s["high_by_vector"], 1)
                    ve.wait_ge(s["high_by_vector"], HIGH_BY_VECTOR.index(group) + 1)
                else:
                    ve.wait_ge(s["high_by_scalar"], HIGH_BY_SCALAR.index(group) + 1)
                for i in range(4):
                    c = 4 * k + i
                    last = V.scalar_tensor_tensor(dst[:, 1, c, r], bank(group)[:, i * P:(i + 1) * P],
                                                  vecs[:, gain + c:gain + c + 1], dst[:, 0, c, r],
                                                  ALU.mult, ALU.subtract)
                last.then_inc(bank_emptied[bank_of(group)], 1)

            ve.wait_ge(s["x_in1"], 16)
            V.tensor_tensor_reduce(normed[:, 1, :], rows[:, 1, :], rows[:, 1, :], 1.0, 0.0, ALU.mult, ALU.add,
                                   stat[:, N_X + 5:N_X + 6]).then_inc(s["x_sq"], 1)
            inv(N_X + 4, 2, "x_std", "x_rstd")
            scale_rows(normed, rows, N_X + 4, "x_rstd", "x_normed")
            filled(ve, "vecs")
            V.tensor_copy(vecs[:], bank("vecs")[:, 0:30]).then_inc(bank_emptied[bank_of("vecs")], 1)
            emptied(ve, "vecs")
            for k in range(2):
                for t in range(TT):
                    scaled_T("xT", t, k, hT, G_MIX)
            filled(ve, "aL")
            V.tensor_copy(aT[:], bank("aL")[0:RANK, 0:T]).then_inc(bank_emptied[bank_of("aL")], 1)
            filled(ve, "la")
            V.tensor_scalar(z[:, 0, :], bank("la")[:, 0:T], vecs[:, B_A:B_A + 1], None, ALU.add)
            V.tensor_scalar(z[:, 1, :], bank("la")[:, T:2 * T], vecs[:, B_A + 1:B_A + 2], None,
                            ALU.add).then_inc(bank_emptied[bank_of("la")], 1)
            inv(N_MEM + 4, 2, "mem_std", "mem_rstd")
            scale_rows(side, side, N_MEM + 4, "mem_rstd", "mem_normed")
            ve.wait_ge(s["z_ln"], 1)
            logs = q_in
            V.scalar_tensor_tensor(logs, z, 0.0, lns, ALU.min, ALU.subtract).then_inc(s["logs_made"], 1)
            ve.wait_ge(s["logs_made"], 1)
            ve.wait_ge(s["consts_made"], 3)
            for f in range(2):
                V.tensor_tensor_scan(cum[:, f, :], scan_keep[:], logs[:, f, :], 0.0, ALU.mult, ALU.add).then_inc(
                    s["cum_made"], 1)
            ve.wait_ge(s["cum_made"], 2)
            cum4 = cum.rearrange("p f (n c) -> p (f n) c", c=GLA_C)
            V.tensor_tensor(lns.rearrange("p f (n c) -> p (f n) c", c=GLA_C),
                            cum4[:, :, GLA_C - 1:GLA_C].to_broadcast([P, 2 * NCH, GLA_C]), cum4,
                            ALU.subtract).then_inc(s["cum_diff"], 1)
            filled(ve, "q")
            ve.wait_ge(s["cum_exp"], 1)
            V.scalar_tensor_tensor(q_in, bank("q").rearrange("p (a b) -> p a b", a=2), GLA_DK ** -0.5, ec,
                                   ALU.mult, ALU.mult).then_inc(bank_emptied[bank_of("q")], 1)
            filled(ve, "k")
            ve.wait_ge(s["cum_neg_exp"], 1)
            ve.wait_ge(s["zeros_made"], 1)
            for h in range(GLA_H):
                p0, f = 64 * (h % 2), h // 2
                V.tensor_tensor(kz[p0:p0 + 64, h, :], bank("k")[p0:p0 + 64, f * T:(f + 1) * T], z[p0:p0 + 64, f, :],
                                ALU.mult).then_inc(s["keys_made"], 1)
            ve.wait_ge(s["rest_exp"], 1)
            V.tensor_tensor(k_out, bank("k").rearrange("p (a b) -> p a b", a=2), lns, ALU.mult).then_inc(
                bank_emptied[bank_of("k")], 1)
            ve.wait_ge(s["gsgu_in"], 48)
            for t in range(TT):
                ve.wait_ge(s["r_sig"], t + 1)
                V.tensor_tensor(gate_r[:, t, :], bank(f"r{t}"), gate_r[:, t, :], ALU.mult).then_inc(
                    bank_emptied[bank_of(f"r{t}")], 1)
                emptied(ve, f"r{t}")
                V.tensor_tensor(gate_r[:, t, :], gate_r[:, t, :], g_out, ALU.mult).then_inc(s["r_gate"], 1)
            copy_out("wsT", w_sguT)
            for t in range(TT):
                emptied(ve, f"sv{t}")
                V.bn_stats(stat[:, 96 + 6 * t:102 + 6 * t], sgu_v[:, t, :]).then_inc(s["sv_stat"], 1)
            for t in range(TT):
                ve.wait_ge(s["sv_stat"], t + 1)
                V.bn_aggr(stat[:, 112 + 2 * t:114 + 2 * t], stat[:, 96 + 6 * t:102 + 6 * t]).then_inc(s["sv_mv"], 1)
            for t in range(TT):
                filled(ve, f"att{t}")
                V.copy_predicated(attz[:, t], keep_att[:].bitcast(U32).unsqueeze(1).to_broadcast([P, GLA_H, P]),
                                  bank(f"att{t}").rearrange("p (h c) -> p h c", h=GLA_H)).then_inc(
                    bank_emptied[bank_of(f"att{t}")], 1)
            filled(ve, "koT")
            for m in range(2):
                last = V.tensor_copy(koz[64 * m:64 * m + 64, :, m, :],
                                     bank("koT")[64 * m:64 * m + 64, :].rearrange("p (t d) -> p t d", t=TT))
            last.then_inc(bank_emptied[bank_of("koT")], 1)
            for g in TN:
                scaled_T("memT", int(g[0]), int(g[1]), memT, G_MEM)
            inv(4, 2, "sv_std", "sv_rstd")
            ve.wait_ge(s["sv_rstd"], 1)
            for t in range(TT):
                V.tensor_scalar(sgu_v[:, t, :], sgu_v[:, t, :], stat[:, 112 + 2 * t:113 + 2 * t],
                                stat[:, 4 + t:5 + t], ALU.subtract, ALU.mult).then_inc(s["sv_g"], 1)
            for t in range(TT):
                ve.wait_ge(s["sv_g"], t + 1)
                V.tensor_tensor(sgu_v[:, t, :], sgu_v[:, t, :], g_sgu, ALU.mult).then_inc(s["sv_g"], 1)
            for t in range(TT):
                ve.wait_ge(s["sv_g"], t + 3)
                V.tensor_tensor(sgu_v[:, t, :], sgu_v[:, t, :], b_sgu, ALU.add).then_inc(s["sv_normed"], 1)
            for n in range(3):
                filled(ve, f"kv{n}")
                if n:
                    emptied(ve, f"kv{n - 1}")
                for f in range(2):
                    for hh in range(2):
                        q, e = slice(64 * hh, 64 * hh + 64), slice(P * hh, P * hh + P)
                        src = bank(f"kv{n}")[q, f * T + P * hh:f * T + P * hh + P]
                        if n == 0:
                            last = V.tensor_copy(states[q, n, f, e], src)
                        else:
                            last_token = GLA_C * n + GLA_C - 1
                            last = V.scalar_tensor_tensor(states[q, n, f, e], states[q, n - 1, f, e],
                                                         ec[q, f, last_token:last_token + 1], src, ALU.mult, ALU.add)
                last.then_inc(bank_emptied[bank_of(f"kv{n}")], 1)
            for t in range(TT):
                filled(ve, f"mix{t}")
                emptied(ve, f"u{t}")
                for g in range(SGU_G):
                    c = slice(g * P, (g + 1) * P)
                    last = V.scalar_tensor_tensor(sgu_u[:, t, c], bank(f"mix{t}")[:, c], vecs[:, B_SGU + g:B_SGU + g + 1],
                                                  sgu_u[:, t, c], ALU.add, ALU.mult)
                last.then_inc(bank_emptied[bank_of(f"mix{t}")], 1)
            for t in range(TT):
                ve.wait_ge(s["o_sq"], t + 1)
                V.tensor_reduce(stat[:, 16 + 4 * t:20 + 4 * t], sq_o[:, t, :].rearrange("p (h e) -> p h e", h=GLA_H),
                                AX, ALU.add).then_inc(s["o_ss"], 1)
            inv(16, 8, "o_std", "o_rstd")
            ve.wait_ge(s["o_rstd"], 1)
            for t in range(TT):
                V.tensor_tensor(o_rows[:, t, :].rearrange("p (h e) -> p h e", h=GLA_H),
                                bank(f"o{t}").rearrange("p (h e) -> p h e", h=GLA_H),
                                stat[:, 16 + 4 * t:20 + 4 * t].unsqueeze(2).to_broadcast([P, GLA_H, GLA_DV]),
                                ALU.mult).then_inc(bank_emptied[bank_of(f"o{t}")], 1)
            ve.wait_ge(s["r_gate"], 2)
            for t in range(TT):
                emptied(ve, f"o{t}")
                V.tensor_tensor(o_rows[:, t, :], o_rows[:, t, :], gate_r[:, t, :], ALU.mult).then_inc(s["o_made"], 1)
            for name, dst in (("oT", oT), ("sboT", sboT)):
                for k in range(2):
                    c = slice(2 * k, 2 * k + 2)
                    low_of(f"{name}{k}", dst[:, 1, c, :], dst[:, 0, c, :])
            for g in TN:
                t, n = int(g[0]), int(g[1])
                c = slice(n * HALF, (n + 1) * HALF)
                filled(ve, "ya" + g)
                emptied(ve, "ga" + g)
                V.tensor_tensor(normed[:, t, c], bank("ya" + g), normed[:, t, c], ALU.mult).then_inc(
                    bank_emptied[bank_of("ya" + g)], 1)
            for g in TN:
                t, n = int(g[0]), int(g[1])
                c = slice(n * HALF, (n + 1) * HALF)
                filled(ve, "yb" + g)
                emptied(ve, "gb" + g)
                V.tensor_tensor(side[:, t, c], bank("yb" + g), side[:, t, c], ALU.mult).then_inc(
                    bank_emptied[bank_of("yb" + g)], 1)
                emptied(ve, "yb" + g)
                emptied(ve, "ya" + g)
                V.tensor_tensor(normed[:, t, c], normed[:, t, c], side[:, t, c], ALU.add).then_inc(s["mixed"], 1)
            for g in TN:
                t, k = int(g[0]), int(g[1])
                dst = hT[:, :, 4 * k:4 * k + 4, t * P:(t + 1) * P]
                low_of("mT" + g, dst[:, 1], dst[:, 0])

            def add_rows(name, t, n):
                group, c = f"{name}{t}{n}", slice(n * HALF, (n + 1) * HALF)
                filled(ve, group)
                V.tensor_tensor(rows[:, t, c], bank(group), rows[:, t, c], ALU.add).then_inc(
                    bank_emptied[bank_of(group)], 1)

            add_rows("x1", 0, 0)
            add_rows("x1", 1, 0)
            add_rows("x1", 0, 1)
            norm_tile("x1", N_X1, 0, normed, "x1_normed", 3)
            add_rows("x1", 1, 1)
            norm_tile("x1", N_X1, 1, normed, "x1_normed", 4)
            for g in TN:
                scaled_T("hT", int(g[0]), int(g[1]), hT, G_X)

            def row_max(h):
                filled(ve, f"sc{h}")
                V.tensor_reduce(stat[:, 32 + 2 * h:34 + 2 * h], bank(f"sc{h}").rearrange("p (t m) -> p t m", t=TT),
                                AX, ALU.max).then_inc(s["s_max"], 1)
                ve.wait_ge(s["s_max"], h + 1)
                V.tensor_scalar(stat[:, 40 + 2 * h:42 + 2 * h], stat[:, 32 + 2 * h:34 + 2 * h], -(XDH ** -0.5), None,
                                ALU.mult).then_inc(s["s_neg"], 1)

            def normalise(h):
                ve.wait_ge(s["s_exp"], 2 * h + 2)
                V.reciprocal(stat[:, 32 + 2 * h:34 + 2 * h], stat[:, 48 + 2 * h:50 + 2 * h]).then_inc(s["s_rec"], 1)
                ve.wait_ge(s["s_rec"], h + 1)
                V.tensor_tensor(probs[:, h], probs[:, h],
                                stat[:, 32 + 2 * h:34 + 2 * h].unsqueeze(2).to_broadcast([P, TT, T]),
                                ALU.mult).then_inc(bank_emptied[bank_of(f"sc{h}")], 1)

            def probs_turned(h):
                if h >= 2:
                    filled(ve, f"ao{h - 2}")
                copy_out(f"pT{h}", probsT[:, h % 2])

            for h in range(0, XH, 2):
                row_max(h)
                row_max(h + 1)
                normalise(h)
                normalise(h + 1)
                probs_turned(h)
                probs_turned(h + 1)
            for h in range(XH):
                low_of(f"ao{h}", hT[:, 1, 2 * h:2 * h + 2, :], hT[:, 0, 2 * h:2 * h + 2, :])
            add_rows("x2", 0, 0)
            add_rows("x2", 1, 0)
            add_rows("x2", 0, 1)
            ve.wait_ge(s["gffn_in"], 16)
            norm_tile("x2", N_X2, 0, normed, "x2_normed", 3, g_ffn)
            add_rows("x2", 1, 1)
            plain_T("hf", 0, 0, side_T)
            norm_tile("x2", N_X2, 1, normed, "x2_normed", 4, g_ffn)

            ve.wait_ge(s["wr_in"], 32)
            idx = stat[:, 0:8].rearrange("p (t k) -> p t k", t=TT)

            def route(t):
                filled(ve, f"lg{t}")
                V.tensor_tensor(lg[:, t], bank(f"lg{t}")[:, 0:N_EXP], router_bias[:], ALU.add).then_inc(
                    bank_emptied[bank_of(f"lg{t}")], 1)
                emptied(ve, f"lg{t}")
                top = stat[:, 64 + 8 * t:72 + 8 * t]
                V.max(top, lg[:, t, :]).then_inc(s["top_made"], 1)
                ve.wait_ge(s["top_made"], t + 1)
                V.max_index(top_i[:, t, :], top, lg[:, t, :]).then_inc(s["idx_made"], 1)
                V.tensor_scalar(stat[:, 60 + t:61 + t], top[:, 0:1], -1.0, None, ALU.mult).then_inc(s["top_neg"], 1)
                ve.wait_ge(s["idx_made"], t + 1)
                V.tensor_copy(idx[:, t, :], top_i[:, t, 0:TOPK]).then_inc(s["idxf_made"], 1)
                ve.wait_ge(s["idxf_made"], t + 1)
                V.tensor_tensor(eq[:, t], idx[:, t, :].unsqueeze(2).to_broadcast([P, TOPK, N_EXP]),
                                exp_iota[:].unsqueeze(1).to_broadcast([P, TOPK, N_EXP]), ALU.is_equal).then_inc(
                    s["eq_made"], 1)
                ve.wait_ge(s["eq_made"], t + 1)
                with nc.allow_low_precision(reason="the sums are 0 and 1"):
                    V.tensor_reduce(mask[:, t], eq[:, t].rearrange("p k e -> p e k"), AX, ALU.add).then_inc(
                        s["mask_made"], 1)

            plain_T("hf", 1, 0, side_T)
            route(0)
            route(1)
            filled(ve, "pos")
            V.scalar_tensor_tensor(lg, bank("pos")[:, 0:TT * N_EXP].rearrange("p (t e) -> p t e", t=TT), 1.0, mask[:],
                                   ALU.add, ALU.mult).then_inc(s["pos_masked"], 1)
            V.tensor_reduce(stat[:, 92:93], bank("pos")[:, TT * N_EXP:3 * N_EXP], AX, ALU.max).then_inc(
                bank_emptied[bank_of("pos")], 1)
            ve.wait_ge(s["pos_masked"], 1)
            for r in range(ROUNDS):
                V.tensor_scalar(table[:, :, r * N_EXP:(r + 1) * N_EXP], lg, float(-1 - SLOTS * r), None, ALU.add)
            V.memset(table[:, :, VEXP:160], -1.0).then_inc(s["table_made"], 1)

            def make_take(v):
                for t in range(TT):
                    last = V.tensor_scalar(take[:, t, :], slot_iota[:], table[:, t, bass.ds(v, 1)], None, ALU.is_equal)
                last.then_inc(s["take_made"], 1)

            ve.wait_ge(s["table_made"], 1)
            make_take(0)
            emptied(ve, "pos")
            V.tensor_scalar(stat[0:1, 100:100 + ROUNDS - 1], slot_iota[0:1, 1:ROUNDS], float(SLOTS), stat[0:1, 92:93],
                            ALU.mult, ALU.is_lt).then_inc(s["cnt_cmp"], 1)
            ve.wait_ge(s["cnt_cmp"], 1)
            V.tensor_reduce(stat[0:1, 104:105], stat[0:1, 100:100 + ROUNDS - 1], AX, ALU.add).then_inc(s["cnt_sum"], 1)
            ve.wait_ge(s["cnt_sum"], 1)
            V.tensor_scalar(stat[0:1, 105:106], stat[0:1, 104:105], 1.0, float(GROUPS_OF_EXPERTS), ALU.add,
                            ALU.mult).then_inc(s["cnt_mul"], 1)
            ve.wait_ge(s["cnt_mul"], 1)
            V.tensor_copy(trips[0:1, 0:1], stat[0:1, 105:106]).then_inc(s["trips_made"], 1)
            gate4 = stat[:, 80:88].rearrange("p (t k) -> p t k", t=TT)
            for t in range(TT):
                ve.wait_ge(s["gate_exp"], t + 1)
                V.reciprocal(stat[:, 90 + t:91 + t], stat[:, 88 + t:89 + t]).then_inc(s["gate_rec"], 1)
            for t in range(TT):
                ve.wait_ge(s["gate_rec"], t + 1)
                V.tensor_scalar(gate4[:, t, :], gate4[:, t, :], stat[:, 90 + t:91 + t], None,
                                ALU.mult).then_inc(s["gate_made"], 1)
            for t in range(TT):
                ve.wait_ge(s["gate_made"], t + 1)
                V.tensor_tensor(eq[:, t], eq[:, t], gate4[:, t, :].unsqueeze(2).to_broadcast([P, TOPK, N_EXP]),
                                ALU.mult).then_inc(s["geq_made"], 1)
            ve.wait_ge(s["geq_made"], 2)
            for r in range(ROUNDS):
                V.tensor_reduce(gates[:, :, r * N_EXP:(r + 1) * N_EXP], eq.rearrange("p t k e -> p t e k"), AX,
                                ALU.add).then_inc(s["gate_table"], 1)
            filled(ve, "gT")
            V.tensor_copy(gateT, bank("gT")[0:N_EXP, 0:T]).then_inc(bank_emptied[bank_of("gT")], 1)
            V.tensor_copy(pick.rearrange("p (r e) -> p r e", r=ROUNDS),
                          ident[0:N_EXP, 0:N_EXP].unsqueeze(1).to_broadcast([N_EXP, ROUNDS, N_EXP])).then_inc(
                s["pick_made"], 1)
            ve.wait_ge(s["gate_table"], ROUNDS)
            ve.wait_ge(s["pick_made"], 1)
            ve.wait_ge(s["trips_made"], 1)
            n = ve.value_load(trips[0:1, 0:1], min_val=GROUPS_OF_EXPERTS, max_val=ROUNDS * GROUPS_OF_EXPERTS)

            def expert(v):
                ve.wait_ge(s["gather_filled"], v + 1)
                make_take(v + 1)
                for t in range(TT):
                    last = V.tensor_scalar(put[:, t], slot_iota[:].unsqueeze(1).to_broadcast([P, 2, SLOTS]),
                                           table[:, t, bass.ds(v, 1)], gates[:, t, bass.ds(v, 1)],
                                           ALU.is_equal, ALU.mult)
                last.then_inc(s["put_made"], 1)
                V.tensor_scalar(pick_e, ones[0:N_EXP, 0:SLOTS], pick[:, bass.ds(v, 1)], None,
                                ALU.mult).then_inc(s["pick_e_made"], 1)
                ve.wait_ge(s["h_filled"], v + 1)
                V.tensor_scalar(glu, ps[:, HIDDEN_BANKS[0], :], LIMIT, None, ALU.min).then_inc(s["glu_made"], 1)
                V.tensor_scalar(lin, ps[:, HIDDEN_BANKS[1], :], LIMIT, -LIMIT, ALU.min, ALU.max).then_inc(s["lin_made"], 1)
                ve.wait_ge(s["lin_made"], v + 1)
                V.scalar_tensor_tensor(lin, lin, 1.0, glu, ALU.add, ALU.mult).then_inc(s["lin_glu"], 1)
                ve.wait_ge(s["lin_glu"], v + 1)
                ve.wait_ge(s["sig_made"], v + 1)
                V.tensor_tensor(act, lin, sig, ALU.mult).then_inc(s["act_made"], 1)
                for t in range(TT):
                    for j in range(2):
                        k = 2 * t + j
                        c = slice(j * HALF, (j + 1) * HALF)
                        ve.wait_ge(s["scatter_filled"], v * 4 + (k + 1))
                        V.tensor_tensor(rows[:, t, c], ps[:, SCATTER_BANKS[k], :], rows[:, t, c], ALU.add).then_inc(
                            s[f"y_added{k}"], 1)

            with ve.Fori(0, n) as i:
                for k in range(UNROLL):
                    expert(i * UNROLL + k)
            ve.wait_ge(s["gfin_in"], 16)
            for t in range(TT):
                norm_tile("f", N_OUT, t, rows, "f_made", 2 * t + 2, g_final)

        @block.tensor
        def _(pe):
            M = nc.tensor

            def start_group(group):
                if INDEX[group] >= N_BANKS:
                    pe.wait_ge(bank_emptied[bank_of(group)], use_of(group) - 1)

            def end_group(ins, group):
                ins.then_inc(bank_filled[bank_of(group)], 1)

            def transposes(group, blocks):
                start_group(group)
                for n, (src, rows_) in enumerate(blocks):
                    w = src.shape[0]
                    last = M.transpose(bank(group)[0:rows_, n * w:(n + 1) * w], src, ident[0:w, 0:w])
                end_group(last, group)

            def rows_T(prefix, t, k, src, ready, need):
                pe.wait_ge(s[ready], need)
                transposes(f"{prefix}{t}{k}", [(src[:, t, c * P:(c + 1) * P], P) for c in range(4 * k, 4 * k + 4)])

            PART_PRODUCTS = [(0, 0), (0, 1), (1, 0)]

            def has_half(name, half):
                pe.wait_ge(s["low_made"], 2 * PIECES.index(name) + half + 1)

            def rows_half(group, lhs, name, half, t):
                if half == 0:
                    start_group(group)
                w = pair(2 * PIECES.index(name) + half)
                for a, b in PART_PRODUCTS:
                    for c in range(DC // 2):
                        first, final = half == 0 and a + b + c == 0, half == 1 and a == 1 and c == DC // 2 - 1
                        last = M.matmul(bank(group), lhs[:, a, half * (DC // 2) + c, t * P:(t + 1) * P], w[:, b, c, :],
                                        start=first, stop=final, skip_group_check=True)
                if half == 1:
                    end_group(last, group)
                return last

            def row_products(prefix, suffix, lhs, name, made=None):
                for half in range(2):
                    has_half(name, half)
                    for t in range(TT):
                        if made:
                            made(half, t)
                        last = rows_half(f"{prefix}{t}{suffix}", lhs, name, half, t)
                    if half == 0:
                        last.then_inc(s["first_half_used"], 1)

            def row_products_in_turn(prefix, suffix, lhs, name):
                for t in range(TT):
                    for half in range(2):
                        if t == 0:
                            has_half(name, half)
                        last = rows_half(f"{prefix}{t}{suffix}", lhs, name, half, t)
                        if half == 0 and t == TT - 1:
                            last.then_inc(s["first_half_used"], 1)

            def features_half(groups, name, half, rhs, made=None):
                has_half(name, half)
                if made:
                    for t in range(TT):
                        made(half, t)
                w = pair(2 * PIECES.index(name) + half)
                for n, group in enumerate(groups):
                    if half == 0:
                        start_group(group)
                    for i in range(2):
                        f = 2 * n + i
                        for b, a in PART_PRODUCTS:
                            for c in range(DC // 2):
                                first = half == 0 and i + a + b + c == 0
                                final = half == 1 and i == 1 and b == 1 and c == DC // 2 - 1
                                last = M.matmul(bank(group)[:, i * T:(i + 1) * T], w[:, b, c, f * P:(f + 1) * P],
                                                rhs[:, a, half * (DC // 2) + c, :], start=first, stop=final,
                                                skip_group_check=True)
                    if half == 1:
                        end_group(last, group)
                if half == 0:
                    last.then_inc(s["first_half_used"], 1)

            def turned(prefix):
                return lambda half, t: emptied(pe, f"{prefix}{t}{half}")

            pe.wait_ge(s["ident_made"], 2)
            pe.wait_ge(s["small_in"], 16 * 5)
            transposes("vecs", [(vec_rows[:], P)])
            for g in TN:
                t, k = int(g[0]), int(g[1])
                rows_T("xT", t, k, normed, "x_normed", 2 * t + k + 1)
            pe.wait_ge(s["wa_split"], 2)
            start_group("aL")
            for half in range(2):
                for t in range(TT):
                    emptied(pe, f"xT{t}{half}")
                for b, a in PART_PRODUCTS:
                    for c in range(half * (DC // 2), (half + 1) * (DC // 2)):
                        last = M.matmul(bank("aL")[0:RANK, 0:T], wa_parts[:, b, c, :], hT[:, a, c, :],
                                        start=half + a + b + c == 0, stop=half == 1 and b == 1 and c == DC - 1)
            end_group(last, "aL")
            for half in range(2):
                features_half(["q", "k"], "qk", half, hT)
            emptied(pe, "aL")
            pe.wait_ge(s["wa2_in"], 16)
            start_group("la")
            for f in range(2):
                last = M.matmul(bank("la")[:, f * T:(f + 1) * T], wa2[:, f * P:(f + 1) * P], aT[:], start=True, stop=True)
            end_group(last, "la")
            for name in ("v", "r", "sv"):
                row_products(name, "", hT, name)
            pe.wait_ge(s["wsgu_masked"], 1)
            transposes("wsT", [(w_sgu[:, g, :], P) for g in range(SGU_G)])
            row_products("u", "", hT, "u")
            emptied(pe, "q")
            pe.wait_ge(s["keys_made"], GLA_H)
            for t in range(TT):
                start_group(f"att{t}")
                for h in range(GLA_H):
                    last = M.matmul(bank(f"att{t}")[:, h * P:(h + 1) * P], kz[:, h, t * P:(t + 1) * P],
                                    q_in[:, h // 2, t * P:(t + 1) * P], start=True, stop=True)
                end_group(last, f"att{t}")
            emptied(pe, "k")
            transposes("koT", [(k_out[:, f, t * P:(t + 1) * P], P) for t in range(TT) for f in range(2)])
            for g in TN:
                t, k = int(g[0]), int(g[1])
                rows_T("memT", t, k, side, "mem_normed", 2 * t + k + 1)

            row_products("ga", "0", hT, "ga0")
            emptied(pe, "koT")
            emptied(pe, "v1")
            emptied(pe, "v0")
            for n in range(3):
                start_group(f"kv{n}")
                for f in range(2):
                    last = M.matmul(bank(f"kv{n}")[:, f * T:(f + 1) * T], koz[:, n // 2, n % 2, f * P:(f + 1) * P],
                                    values[:, n // 2, f * T:(f + 1) * T], start=True, stop=True)
                end_group(last, f"kv{n}")
            emptied(pe, "wsT")
            pe.wait_ge(s["sv_normed"], 2)
            for t in range(TT):
                start_group(f"mix{t}")
                for g in range(SGU_G):
                    c = slice(g * P, (g + 1) * P)
                    last = M.matmul(bank(f"mix{t}")[:, c], w_sguT[:, g, :], sgu_v[:, t, c], start=True, stop=True)
                end_group(last, f"mix{t}")
            row_products("ga", "1", hT, "ga1")
            emptied(pe, "att0")
            emptied(pe, "att1")
            for t in range(TT):
                start_group(f"o{t}")
                emptied(pe, f"kv{2 * t}")
                todo = []
                for h in range(GLA_H):
                    c = slice(h * P, (h + 1) * P)
                    todo.append((bank(f"o{t}")[:, c], attz[:, t, h, :], values[:, t, c]))
                for m in range(2):
                    n = 2 * t + m
                    if n:
                        for f in range(2):
                            todo.append((bank(f"o{t}")[64 * m:64 * m + 64, f * T:(f + 1) * T],
                                         q_in[:, f, n * GLA_C:(n + 1) * GLA_C], states[:, n - 1, f, :]))
                for i, (o, l, r) in enumerate(todo):
                    last = M.matmul(o, l, r, start=i == 0, stop=i == len(todo) - 1, skip_group_check=True)
                end_group(last, f"o{t}")
            row_products("gb", "0", hT, "gb0")
            row_products("gb", "1", hT, "gb1")
            pe.wait_ge(s["o_made"], 2)
            for k in range(2):
                transposes(f"oT{k}", [(o_rows[:, t, (2 * k + i) * P:(2 * k + i + 1) * P], P)
                                      for i in range(2) for t in range(TT)])
            for t in range(TT):
                emptied(pe, f"mix{t}")
            for k in range(2):
                transposes(f"sboT{k}", [(sgu_u[:, t, (2 * k + i) * P:(2 * k + i + 1) * P], P)
                                        for i in range(2) for t in range(TT)])
            for branch, src, name, tr in (("ya", oT, "pa", "oT"), ("yb", sboT, "pb", "sboT")):
                for half in range(2):
                    has_half(name, half)
                    emptied(pe, f"{tr}{half}")
                    w = pair(2 * PIECES.index(name) + half).rearrange("p b (c n) m -> p b c (n m)", c=2)
                    for g in TN:
                        t, n = int(g[0]), int(g[1])
                        if half == 0:
                            start_group(branch + g)
                        for a, b in PART_PRODUCTS:
                            for c in range(2):
                                last = M.matmul(bank(branch + g), src[:, a, 2 * half + c, t * P:(t + 1) * P],
                                                w[:, b, c, n * HALF:(n + 1) * HALF], start=half + a + b + c == 0,
                                                stop=half + a + c == 3, skip_group_check=True)
                        if half == 1:
                            end_group(last, branch + g)
                    if half == 0:
                        last.then_inc(s["first_half_used"], 1)
            for half in range(2):
                features_half(["kT0", "kT1"], "xk0", half, memT, turned("memT"))
            for g in TN:
                t, k = int(g[0]), int(g[1])
                rows_T("mT", t, k, normed, "mixed", 2 * t + k + 1)
            for half in range(2):
                features_half(["kT2", "kT3"], "xk1", half, memT)
            row_products("x1", "0", hT, "mx0", turned("mT"))
            row_products_in_turn("x1", "1", hT, "mx1")
            rows_T("hT", 0, 0, normed, "x1_normed", 1)
            rows_T("hT", 0, 1, normed, "x1_normed", 2)
            row_products("vm", "0", memT, "xv0")
            rows_T("hT", 1, 0, normed, "x1_normed", 3)
            rows_T("hT", 1, 1, normed, "x1_normed", 4)
            row_products("vm", "1", memT, "xv1")

            def scores(h):
                emptied(pe, f"xq{h}")
                emptied(pe, f"kT{h}")
                start_group(f"sc{h}")
                for t in range(TT):
                    for i in range(2):
                        last = M.matmul(bank(f"sc{h}")[:, t * T:(t + 1) * T], side_T[:, 2 * h + i, t * P:(t + 1) * P],
                                        kT[:, 2 * h + i, :], start=i == 0, stop=i == 1)
                end_group(last, f"sc{h}")

            def probs_T(h):
                emptied(pe, f"sc{h}")
                transposes(f"pT{h}", [(probs[:, h, t, m * P:(m + 1) * P], P) for m in range(2) for t in range(TT)])

            def attend(h):
                emptied(pe, f"pT{h}")
                if h == 0:
                    for g in TN:
                        emptied(pe, "vm" + g)
                start_group(f"ao{h}")
                for i in range(2):
                    for m in range(2):
                        c = XDH * h + P * i
                        last = M.matmul(bank(f"ao{h}")[:, i * T:(i + 1) * T], vm[:, m, c:c + P], probsT[:, h % 2, m, :],
                                        start=m == 0, stop=m == 1)
                end_group(last, f"ao{h}")

            for half in range(2):
                features_half(["xq0", "xq1"], "xq0", half, hT, turned("hT"))
            features_half(["xq2", "xq3"], "xq1", 0, hT)
            scores(0)
            scores(1)
            features_half(["xq2", "xq3"], "xq1", 1, hT)
            probs_T(0)
            probs_T(1)
            scores(2)
            scores(3)
            attend(0)
            attend(1)
            probs_T(2)
            probs_T(3)
            attend(2)
            attend(3)

            def logits(t):
                start_group(f"lg{t}")
                for c in range(DC):
                    if c % 4 == 0:
                        emptied(pe, f"hf{t}{c // 4}")
                    last = M.matmul(bank(f"lg{t}")[:, 0:N_EXP], side_T[:, c, t * P:(t + 1) * P], wr[:, c, :],
                                    start=c == 0, stop=c == DC - 1)
                end_group(last, f"lg{t}")

            def heads_made(half, t):
                emptied(pe, f"ao{2 * half}")
                emptied(pe, f"ao{2 * half + 1}")

            row_products("x2", "0", hT, "xo0", heads_made)
            row_products_in_turn("x2", "1", hT, "xo1")
            rows_T("hf", 0, 0, normed, "x2_normed", 1)
            rows_T("hf", 0, 1, normed, "x2_normed", 2)
            pe.wait_ge(s["wr_in"], 32)
            logits(0)
            rows_T("hf", 1, 0, normed, "x2_normed", 3)
            rows_T("hf", 1, 1, normed, "x2_normed", 4)
            logits(1)
            pe.wait_ge(s["consts_made"], 4)
            start_group("pos")
            pos = [(0, upper_r, 0), (1, ones_r, 0), (2, ones_r, 0), (1, upper_r, 1), (2, ones_r, 1)]
            for n, (o, l, t) in enumerate(pos):
                pe.wait_ge(s["mask_made"], t + 1)
                last = M.matmul(bank("pos")[:, o * N_EXP:(o + 1) * N_EXP], l[:], mask[:, t, :], start=n == 0,
                                stop=n == len(pos) - 1, skip_group_check=True)
            end_group(last, "pos")
            def gather(need_take):
                pe.wait_ge(s["take_made"], need_take)
                for t in range(TT):
                    for j in range(2):
                        last = M.matmul(ps[64 * j:64 * j + 64, GATHER_BANK, :], take[:, t, :],
                                        normed[:, t, j * HALF:(j + 1) * HALF], start=t == 0, stop=t == 1,
                                        skip_group_check=True)
                last.then_inc(s["gather_filled"], 1)

            def gather_T(need_copy):
                pe.wait_ge(s["gather_copied"], need_copy)
                for q in range(4):
                    last = M.transpose(ps[:, GATHER_BANK, q * P:(q + 1) * P], gathered[:, q * P:(q + 1) * P], ident[:])
                last.then_inc(s["xeT_filled"], 1)

            pe.wait_ge(bank_emptied[GATHER_BANK], GATHER_BANK_USES)
            gather(1)
            pe.wait_ge(s["trips_made"], 1)
            loop_count = pe.value_load(trips[0:1, 0:1], min_val=GROUPS_OF_EXPERTS, max_val=ROUNDS * GROUPS_OF_EXPERTS)
            pe.wait_ge(s["gate_table"], ROUNDS)
            transposes("gT", [(gates[:, t, 0:N_EXP], N_EXP) for t in range(TT)])
            gather_T(1)

            def output_biases(k):
                t, j = k // 2, k % 2
                M.matmul(ps[:, SCATTER_BANKS[k], :], gateT[:, t * P:(t + 1) * P], b2[:, j * HALF:(j + 1) * HALF],
                         start=True, stop=False, skip_group_check=True)

            def chunk_arrived(i, c, step_is_first):
                if not step_is_first:
                    turn = c - len(EXTRA_CHUNKS)
                    pe.wait_ge(chunk_full[turn % N_CHUNK_SLOTS],
                               i * (16 * LOADS_PER_SLOT) + 16 * (turn // N_CHUNK_SLOTS + 1))
                elif c == EXTRA_CHUNKS[-1]:
                    pe.wait_ge(last_extra_full, 16)
                elif c in EXTRA_CHUNKS:
                    pe.wait_ge(extras_full, 16 * (len(EXTRA_CHUNKS) - 1))
                else:
                    pe.wait_ge(chunk_full[slot_of(c, True)], 16 * (turn_of(c) // N_CHUNK_SLOTS + 1))

            def expert(i, k, step_is_first=False):
                v = i * UNROLL + k
                pe.wait_ge(s["xeT_made"], v + 1)
                for c in range(W1_CHUNKS):
                    chunk_arrived(i, k * CHUNKS + c, step_is_first)
                    for h in range(2):
                        for j in range(2):
                            last = M.matmul(ps[64 * j:64 * j + 64, HIDDEN_BANKS[h], :],
                                            xeT[:, c % 4, (c // 4) * SLOTS:(c // 4 + 1) * SLOTS],
                                            chunk(k * CHUNKS + c, step_is_first)[:, h * D + j * HALF:h * D + (j + 1) * HALF],
                                            start=c == 0, stop=False, skip_group_check=True)
                    last.then_inc(s["chunk_used"], 1)
                if step_is_first and k == 0:
                    pe.wait_ge(s["b1_in"], 16)
                pe.wait_ge(s["pick_e_made"], v + 1)
                for h in range(2):
                    for j in range(2):
                        last = M.matmul(ps[64 * j:64 * j + 64, HIDDEN_BANKS[h], :], pick_e,
                                        b1[:, h * D + j * HALF:h * D + (j + 1) * HALF],
                                        start=False, stop=True, skip_group_check=True)
                last.then_inc(s["h_filled"], 1)
                pe.wait_ge(s["put_made"], v + 1)
                for t in range(TT):
                    last = M.transpose(ps[:, PUT_BANK, t * P:(t + 1) * P], put[:, t].rearrange("p j s -> p (j s)"), ident[:])
                last.then_inc(s["putT_filled"], 1)
                gather(v + 2)
                gather_T(v + 2)
                pe.wait_ge(s["act_made"], v + 1)
                pe.wait_ge(s["putT_made"], v + 1)
                for q in range(4):
                    last = M.transpose(ps[:, PUT_BANK, q * P:(q + 1) * P], act[:, q * P:(q + 1) * P], ident[:])
                last.then_inc(s["actT_filled"], 1)
                pe.wait_ge(s["actT_made"], v + 1)
                for w2 in range(W2_CHUNKS):
                    c2 = k * CHUNKS + W1_CHUNKS + w2
                    chunk_arrived(i, c2, step_is_first)
                    w = chunk(c2, step_is_first).rearrange("p (i n) -> p i n", i=2)
                    for h in range(2):
                        c = 2 * w2 + h
                        for j in range(2):
                            last = M.matmul(ps[64 * j:64 * j + 64, Y_BANK, :],
                                            actT[:, c % 4, (c // 4) * SLOTS:(c // 4 + 1) * SLOTS],
                                            w[:, h, j * HALF:(j + 1) * HALF], start=c == 0, stop=c == DC - 1,
                                            skip_group_check=True)
                    last.then_inc(s["chunk_used"] if w2 < W2_CHUNKS - 1 else s["y_filled"], 1)
                if step_is_first and k < 3:
                    if k == 0:
                        emptied(pe, "gT")
                        pe.wait_ge(s["b2_in"], 16)
                    output_biases(k)
                pe.wait_ge(s["y_copied"], v + 1)
                if step_is_first and k == 3:
                    output_biases(k)
                for t in range(TT):
                    for j in range(2):
                        q = slice(64 * j, 64 * j + 64)
                        begun = step_is_first and 2 * t + j == k
                        M.matmul(ps[:, SCATTER_BANKS[2 * t + j], :], putT[q, t, :], y_rows[q, :], start=not begun,
                                 stop=True, skip_group_check=True).then_inc(s["scatter_filled"], 1)

            for k in range(UNROLL):
                expert(0, k, True)
            with pe.Fori(1, loop_count) as i:
                for k in range(UNROLL):
                    expert(i, k)


INPUTS = ["x", "mem", "norm_mix_g", "w_in", "gla_w_a2", "gla_b_a", "gla_out_g", "sgu_norm_g", "sgu_norm_b", "sgu_w",
          "sgu_b", "w_proj_a", "w_proj_b", "w_mix_out", "norm_x_g", "norm_mem_g", "w_xq", "w_xk", "w_xv", "w_xo",
          "norm_ffn_g", "w_router", "b_router", "w_e1", "b_e1", "w_e2", "b_e2", "norm_final_g"]


def kernel(**inputs):
    import numpy as np
    import concourse.bacc as bacc
    from concourse.bass_utils import run_bass_kernel_spmd

    nc = bacc.Bacc("TRN2", target_bir_lowering=False, num_devices=1)
    arrays = {f"in_{n}": np.ascontiguousarray(inputs[n]) for n in INPUTS}
    aps = {n: nc.dram_tensor(f"in_{n}", arrays[f"in_{n}"].shape, F32, kind="ExternalInput").ap() for n in INPUTS}
    out = nc.dram_tensor("out", (1, T, D), F32, kind="ExternalOutput").ap()
    layer_program(nc, aps, out)
    result = run_bass_kernel_spmd(nc, [arrays], core_ids=[0])
    return result.results[0]["out"]
```
